# Optimizing a Trainium2 kernel written in Bass

```python
import math
import jax, jax.numpy as jnp
from jax import lax
import numpy as np

D_MODEL = 1024
BATCH = 1
SEQ = 512
DEPTH = 1

GRID_W = 64
CTX_LEN = 256
ATTN_HEADS = 4
ATTN_QK_DIM = 64
ATTN_V_DIM = 2 * ATTN_QK_DIM
ATTN_WIDTH = ATTN_HEADS * ATTN_V_DIM
QKV_WIDTH = 3 * ATTN_WIDTH
AXIS_DIM = ATTN_QK_DIM // 2
ROPE_THETA = 10000.0
Q_BLOCK = 128
POOL_WIDTH = D_MODEL - ATTN_WIDTH
POOL_WINDOWS = (2, 4, 8, 16)
N_POOL_GROUPS = len(POOL_WINDOWS)
POOL_GROUP = POOL_WIDTH // N_POOL_GROUPS
IN_WIDTH = QKV_WIDTH + POOL_WIDTH
N_EXPERTS = 64
TOP_K = 8
N_GROUPS = 8
TOPK_GROUPS = 4
EXPERT_DIM = 256
SHARED_DIM = 256
ROUTED_SCALE = 2.5
EXPERT_BLOCK = 256
EPS = 1e-6

kernel_name = "hybrid_diffattn_pool_moe_dit_layer"

def rmsnorm(x, g):
    xf = x.astype(jnp.float32)
    y = xf * lax.rsqrt(jnp.mean(xf * xf, axis=-1, keepdims=True) + EPS)
    return (y * g.astype(jnp.float32)).astype(x.dtype)

def adaln(cvec, w, b):
    m = jax.nn.silu(cvec) @ w + b
    return jnp.split(m, 6, axis=-1)

def modulate(h, shift, scale):
    return h * (1.0 + scale) + shift

def axial_rope_tables(rows):
    row = jnp.broadcast_to(jnp.arange(rows)[:, None], (rows, GRID_W)).reshape(-1).astype(jnp.float32)
    col = jnp.broadcast_to(jnp.arange(GRID_W)[None, :], (rows, GRID_W)).reshape(-1).astype(jnp.float32)
    freqs = ROPE_THETA ** (-jnp.arange(0, AXIS_DIM, 2, dtype=jnp.float32) / AXIS_DIM)
    ar = row[:, None] * freqs
    ac = col[:, None] * freqs
    return (jnp.cos(ar), jnp.sin(ar), jnp.cos(ac), jnp.sin(ac))

def rope_axis(x, cos, sin):
    x1, x2 = jnp.split(x, 2, axis=-1)
    cos = cos[None, :, None, :]
    sin = sin[None, :, None, :]
    return jnp.concatenate([x1 * cos - x2 * sin, x2 * cos + x1 * sin], axis=-1)

def rope2d(x, tabs):
    cr, sr, cc, sc = tabs
    out = jnp.concatenate([rope_axis(x[..., :AXIS_DIM], cr, sr), rope_axis(x[..., AXIS_DIM:], cc, sc)], axis=-1)
    return out.astype(x.dtype)

def split_q(pq):
    b, n, _ = pq.shape
    q = pq.reshape(b, n, ATTN_HEADS, 2, ATTN_QK_DIM)
    return q[..., 0, :], q[..., 1, :]

def split_kv(pkv):
    b, n, _ = pkv.shape
    k = pkv[..., :ATTN_WIDTH].reshape(b, n, ATTN_HEADS, 2, ATTN_QK_DIM)
    v = pkv[..., ATTN_WIDTH:].reshape(b, n, ATTN_HEADS, ATTN_V_DIM)
    return k[..., 0, :], k[..., 1, :], v

def bhnd(x):
    return jnp.swapaxes(x, 1, 2)

def diff_lambda(lq1, lk1, lq2, lk2, lam_init):
    f = jnp.float32
    return (jnp.exp(jnp.sum(lq1.astype(f) * lk1.astype(f))) - jnp.exp(jnp.sum(lq2.astype(f) * lk2.astype(f)))
            + lam_init)

def diff_attn(q1, q2, k1, k2, v, lam):
    scale = ATTN_QK_DIM ** -0.5
    s1 = jnp.einsum('bhqd,bhkd->bhqk', q1, k1, preferred_element_type=jnp.float32) * scale
    s2 = jnp.einsum('bhqd,bhkd->bhqk', q2, k2, preferred_element_type=jnp.float32) * scale
    a = jax.nn.softmax(s1, axis=-1) - lam * jax.nn.softmax(s2, axis=-1)
    return jnp.einsum('bhqk,bhkd->bhqd', a.astype(v.dtype), v)

def blocked_diff_attn(q1, q2, k1, k2, v, lam):
    b, h, n, d = q1.shape
    nb = n // Q_BLOCK
    to_blocks = lambda q: jnp.moveaxis(q.reshape(b, h, nb, Q_BLOCK, d), 2, 0)
    o = lax.map(lambda qq: diff_attn(qq[0], qq[1], k1, k2, v, lam), (to_blocks(q1), to_blocks(q2)))
    return jnp.moveaxis(o, 0, 2).reshape(b, h, n, ATTN_V_DIM)

def attn_heads_out(o, g_subln, lam_init):
    o = rmsnorm(o, g_subln) * (1.0 - lam_init)
    b, h, n, dv = o.shape
    return bhnd(o).reshape(b, n, h * dv)

def pool_mix(p, w_pool, b_pool, pool_scale):
    b, n, _ = p.shape
    pf = p.astype(jnp.float32)
    cs = jnp.concatenate([jnp.zeros((b, 1, POOL_WIDTH), jnp.float32), jnp.cumsum(pf, axis=1)], axis=1)
    t = jnp.arange(n)
    outs = []
    for gi, w in enumerate(POOL_WINDOWS):
        lo = jnp.clip(t - w // 2, 0, n)
        hi = jnp.clip(t + (w - w // 2), 0, n)
        sl = slice(gi * POOL_GROUP, (gi + 1) * POOL_GROUP)
        csg = cs[..., sl]
        mean = (csg[:, hi] - csg[:, lo]) / (hi - lo).astype(jnp.float32)[None, :, None]
        outs.append(mean - pf[..., sl])
    d = jnp.stack(outs, axis=2)
    y = jnp.einsum('bngc,gce->bnge', d, w_pool.astype(jnp.float32)).reshape(b, n, POOL_WIDTH) + b_pool
    return (y * pool_scale).astype(p.dtype)

def swiglu(t, wg, wu, wd):
    return (jax.nn.silu(t @ wg) * (t @ wu)) @ wd

def moe_ffn(h, w_router, router_bias, w_e_gate, w_e_up, w_e_down, w_sh_gate, w_sh_up, w_sh_down):
    b, n, d = h.shape
    t = h.reshape(-1, d)
    T = t.shape[0]
    scores = jax.nn.sigmoid((t @ w_router).astype(jnp.float32))
    biased = scores + router_bias.astype(jnp.float32)
    grp = biased.reshape(T, N_GROUPS, N_EXPERTS // N_GROUPS)
    grp_score = lax.top_k(grp, 2)[0].sum(-1)
    _, top_groups = lax.top_k(grp_score, TOPK_GROUPS)
    group_mask = jax.nn.one_hot(top_groups, N_GROUPS, dtype=jnp.float32).sum(1) > 0
    expert_mask = jnp.repeat(group_mask, N_EXPERTS // N_GROUPS, axis=1)
    _, top_e = lax.top_k(jnp.where(expert_mask, biased, -jnp.inf), TOP_K)
    wts = jnp.take_along_axis(scores, top_e, axis=1)
    wts = wts / jnp.sum(wts, axis=-1, keepdims=True) * ROUTED_SCALE
    A = T * TOP_K
    flat_e = top_e.reshape(-1)
    flat_tok = jnp.repeat(jnp.arange(T, dtype=jnp.int32), TOP_K)
    flat_w = wts.reshape(-1)
    order = jnp.argsort(flat_e)
    sorted_e = flat_e[order]
    counts = jnp.bincount(flat_e, length=N_EXPERTS)
    starts = jnp.cumsum(counts) - counts
    padded = ((counts + EXPERT_BLOCK - 1) // EXPERT_BLOCK) * EXPERT_BLOCK
    pends = jnp.cumsum(padded)
    pstarts = pends - padded
    dest = pstarts[sorted_e] + (jnp.arange(A) - starts[sorted_e])
    P = A + N_EXPERTS * EXPERT_BLOCK
    nblk = P // EXPERT_BLOCK
    slot_tok = jnp.full((P,), T, jnp.int32).at[dest].set(flat_tok[order])
    slot_w = jnp.zeros((P,), jnp.float32).at[dest].set(flat_w[order])
    block_e = jnp.minimum(jnp.searchsorted(pends, jnp.arange(nblk) * EXPERT_BLOCK, side='right'), N_EXPERTS - 1)
    t_pad = jnp.concatenate([t, jnp.zeros((1, d), t.dtype)], axis=0)

    def expert_block(args):
        tok, wb, e = args
        xb = t_pad[tok]
        yb = swiglu(xb, w_e_gate[e], w_e_up[e], w_e_down[e])
        return yb * wb[:, None]

    yb = lax.map(expert_block, (slot_tok.reshape(nblk, EXPERT_BLOCK), slot_w.reshape(nblk, EXPERT_BLOCK), block_e))
    routed = jax.ops.segment_sum(yb.reshape(P, d), slot_tok, num_segments=T + 1)[:T]
    shared = swiglu(t, w_sh_gate, w_sh_up, w_sh_down)
    return (routed + shared).astype(h.dtype).reshape(b, n, d)

def setup_inputs(seed: int = 0) -> dict:
    key = jax.random.key(seed)
    ks = jax.random.split(key, 32)
    f32 = jnp.float32
    L, D, E, F, FS = DEPTH, D_MODEL, N_EXPERTS, EXPERT_DIM, SHARED_DIM

    def nrm(k, shape, scale=1.0):
        return jax.random.normal(k, shape, f32) * scale

    def gain(k, shape, s=0.05):
        return 1.0 + s * jax.random.normal(k, shape, f32)

    return {
        "x": nrm(ks[0], (BATCH, SEQ, D)),
        "c": nrm(ks[1], (BATCH, D)),
        "ctx": nrm(ks[2], (BATCH, CTX_LEN, D)),
        "c_ctx": nrm(ks[3], (D,)),
        "w_ada": nrm(ks[4], (L, D, 6 * D), D ** -0.5),
        "b_ada": nrm(ks[5], (L, 6 * D), 0.01),
        "g_pre_mix": gain(ks[6], (L, D)),
        "g_post_mix": gain(ks[7], (L, D)),
        "g_pre_ffn": gain(ks[8], (L, D)),
        "g_post_ffn": gain(ks[9], (L, D)),
        "w_in": nrm(ks[10], (L, D, IN_WIDTH), D ** -0.5),
        "lambda_q1": nrm(ks[11], (L, ATTN_QK_DIM), 0.1),
        "lambda_k1": nrm(ks[12], (L, ATTN_QK_DIM), 0.1),
        "lambda_q2": nrm(ks[13], (L, ATTN_QK_DIM), 0.1),
        "lambda_k2": nrm(ks[14], (L, ATTN_QK_DIM), 0.1),
        "g_subln": gain(ks[15], (L, ATTN_V_DIM)),
        "w_pool": nrm(ks[16], (L, N_POOL_GROUPS, POOL_GROUP, POOL_GROUP), POOL_GROUP ** -0.5),
        "b_pool": nrm(ks[17], (L, POOL_WIDTH), 0.01),
        "pool_scale": gain(ks[18], (L, POOL_WIDTH), 0.1),
        "w_out": nrm(ks[19], (L, D, D), D ** -0.5),
        "w_router": nrm(ks[20], (L, D, E), D ** -0.5),
        "router_bias": nrm(ks[21], (L, E), 0.01),
        "w_e_gate": nrm(ks[22], (L, E, D, F), D ** -0.5),
        "w_e_up": nrm(ks[23], (L, E, D, F), D ** -0.5),
        "w_e_down": nrm(ks[24], (L, E, F, D), F ** -0.5),
        "w_sh_gate": nrm(ks[25], (L, D, FS), D ** -0.5),
        "w_sh_up": nrm(ks[26], (L, D, FS), D ** -0.5),
        "w_sh_down": nrm(ks[27], (L, FS, D), FS ** -0.5),
    }

def reference(x, c, ctx, c_ctx, w_ada, b_ada, g_pre_mix, g_post_mix, g_pre_ffn, g_post_ffn, w_in,
              lambda_q1, lambda_k1, lambda_q2, lambda_k2, g_subln, w_pool, b_pool, pool_scale, w_out,
              w_router, router_bias, w_e_gate, w_e_up, w_e_down, w_sh_gate, w_sh_up, w_sh_down):
    n = x.shape[1]
    rows = n // GRID_W
    tabs = axial_rope_tables(rows)
    ex = lambda m: m[:, None, :]
    for l in range(DEPTH):
        last = l == DEPTH - 1
        lam_init = 0.8 - 0.6 * math.exp(-0.3 * l)
        sh_a, sc_a, g_a, sh_f, sc_f, g_f = adaln(c, w_ada[l], b_ada[l])
        csh_a, csc_a, cg_a, csh_f, csc_f, cg_f = adaln(c_ctx, w_ada[l], b_ada[l])
        lam = diff_lambda(lambda_q1[l], lambda_k1[l], lambda_q2[l], lambda_k2[l], lam_init)

        hx = modulate(rmsnorm(x, g_pre_mix[l]), ex(sh_a), ex(sc_a))
        hc = modulate(rmsnorm(ctx, g_pre_mix[l]), csh_a, csc_a)
        px = hx @ w_in[l]
        q1x, q2x = split_q(px[..., :ATTN_WIDTH])
        k1x, k2x, vx = split_kv(px[..., ATTN_WIDTH:QKV_WIDTH])
        q1x, q2x, k1x, k2x = (rope2d(t, tabs) for t in (q1x, q2x, k1x, k2x))
        k1c, k2c, vc = split_kv(hc @ w_in[l][:, ATTN_WIDTH:QKV_WIDTH])
        k1_all = jnp.concatenate([bhnd(k1c), bhnd(k1x)], axis=2)
        k2_all = jnp.concatenate([bhnd(k2c), bhnd(k2x)], axis=2)
        v_all = jnp.concatenate([bhnd(vc), bhnd(vx)], axis=2)
        att_x = blocked_diff_attn(bhnd(q1x), bhnd(q2x), k1_all, k2_all, v_all, lam)
        att_x = attn_heads_out(att_x, g_subln[l], lam_init)
        pool_x = pool_mix(px[..., QKV_WIDTH:], w_pool[l], b_pool[l], pool_scale[l])
        yx = jnp.concatenate([att_x, pool_x], axis=-1) @ w_out[l]
        x = x + ex(g_a) * rmsnorm(yx, g_post_mix[l])
        if not last:
            q1c, q2c = split_q(hc @ w_in[l][:, :ATTN_WIDTH])
            att_c = diff_attn(bhnd(q1c), bhnd(q2c), bhnd(k1c), bhnd(k2c), bhnd(vc), lam)
            att_c = attn_heads_out(att_c, g_subln[l], lam_init)
            pool_c = pool_mix(hc @ w_in[l][:, QKV_WIDTH:], w_pool[l], b_pool[l], pool_scale[l])
            yc = jnp.concatenate([att_c, pool_c], axis=-1) @ w_out[l]
            ctx = ctx + cg_a * rmsnorm(yc, g_post_mix[l])

        moe_w = (w_router[l], router_bias[l], w_e_gate[l], w_e_up[l], w_e_down[l],
                 w_sh_gate[l], w_sh_up[l], w_sh_down[l])
        hx = modulate(rmsnorm(x, g_pre_ffn[l]), ex(sh_f), ex(sc_f))
        x = x + ex(g_f) * rmsnorm(moe_ffn(hx, *moe_w), g_post_ffn[l])
        if not last:
            hc = modulate(rmsnorm(ctx, g_pre_ffn[l]), csh_f, csc_f)
            ctx = ctx + cg_f * rmsnorm(moe_ffn(hc, *moe_w), g_post_ffn[l])
    return x


_drawn_inputs = setup_inputs


def setup_inputs(seed=0):
    import zlib

    import numpy as np

    out = dict(_drawn_inputs(seed))
    spreads = {}
    factors = {}
    for name, (base, spread) in spreads.items():
        noise = np.random.default_rng([zlib.crc32(name.encode()), seed]).standard_normal(out[name].shape)
        drawn = base * np.exp(spread * noise) if base else spread * noise
        out[name] = __import__('jax').numpy.asarray(drawn.astype(out[name].dtype))
    for name, factor in factors.items():
        out[name] = (out[name] * factor).astype(out[name].dtype)
    return out
```

```python
from contextlib import ExitStack

import concourse.bass as bass
import numpy as np
from concourse import mybir

F32 = mybir.dt.float32
I32 = mybir.dt.int32
U32 = mybir.dt.uint32
ALU = mybir.AluOpType
ACT = mybir.ActivationFunctionType
AX = mybir.AxisListType.X

P = 128
D = 1024
KD = D // P
T = 512
NT = T // P
CTX = 256
NC_ = CTX // P
KEYS = CTX + T
NKEY = KEYS // P
HEADS = 4
E = 64
TOPK = 8
F = 256
FJ = F // P
GRID_W = 64
EPS = 1e-6
LAM_INIT = 0.2
SCALE = 64 ** -0.5
ROUTED_SCALE = 2.5
WINDOWS = (2, 4, 8, 16)
FAR = 8192.0
MAXB = E + T * TOPK // P
EW = 3 * KD * F
IOTA = 640
PAD = 8
TP = T + 2 * PAD

C_ID = 0
C_ROPE = C_ID + P
C_TRI = C_ROPE + 2 * T
C_ONE = C_TRI + P
C_IOTA = C_ONE + P
C_JLT = C_IOTA + IOTA
C_TOK = C_JLT + 64
C_TOK8 = C_TOK + NT
C_PART = C_TOK8 + NT
C_FAC = C_PART + 1
C_EPS = C_FAC + 64
NCONST = C_EPS + 1


def constants():
    c = np.zeros((P, NCONST), np.float32)
    p = np.arange(P)
    c[:, C_ID:C_ID + P] = np.eye(P)
    f = p % 64
    freqs = (np.float32(10000.0) ** (-np.arange(0, 32, 2, dtype=np.float32) / np.float32(32))).astype(np.float32)
    t = np.arange(T)
    pos = np.where((f // 32 == 0)[:, None], (t // GRID_W)[None], (t % GRID_W)[None]).astype(np.float32)
    angle = (pos * freqs[f % 16][:, None]).astype(np.float32)
    c[:, C_ROPE:C_ROPE + T] = np.cos(angle)
    c[:, C_ROPE + T:C_ROPE + 2 * T] = np.sin(angle) * np.where(f % 32 < 16, -1.0, 1.0)[:, None]
    c[:, C_TRI:C_TRI + P] = p[:, None] < p[None]
    c[:, C_ONE:C_ONE + P] = 1.0
    c[:, C_IOTA:C_IOTA + IOTA] = np.arange(IOTA)
    c[:, C_JLT:C_JLT + 64] = (np.arange(8)[None] < np.arange(8)[:, None]).reshape(1, 64)
    for a in range(NT):
        c[:, C_TOK + a] = a * P + p - FAR
        c[:, C_TOK8 + a] = (a * P + p) * TOPK - FAR
    c[:, C_PART] = p
    fac = np.ones((4, 2, 8), np.float32)
    for g, w in enumerate(WINDOWS):
        for side, ts in enumerate((range(8), range(T - 8, T))):
            for i, tt in enumerate(ts):
                fac[g, side, i] = w / (min(tt + w - w // 2, T) - max(tt - w // 2, 0))
    c[:, C_FAC:C_FAC + 64] = fac.reshape(1, 64)
    c[:, C_EPS] = EPS
    return c


def build(nc, a, hbuf, ybuf, out):
    with ExitStack() as ctx:
        def sb(name, shape, dt=F32):
            return ctx.enter_context(nc.sbuf_tensor(name, shape, dt))

        def sem(name):
            return ctx.enter_context(nc.semaphore(name))

        ring = sb("ring", [P, 4 * EW])
        actT = sb("actT", [P, 6144])
        xres = sb("xres", [P, NT, D])
        cst = sb("cst", [P, NCONST])
        heads = sb("heads", [P, 10240])
        rows = sb("rows", [P, 4096])
        vec = sb("vec", [P, 256])
        lamv = sb("lamv", [P, 4, 64])
        tab = sb("tab", [1, 448], I32)
        ntab = sb("ntab", [1, 1], I32)
        slotf = sb("slotf", [P, 4])
        gidx = sb("gidx", [P, 1], U32)
        sidx = sb("sidx", [P, 1], U32)

        pp = [ctx.enter_context(nc.psum_tensor(f"pp{i}", [P, 1024], F32)) for i in range(4)]

        ident = cst[:, C_ID:C_ID + P]
        ones = cst[:, C_ONE:C_ONE + P]
        w_in = ring[:, 0:16384].rearrange("p (k n) -> p k n", k=KD)
        wa0 = ring[:, 16384:24576].rearrange("p (k n) -> p k n", k=KD)
        wa1 = heads[:, 0:8192].rearrange("p (k n) -> p k n", k=KD)
        wac = [ring[:, 16384 + 4096 * i:20480 + 4096 * i].rearrange("p (k n) -> p k n", k=KD) for i in range(2)]
        ctx_in = heads[:, 8192:10240].rearrange("p (c d) -> p c d", c=NC_)
        xn = rows[:, :].rearrange("p (b k q) -> p b k q", b=4, k=KD)
        hxT = actT[:, 0:4096].rearrange("p (k t) -> p k t", k=KD)
        hcT = actT[:, 4096:6144].rearrange("p (k t) -> p k t", k=KD)
        qT = heads[:, 0:2048].rearrange("p (h t) -> p h t", h=HEADS)
        kT = heads[:, 2048:5120].rearrange("p (h t) -> p h t", h=HEADS)
        pT = heads[:, 5120:7168].rearrange("p (g t) -> p g t", g=4)
        vv = heads[:, 7168:10240].rearrange("p (c n) -> p c n", c=NKEY)
        raw = rows[:, 0:1024].rearrange("p (b t) -> p b t", b=2)
        swp = rows[:, 1024:1536]
        sumA = rows[:, 1536:1536 + TP]
        sumB = rows[:, 2064:2064 + TP]
        wpool = rows[:, 3072:3584].rearrange("p (g e) -> p g e", g=4)
        w_out = ring[:, 0:8192].rearrange("p (j n) -> p j n", j=KD)
        e12 = ring[:, 8192:9728].rearrange("p (s n) -> p s n", s=2)
        aT = ring[:, 9728:11264].rearrange("p (b c q) -> p b c q", b=2, c=NKEY)
        junk = ring[:, 11264:12288]
        catT = actT[:, 0:4096].rearrange("p (j t) -> p j t", j=KD)
        oall = actT[:, 4096:6144].rearrange("p (u n) -> p u n", u=16)
        arow = rows[:, :].rearrange("p (r n) -> p r n", r=4)
        grow = heads[:, 5120:7168].rearrange("p (r n) -> p r n", r=2)
        y1 = heads[:, 6144:10240].rearrange("p (c n) -> p c n", c=NT)
        hT = actT[:, 0:4096].rearrange("p (k t) -> p k t", k=KD)
        w_r = actT[:, 4096:4608].rearrange("p (k e) -> p k e", k=KD)
        rt = actT[:, 4608:6144].rearrange("p (s n) -> p s n", s=6)
        wsg = heads[:, 0:2048].rearrange("p (k f) -> p k f", k=KD)
        wsu = heads[:, 2048:4096].rearrange("p (k f) -> p k f", k=KD)
        wsd = heads[:, 4096:6144].rearrange("p (j n) -> p j n", j=FJ)
        xg = heads[:, 6144:7168]
        xT = heads[:, 7168:8192].rearrange("p (k s) -> p k s", k=KD)
        ysb = heads[:, 8192:9216]
        sg = heads[:, 9216:9472]
        hmid = heads[:, 9472:9728].rearrange("p (j q) -> p j q", j=FJ)
        hTs = heads[:, 9728:9984].rearrange("p (j q) -> p j q", j=FJ)
        tnb = heads[:, 9984:10240]
        rtab = rows[:, 0:1024].rearrange("p (c e w) -> p c e w", c=NT, w=4)
        key = rows[:, 1024:1280].rearrange("p (c e) -> p c e", c=NT)
        oneh = rows[:, 1280:1792].rearrange("p (c s) -> p c s", c=NT)
        selt = rows[:, 1792:2048].rearrange("p (c e) -> p c e", c=NT)
        sct = rows[:, 2048:2304].rearrange("p (c e) -> p c e", c=NT)
        brow = rows[:, 2304:2368]
        m8 = rows[:, 2368:2624]
        hs = ring[:, 16384:17408].rearrange("p (j t) -> p j t", j=FJ)
        sgs = ring[:, 17408:18432].rearrange("p (j t) -> p j t", j=FJ)
        yin = [ring[:, 0:8192], ring[:, 8192:16384]]
        acc = ring[:, 18432:22528].rearrange("p (c n) -> p c n", c=NT)

        sc2 = vec[:, 0:16].rearrange("p (k s) -> p k s", s=2)
        c2 = vec[:, 16:32].rearrange("p (s k) -> p s k", s=2)
        gcol = vec[:, 32:40]
        bcol = vec[:, 40:56].rearrange("p (r k) -> p r k", r=2)
        modc = vec[:, 56:88].rearrange("p (r k s) -> p r k s", r=2, s=2)
        ssq = vec[:, 88:94]
        rstd = vec[:, 94:100]
        gsub = vec[:, 100:101]
        bpool = vec[:, 101:105]
        pscale = vec[:, 105:109]
        dots = vec[:, 109:111]
        lam = vec[:, 111:112]
        mx = vec[:, 112:114]
        nmx = vec[:, 114:116]
        lsum = vec[:, 116:118]
        rl = vec[:, 118:120]
        ossq = vec[:, 120:136]
        orst = vec[:, 136:152]
        yssq = vec[:, 152:156]
        yrst = vec[:, 156:160]
        hssq = vec[:, 160:164]
        hrst = vec[:, 164:168]
        fssq = vec[:, 168:172]
        frst = vec[:, 172:176]
        btab = vec[:, 176:180]
        rsum = vec[:, 180:184]

        s_small = sem("small_loaded")
        s_x = sem("x_loaded")
        s_ctx = sem("ctx_loaded")
        s_wa0 = sem("ada_shift_loaded")
        s_wa1 = sem("ada_scale_loaded")
        s_win = sem("w_in_loaded")
        s_wac = [sem(f"ada_chunk_loaded{i}") for i in range(2)]
        s_brow = sem("b_ada_rows_loaded")
        s_grow = sem("gain_rows_loaded")
        s_gpf = sem("gain_post_ffn_loaded")
        s_wout = sem("w_out_loaded")
        s_wpool = sem("w_pool_loaded")
        s_wr = sem("router_loaded")
        s_rb = sem("router_bias_loaded")
        s_wsh = sem("shared_loaded")
        s_we = [sem(f"expert_slot_loaded{i}") for i in range(4)]
        s_hst = sem("h_stored")
        s_out = sem("out_stored")
        s_silc = sem("silu_c")
        s_ssq = sem("tile_squares")
        s_sq = sem("tile_rms")
        s_xn = sem("tile_normalised")
        s_tp = sem("tile_transposed")
        s_tev = sem("tile_evacuated")
        s_adc = sem("ada_columns")
        s_mod = sem("modulated")
        s_ip = sem("in_projection")
        s_ipe = sem("in_projection_evacuated")
        s_rope = sem("rotated")
        s_pd = sem("pool_differences")
        s_pm = sem("pool_products")
        s_adr = sem("ada_rows")
        s_adre = sem("ada_rows_added")
        s_poolout = sem("pool_out")
        s_gac = sem("gain_rows_used")
        s_sc = sem("scores")
        s_nmx = sem("score_maxima")
        s_exp = sem("exponentials")
        s_a = sem("probabilities")
        s_aTp = sem("probabilities_transposed")
        s_aTe = sem("probabilities_evacuated")
        s_o = sem("attention_products")
        s_oe = sem("attention_evacuated")
        s_ors = sem("head_rms")
        s_on = sem("heads_normalised")
        s_oT = sem("heads_transposed")
        s_cat = sem("concat_ready")
        s_y = sem("out_projection")
        s_ye = sem("out_projection_evacuated")
        s_yrs = sem("y_rms")
        s_x1 = sem("x1_ready")
        s_hrs = sem("h_rms")
        s_h = sem("h_ready")
        s_htp = sem("h_transposed")
        s_hte0 = sem("hT_evacuated")
        s_lg = sem("router_logits")
        s_lge = sem("router_exponentials")
        s_sel = sem("selection")
        s_rk = sem("ranks")
        s_bt = sem("block_columns")
        s_btr = sem("block_rows")
        s_tab = sem("block_table")
        s_oh = sem("onehot")
        s_im = sem("slot_products")
        s_sf = sem("slot_values_kept")
        s_gi = sem("gather_indices")
        s_gt = sem("gathered")
        s_xt = sem("block_transposed")
        s_xte = sem("block_evacuated")
        s_gu = sem("gate_up")
        s_sil = sem("block_silu")
        s_hm = sem("hidden")
        s_ht = sem("hidden_transposed")
        s_hte = sem("hidden_evacuated")
        s_si = sem("scatter_indices")
        s_dn = sem("down")
        s_yeA = sem("down_evacuated_act")
        s_yeD = sem("down_evacuated_dve")
        s_scat = sem("scattered")
        s_routed = sem("all_scattered")
        s_pinit = sem("buffers_cleared")
        s_yin = [sem(f"contributions_loaded{i}") for i in range(2)]
        s_comb = sem("contributions_summed")
        s_shp = sem("shared_gate_up")
        s_shs = sem("shared_silu")
        s_shm = sem("shared_hidden")
        s_shd = sem("shared_down")
        s_she = sem("shared_added")
        s_frs = sem("final_rms")
        s_fin = sem("final_ready")
        s_yfree = sem("y_buffer_free")
        s_pgo = sem("pool_passed")
        s_ca = sem("act_order")
        s_cd = sem("dve_order")

        block = ctx.enter_context(nc.Block())

        NSMALL = 12

        def kp(w, n):
            return w.rearrange("(p k) n -> p k n", k=n)

        @block.sync
        def _(sp):
            sp.dma_start(ctx_in, a["ctx"].rearrange("b (c p) d -> p (b c) d", p=P)).then_inc(s_ctx, 16)
            sp.dma_start(xres[:], a["x"].rearrange("b (c p) d -> p (b c) d", p=P)).then_inc(s_x, 16)
            wada = kp(a["w_ada"][0], KD)
            sp.dma_start(wa0, wada[:, :, 0:D]).then_inc(s_wa0, 16)
            sp.dma_start(wa1, wada[:, :, D:2 * D]).then_inc(s_wa1, 16)
            sp.dma_start(w_in, kp(a["w_in"][0], KD)).then_inc(s_win, 16)
            sp.wait_ge(s_tp, NC_ + NT)
            sp.dma_start(wpool, a["w_pool"][0].rearrange("g c e -> c g e")).then_inc(s_wpool, 16)
            for cc in range(8):
                if cc == 0:
                    sp.wait_ge(s_adc, 1)
                if cc == 2:
                    sp.wait_ge(s_ip, 22)
                    sp.dma_start(w_out, a["w_out"][0].rearrange("(j p) n -> p j n", p=P)).then_inc(s_wout, 16)
                    sp.wait_ge(s_pm, 4)
                    sp.dma_start(rows[:, :], a["b_ada"][0:1, 2 * D:6 * D].to_broadcast([P, 4 * D]),
                                 ).then_inc(s_brow, 16)
                    sp.dma_start(grow[:, 0, :], a["g_post_mix"].to_broadcast([P, D])).then_inc(s_grow, 16)
                    sp.dma_start(grow[:, 1, :], a["g_pre_ffn"].to_broadcast([P, D])).then_inc(s_grow, 16)
                if cc >= 2:
                    sp.wait_ge(s_adr, cc - 1)
                c0 = 2 * D + 512 * cc
                sp.dma_start(wac[cc % 2], wada[:, :, c0:c0 + 512]).then_inc(s_wac[cc % 2], 16)

            def load_expert(e, j):
                w = ring[:, j * EW:(j + 1) * EW]
                for s, name in enumerate(("w_e_gate", "w_e_up")):
                    sp.dma_start(w[:, s * KD * F:(s + 1) * KD * F],
                                 a[name][0, e].rearrange("(p k) f -> p (k f)", k=KD)).then_inc(s_we[j], 16)
                sp.dma_start(w[:, 2 * KD * F:], a["w_e_down"][0, e].rearrange("(p j) n -> p (j n)", j=FJ))\
                  .then_inc(s_we[j], 16)

            sp.wait_ge(s_adr, 8)
            load_expert(2, 2)
            load_expert(3, 3)
            sp.wait_ge(s_gac, 1)
            sp.dma_start(grow[:, 0, :], a["g_post_ffn"].to_broadcast([P, D])).then_inc(s_gpf, 16)
            sp.wait_ge(s_oT, HEADS)
            sp.dma_start(w_r, kp(a["w_router"][0], KD)).then_inc(s_wr, 16)
            sp.wait_ge(s_gac, 2)
            sp.dma_start(wsg, kp(a["w_sh_gate"][0], KD)).then_inc(s_wsh, 16)
            sp.dma_start(wsu, kp(a["w_sh_up"][0], KD)).then_inc(s_wsh, 16)
            sp.dma_start(wsd, a["w_sh_down"][0].rearrange("(j p) n -> p j n", p=P)).then_inc(s_wsh, 16)
            sp.wait_ge(s_y, NT)
            load_expert(0, 0)
            sp.wait_ge(s_fin, 1)
            load_expert(1, 1)
            sp.wait_ge(s_h, NT)
            sp.dma_start(brow, a["router_bias"].to_broadcast([P, E])).then_inc(s_rb, 16)
            sp.wait_ge(s_tab, 1)
            with sp.Fori(1, E // 4) as g:
                for j in range(4):
                    e = sp.snap(g * 4 + j)
                    done = sp.value_load(tab[0:1, bass.ds(e + (256 - 4), 1)], min_val=1, max_val=MAXB)
                    w = ring[:, j * EW:(j + 1) * EW]
                    srcs = [a["w_e_gate"][0, bass.ds(e, 1)].rearrange("a (p k) f -> p (a k f)", k=KD),
                            a["w_e_up"][0, bass.ds(e, 1)].rearrange("a (p k) f -> p (a k f)", k=KD),
                            a["w_e_down"][0, bass.ds(e, 1)].rearrange("a (p j) n -> p (a j n)", j=FJ)]
                    sp.wait_ge(s_dn, done)
                    for s in range(3):
                        sp.dma_start(w[:, s * KD * F:(s + 1) * KD * F], srcs[s]).then_inc(s_we[j], 16)
            sp.wait_ge(s_routed, 1)
            for t in range(NT):
                if t >= 2:
                    sp.wait_ge(s_comb, t - 1)
                sp.dma_start(yin[t % 2], ybuf[t * P * TOPK:(t + 1) * P * TOPK, :]
                             .rearrange("(p k) n -> p (k n)", k=TOPK)).then_inc(s_yin[t % 2], 16)
            for t in range(NT):
                sp.wait_ge(s_fin, t + 2)
                sp.dma_start(out[0, t * P:(t + 1) * P, :], acc[:, t, :]).then_inc(s_out, 16)
            sp.wait_ge(s_out, 16 * NT)

        @block.gpsimd
        def _(pool):
            pool.wait_ge(s_htp, NT)
            pool.wait_ge(s_hst, 16 * NT)
            pool.memset(xg, 0.0).then_inc(s_pinit, 1)
            pool.wait_ge(s_pinit, 1)
            nb = None

            def gather():
                pool.indirect_dma_start(xg, None, hbuf[:, :], bass.IndirectOffsetOnAxis(gidx[:, 0:1], 0),
                                        bounds_check=T - 1, oob_is_err=False).then_inc(s_gt, 16)

            pool.wait_ge(s_gi, 1)
            gather()
            pool.sem_inc(s_yfree, 1)
            nb = pool.value_load(ntab[0:1, 0:1], min_val=E, max_val=MAXB - 1)
            with pool.Fori(0, nb) as b:
                n1 = pool.snap(b + 1)
                n2 = pool.snap(b + 2)
                n16 = pool.snap(b * 16 + 16)
                pool.wait_ge(s_xt, n1)
                pool.wait_ge(s_gi, n2)
                pool.sem_inc(s_pgo, 1)
                gather()
                pool.wait_ge(s_yeA, n2)
                pool.wait_ge(s_yeD, n2)
                pool.wait_ge(s_si, n1)
                pool.sem_inc(s_pgo, 1)
                pool.indirect_dma_start(ybuf[:, :], bass.IndirectOffsetOnAxis(sidx[:, 0:1], 0), ysb, None,
                                        bounds_check=T * TOPK - 1, oob_is_err=False).then_inc(s_scat, 16)
                pool.wait_ge(s_scat, n16)
                pool.sem_inc(s_yfree, 1)
            n_gt = pool.snap(nb * 16 + 16)
            pool.wait_ge(s_gt, n_gt)
            pool.sem_inc(s_routed, 1)

        @block.scalar
        def _(act):
            order = [0]

            def then(ins):
                order[0] += 1
                ins.then_inc(s_ca, 1)
                act.wait_ge(s_ca, order[0])

            act.dma_start(cst[:], a["consts"]).then_inc(s_small, 16)
            act.dma_start(c2[:, 0, :], a["c"][0].rearrange("(p k) -> p k", k=KD)).then_inc(s_small, 16)
            act.dma_start(c2[:, 1, :], a["c_ctx"].rearrange("(p k) -> p k", k=KD)).then_inc(s_small, 16)
            act.dma_start(gcol, a["g_pre_mix"][0].rearrange("(p k) -> p k", k=KD)).then_inc(s_small, 16)
            act.dma_start(bcol, a["b_ada"][0, 0:2 * D].rearrange("(r p k) -> p r k", r=2, k=KD)).then_inc(s_small, 16)
            with nc.allow_non_contiguous_dma(reason="three short vectors as columns"):
                act.dma_start(gsub, a["g_subln"][0].rearrange("(p k) -> p k", k=1)).then_inc(s_small, 16)
                act.dma_start(bpool, a["b_pool"][0].rearrange("(g p) -> p g", p=P)).then_inc(s_small, 16)
                act.dma_start(pscale, a["pool_scale"][0].rearrange("(g p) -> p g", p=P)).then_inc(s_small, 16)
            for i, name in enumerate(("lambda_q1", "lambda_k1", "lambda_q2", "lambda_k2")):
                act.dma_start(lamv[:, i, :], a[name].to_broadcast([P, 64])).then_inc(s_small, 16)
            act.wait_ge(s_small, 16 * NSMALL)
            act.activation(sc2.rearrange("p k s -> p s k"), c2, ACT.Silu).then_inc(s_silc, 1)
            for t in range(NC_ + NT):
                if t == 0:
                    act.wait_ge(s_ctx, 16)
                if t == NC_:
                    act.wait_ge(s_x, 16)
                src = ctx_in[:, t, :] if t < NC_ else xres[:, t - NC_, :]
                then(act.activation(actT[:, 0:D], src, ACT.Square, accum_out=ssq[:, t:t + 1]))
            act.activation(rstd, ssq, ACT.Sqrt, scale=1.0 / D, bias=cst[:, C_EPS:C_EPS + 1]).then_inc(s_sq, 1)
            for t in range(NC_ + NT):
                act.wait_ge(s_tp, t + 1)
                dst = hcT[:, :, t * P:(t + 1) * P] if t < NC_ else hxT[:, :, (t - NC_) * P:(t - NC_ + 1) * P]
                act.copy(dst, pp[t % 2][:, :].rearrange("p (k t) -> p k t", k=KD)).then_inc(s_tev, 1)
            act.wait_ge(s_mod, 1)
            then(act.activation(dots, dots, ACT.Exp))
            act.sem_inc(s_sq, 1)
            for n in range(22):
                bank = pp[(n % 4) // 2][:, 512 * (n % 2):512 * (n % 2) + 512]
                act.wait_ge(s_ip, n + 1)
                if n < 4:
                    act.copy(kT[:, n, 0:CTX], bank[:, 0:CTX]).then_inc(s_ipe, 1)
                elif n < 12:
                    if n >= 6:
                        act.wait_ge(s_rope, n - 5)
                    act.copy(raw[:, n % 2, :], bank).then_inc(s_ipe, 1)
                elif n < 16:
                    act.copy(pT[:, n - 12, :], bank).then_inc(s_ipe, 1)
                else:
                    act.copy(vv[:, n - 16, :], bank).then_inc(s_ipe, 1)
            for u in range(16):
                act.wait_ge(s_nmx, u + 1)
                if u:
                    act.wait_ge(s_a, u)
                for s in range(2):
                    act.activation(e12[:, s, :], pp[s][:, 0:KEYS], ACT.Exp, bias=nmx[:, s:s + 1], scale=SCALE,
                                   accum_out=lsum[:, s:s + 1]).then_inc(s_exp, 1)
                act.wait_ge(s_aTp, u + 1)
                if u >= 2:
                    act.wait_ge(s_o, u - 1)
                act.copy(aT[:, u % 2], pp[2][:, 0:KEYS].rearrange("p (c q) -> p c q", c=NKEY)).then_inc(s_aTe, 1)
                act.wait_ge(s_o, u + 1)
                then(act.copy(oall[:, u, :], pp[3][:, 0:P]))
                then(act.activation(junk[:, 0:P], oall[:, u, :], ACT.Square, accum_out=ossq[:, u:u + 1]))
                act.sem_inc(s_oe, 1)
            act.activation(orst, ossq, ACT.Sqrt, scale=1.0 / P, bias=cst[:, C_EPS:C_EPS + 1]).then_inc(s_ors, 1)
            for t in range(NT):
                act.wait_ge(s_y, t + 1)
                then(act.copy(y1[:, t, :], pp[t][:, :]))
                then(act.activation(junk, y1[:, t, :], ACT.Square, accum_out=yssq[:, t:t + 1]))
                act.activation(yrst[:, t:t + 1], yssq[:, t:t + 1], ACT.Sqrt, scale=1.0 / D,
                               bias=cst[:, C_EPS:C_EPS + 1]).then_inc(s_yrs, 1)
            for t in range(NT):
                act.wait_ge(s_x1, t + 1)
                then(act.activation(junk, xres[:, t, :], ACT.Square, accum_out=hssq[:, t:t + 1]))
                act.activation(hrst[:, t:t + 1], hssq[:, t:t + 1], ACT.Sqrt, scale=1.0 / D,
                               bias=cst[:, C_EPS:C_EPS + 1]).then_inc(s_hrs, 1)
            act.sem_inc(s_fin, 1)
            for t in range(NT):
                act.wait_ge(s_h, t + 1)
                act.dma_start(hbuf[t * P:(t + 1) * P, :], y1[:, t, :]).then_inc(s_hst, 16)
            for t in range(NT):
                act.wait_ge(s_htp, t + 1)
                act.copy(hT[:, :, t * P:(t + 1) * P], pp[t][:, :].rearrange("p (k t) -> p k t", k=KD))\
                   .then_inc(s_hte0, 1)
            act.wait_ge(s_lg, 1)
            act.activation(rt[:, 0, :], pp[0][:, 0:NT * E], ACT.Exp, scale=-1.0).then_inc(s_lge, 1)

            def evacuate_block(n):
                act.wait_ge(s_xt, n)
                act.copy(xT, pp[1][:, :].rearrange("p (k s) -> p k s", k=KD)).then_inc(s_xte, 1)

            evacuate_block(1)
            act.sem_inc(s_yeA, 1)
            act.wait_ge(s_tab, 1)
            nb = act.value_load(ntab[0:1, 0:1], min_val=E, max_val=MAXB - 1)
            with act.Fori(0, nb) as b:
                act.wait_ge(s_gu, b + 1)
                act.activation(sg, pp[2][:, 0:F], ACT.Silu).then_inc(s_sil, 1)
                evacuate_block(b + 2)
                act.wait_ge(s_dn, b + 1)
                act.wait_ge(s_yfree, b + 1)
                act.copy(ysb[:, 512:], pp[0][:, 512:]).then_inc(s_yeA, 1)
            for j in range(FJ):
                act.wait_ge(s_shp, j + 1)
                act.activation(sgs[:, j, :], pp[0][:, 512 * j:512 * j + 512], ACT.Silu).then_inc(s_shs, 1)
            for t in range(NT):
                act.wait_ge(s_she, t + 1)
                then(act.activation(heads[:, 6144:7168], acc[:, t, :], ACT.Square, accum_out=fssq[:, t:t + 1]))
                act.activation(frst[:, t:t + 1], fssq[:, t:t + 1], ACT.Sqrt, scale=1.0 / D,
                               bias=cst[:, C_EPS:C_EPS + 1]).then_inc(s_frs, 1)

        @block.tensor
        def _(pe):
            pe.wait_ge(s_small, 16 * NSMALL)
            for t in range(NC_ + NT):
                pe.wait_ge(s_xn, t + 1)
                if t >= 2:
                    pe.wait_ge(s_tev, t - 1)
                for k in range(KD):
                    last = pe.transpose(pp[t % 2][:, k * P:(k + 1) * P], xn[:, t % 4, k, :], ident)
                last.then_inc(s_tp, 1)
            pe.wait_ge(s_silc, 1)
            for r, (w, s) in enumerate(((wa0, s_wa0), (wa1, s_wa1))):
                pe.wait_ge(s, 16)
                for k in range(KD):
                    o = pp[2][:, (r * KD + k) * 2:(r * KD + k) * 2 + 2]
                    for kk in range(KD):
                        last = pe.matmul(o, w[:, kk, :].rearrange("p (q k) -> p k q", k=KD)[:, k, :],
                                         sc2[:, kk, :], start=(kk == 0), stop=(kk == KD - 1))
                last.then_inc(s_adc, 1)
            pe.wait_ge(s_win, 16)
            pe.wait_ge(s_mod, 1)
            pe.wait_ge(s_tev, NC_ + NT)
            for n in range(22):
                bank = pp[(n % 4) // 2][:, 512 * (n % 2):512 * (n % 2) + 512]
                if n >= 4:
                    pe.wait_ge(s_ipe, n - 3)
                for k in range(KD):
                    if n < 4:
                        o, l, r = bank[:, 0:CTX], w_in[:, k, 512 + n * P:512 + (n + 1) * P], hcT[:, k, :]
                    elif n < 16:
                        c0 = (n - 4) * P if n < 12 else 1536 + (n - 12) * P
                        o, l, r = bank, w_in[:, k, c0:c0 + P], hxT[:, k, :]
                    else:
                        i = n - 16
                        l = hcT[:, k, i * P:(i + 1) * P] if i < NC_ else hxT[:, k, (i - NC_) * P:(i - NC_ + 1) * P]
                        o, r = bank, w_in[:, k, 1024:1536]
                    last = pe.matmul(o, l, r, start=(k == 0), stop=(k == KD - 1))
                last.then_inc(s_ip, 1)
            pe.wait_ge(s_wpool, 16)
            pe.wait_ge(s_ipe, 22)
            for g in range(4):
                pe.wait_ge(s_pd, g + 1)
                pe.matmul(pp[g // 2][:, 512 * (g % 2):512 * (g % 2) + 512], wpool[:, g, :], pT[:, g, :],
                          start=True, stop=True).then_inc(s_pm, 1)
            for cc in range(8):
                pe.wait_ge(s_wac[cc % 2], 16 * (cc // 2 + 1))
                if cc >= 4:
                    pe.wait_ge(s_adre, cc - 3)
                else:
                    pe.wait_ge(s_mod, 1)
                for kk in range(KD):
                    last = pe.matmul(pp[2 + (cc % 4) // 2][:, 512 * (cc % 2):512 * (cc % 2) + 512],
                                     sc2[:, kk, 0:1].to_broadcast([P, P]), wac[cc % 2][:, kk, :],
                                     start=(kk == 0), stop=(kk == KD - 1))
                last.then_inc(s_adr, 1)

            def scores(u):
                h, qb = divmod(u, NT)
                if u:
                    pe.wait_ge(s_exp, 2 * u)
                for s in range(2):
                    for c0, n in ((0, 512), (512, 256)):
                        last = pe.matmul(pp[s][:, c0:c0 + n], qT[64 * s:64 * s + 64, h, qb * P:(qb + 1) * P],
                                         kT[64 * s:64 * s + 64, h, c0:c0 + n], start=True, stop=True)
                last.then_inc(s_sc, 1)

            pe.wait_ge(s_rope, 8)
            pe.wait_ge(s_poolout, 4)
            pe.wait_ge(s_adre, 8)
            scores(0)
            for u in range(16):
                if u + 1 < 16:
                    scores(u + 1)
                h = u // NT
                pe.wait_ge(s_a, u + 1)
                if u:
                    pe.wait_ge(s_aTe, u)
                for c in range(NKEY):
                    last = pe.transpose(pp[2][:, c * P:(c + 1) * P], e12[:, 0, c * P:(c + 1) * P], ident)
                last.then_inc(s_aTp, 1)
                pe.wait_ge(s_aTe, u + 1)
                if u:
                    pe.wait_ge(s_oe, u)
                for c in range(NKEY):
                    last = pe.matmul(pp[3][:, 0:P], aT[:, u % 2, c, :], vv[:, c, h * P:(h + 1) * P],
                                     start=(c == 0), stop=(c == NKEY - 1))
                last.then_inc(s_o, 1)
            pe.wait_ge(s_oe, 16)
            pe.wait_ge(s_on, 1)
            for h in range(HEADS):
                for qb in range(NT):
                    c0 = 512 * (h % 2) + qb * P
                    last = pe.transpose(pp[2 + h // 2][:, c0:c0 + P], oall[:, h * NT + qb, :], ident)
                last.then_inc(s_oT, 1)
            pe.wait_ge(s_wout, 16)
            pe.wait_ge(s_cat, HEADS)
            for t in range(NT):
                for n in range(2):
                    for j in range(KD):
                        last = pe.matmul(pp[t][:, 512 * n:512 * n + 512], catT[:, j, t * P:(t + 1) * P],
                                         w_out[:, j, 512 * n:512 * n + 512], start=(j == 0), stop=(j == KD - 1))
                last.then_inc(s_y, 1)
            for t in range(NT):
                pe.wait_ge(s_h, t + 1)
                for k in range(KD):
                    last = pe.transpose(pp[t][:, k * P:(k + 1) * P], y1[:, t, k * P:(k + 1) * P], ident)
                last.then_inc(s_htp, 1)
            pe.wait_ge(s_wr, 16)
            pe.wait_ge(s_hte0, NT)
            for t in range(NT):
                for k in range(KD):
                    last = pe.matmul(pp[0][:, t * E:(t + 1) * E], hT[:, k, t * P:(t + 1) * P], w_r[:, k, :],
                                     start=(k == 0), stop=(k == KD - 1))
            last.then_inc(s_lg, 1)
            pe.wait_ge(s_sel, 1)
            for t in range(NT):
                for c in range(t + 1):
                    pe.matmul(pp[1][:, t * E:(t + 1) * E], ones if c < t else cst[:, C_TRI:C_TRI + P],
                              selt[:, c, :], start=(c == 0), stop=(c == t))
            for c in range(NT):
                last = pe.matmul(pp[1][:, 512:512 + E], ones, selt[:, c, :], start=(c == 0), stop=(c == NT - 1))
            last.then_inc(s_rk, 1)
            pe.wait_ge(s_bt, 1)
            for i in range(3):
                last = pe.matmul(pp[2][0:1, i * P:(i + 1) * P], btab[:, i:i + 1], ident, start=True, stop=True)
            last.then_inc(s_btr, 1)

            def slots(eb, n):
                pe.wait_ge(s_oh, n)
                for c in range(NT):
                    last = pe.matmul(pp[3][:, 0:4], oneh[:, c, :],
                                     rtab[:, c, :, :].rearrange("p e w -> p (e w)")[:, bass.ds(eb * 4, 4)],
                                     start=(c == 0), stop=(c == NT - 1))
                last.then_inc(s_im, 1)

            def transpose_block(gathered):
                pe.wait_ge(s_gt, gathered)
                for k in range(KD):
                    last = pe.transpose(pp[1][:, k * P:(k + 1) * P], xg[:, k * P:(k + 1) * P], ident)
                last.then_inc(s_xt, 1)

            pe.wait_ge(s_tab, 1)
            slots(pe.value_load(tab[0:1, 0:1], min_val=0, max_val=E - 1), 1)
            transpose_block(16)
            nb = pe.value_load(ntab[0:1, 0:1], min_val=E, max_val=MAXB - 1)
            wflat = ring[:, :]
            with pe.Fori(0, nb) as b:
                eb = pe.value_load(tab[0:1, bass.ds(b, 1)], min_val=0, max_val=E - 1)
                en = pe.value_load(tab[0:1, bass.ds(b + 1, 1)], min_val=0, max_val=E - 1)
                el = pe.value_load(tab[0:1, bass.ds(b + 320, 1)], min_val=3, max_val=E - 1)
                pe.wait_ge(s_sf, b + 1)
                slots(en, b + 2)
                for j in range(4):
                    pe.wait_ge(s_we[j], ((el + (4 - j)) // 4) * 48)
                w0 = pe.snap((eb % 4) * EW)
                pe.wait_ge(s_xte, b + 1)
                pe.wait_ge(s_hm, b + 1)
                gu = wflat[:, bass.ds(w0, 2 * KD * F)].rearrange("p (s k f) -> p s k f", s=2, k=KD)
                for k in range(KD):
                    last = pe.matmul(pp[2][:, 0:2 * F].rearrange("p (s f) -> p s f", s=2), xT[:, k, :], gu[:, :, k, :],
                                     start=(k == 0), stop=(k == KD - 1))
                last.then_inc(s_gu, 1)
                transpose_block(b * 16 + 32)
                pe.wait_ge(s_hm, b + 2)
                pe.wait_ge(s_hte, b + 1)
                for j in range(FJ):
                    last = pe.transpose(pp[2][:, 512 + j * P:512 + (j + 1) * P], hmid[:, j, :], ident)
                last.then_inc(s_ht, 1)
                pe.wait_ge(s_hte, b + 2)
                pe.wait_ge(s_yeA, b + 1)
                pe.wait_ge(s_yeD, b + 1)
                dn = wflat[:, bass.ds(w0 + 2 * KD * F, FJ * D)]
                for n in range(2):
                    for j in range(FJ):
                        last = pe.matmul(pp[0][:, 512 * n:512 * n + 512], hTs[:, j, :],
                                         dn[:, j * D + 512 * n:j * D + 512 * n + 512],
                                         start=(j == 0), stop=(j == FJ - 1))
                last.then_inc(s_dn, 1)
            pe.wait_ge(s_wsh, 48)
            pe.wait_ge(s_yeA, nb + 1)
            pe.wait_ge(s_yeD, nb + 1)
            pe.wait_ge(s_xte, nb + 1)
            for j in range(FJ):
                for s, w in enumerate((wsg, wsu)):
                    for k in range(KD):
                        last = pe.matmul(pp[s][:, 512 * j:512 * j + 512], w[:, k, j * P:(j + 1) * P], hT[:, k, :],
                                         start=(k == 0), stop=(k == KD - 1))
                last.then_inc(s_shp, 1)
            pe.wait_ge(s_shm, FJ)
            for t in range(NT):
                if t >= 2:
                    pe.wait_ge(s_she, t - 1)
                for n in range(2):
                    for j in range(FJ):
                        last = pe.matmul(pp[2 + t % 2][:, 512 * n:512 * n + 512], hs[:, j, t * P:(t + 1) * P],
                                         wsd[:, j, 512 * n:512 * n + 512], start=(j == 0), stop=(j == FJ - 1))
                last.then_inc(s_shd, 1)

        @block.vector
        def _(dve):
            order = [0]

            def then(ins):
                order[0] += 1
                ins.then_inc(s_cd, 1)
                dve.wait_ge(s_cd, order[0])

            dve.wait_ge(s_sq, 1)
            then(dve.reciprocal(rstd, rstd))
            for t in range(NC_ + NT):
                src = ctx_in[:, t, :] if t < NC_ else xres[:, t - NC_, :]
                if t >= 4:
                    dve.wait_ge(s_tp, t - 3)
                dve.tensor_scalar(xn[:, t % 4], src.rearrange("p (q k) -> p k q", k=KD), rstd[:, t:t + 1], None,
                                  ALU.mult).then_inc(s_xn, 1)
            for i in range(2):
                then(dve.tensor_tensor_reduce(lamv[:, 2 * i, :], lamv[:, 2 * i, :], lamv[:, 2 * i + 1, :], 1.0, 0.0,
                                              ALU.mult, ALU.add, dots[:, i:i + 1]))
            dve.wait_ge(s_adc, 2)
            for r in range(2):
                then(dve.tensor_tensor(modc[:, r], pp[2][:, r * 16:r * 16 + 16].rearrange("p (k s) -> p k s", s=2),
                                       bcol[:, r, :].rearrange("p (k s) -> p k s", s=1).to_broadcast([P, KD, 2]),
                                       ALU.add))
            then(dve.scalar_tensor_tensor(modc[:, 1], modc[:, 1], 1.0,
                                          gcol.rearrange("p (k s) -> p k s", s=1).to_broadcast([P, KD, 2]),
                                          ALU.add, ALU.mult))
            dve.wait_ge(s_tev, NC_ + NT)
            for k in range(KD):
                for s, x in ((1, hcT), (0, hxT)):
                    last = dve.tensor_scalar(x[:, k, :], x[:, k, :], modc[:, 1, k, s:s + 1], modc[:, 0, k, s:s + 1],
                                             ALU.mult, ALU.add)
            then(last)
            dve.sem_inc(s_mod, 1)
            mask = [(i + 16) % 32 for i in range(32)]
            cos, sin = cst[:, C_ROPE:C_ROPE + T], cst[:, C_ROPE + T:C_ROPE + 2 * T]
            for n in range(4, 12):
                h = (n - 4) % HEADS
                dst = qT[:, h, :] if n < 8 else kT[:, h, CTX:]
                r = raw[:, n % 2, :]
                dve.wait_ge(s_ipe, n + 1)
                then(dve.stream_shuffle(swp, r, mask))
                then(dve.tensor_tensor(dst, r, cos, ALU.mult))
                then(dve.tensor_tensor(swp, swp, sin, ALU.mult))
                then(dve.tensor_tensor(dst, dst, swp, ALU.add))
                dve.sem_inc(s_rope, 1)
            for g, w in enumerate(WINDOWS):
                p = pT[:, g, :]
                dve.wait_ge(s_ipe, 13 + g)
                cur, nxt = sumA, sumB
                then(dve.memset(cur, 0.0))
                then(dve.tensor_copy(cur[:, PAD:PAD + T], p))
                then(dve.tensor_tensor(nxt[:, 1:], cur[:, :TP - 1], cur[:, 1:], ALU.add))
                m = 1
                while m < w // 2:
                    cur, nxt = nxt, cur
                    lo, hi = 2 * m, TP - 2 * m + 1
                    then(dve.tensor_tensor(nxt[:, lo:hi], cur[:, lo - m:hi - m], cur[:, lo + m:hi + m], ALU.add))
                    m *= 2
                cur = nxt[:, PAD:PAD + T]
                fac = cst[:, C_FAC + 16 * g:C_FAC + 16 * g + 16]
                then(dve.tensor_tensor(cur[:, 0:8], cur[:, 0:8], fac[:, 0:8], ALU.mult))
                then(dve.tensor_tensor(cur[:, T - 8:], cur[:, T - 8:], fac[:, 8:16], ALU.mult))
                then(dve.scalar_tensor_tensor(p, cur, 1.0 / w, p, ALU.mult, ALU.subtract))
                dve.sem_inc(s_pd, 1)
            for g in range(4):
                dve.wait_ge(s_pm, g + 1)
                dve.tensor_scalar(catT[:, 4 + g, :], pp[g // 2][:, 512 * (g % 2):512 * (g % 2) + 512],
                                  bpool[:, g:g + 1], pscale[:, g:g + 1], ALU.add, ALU.mult).then_inc(s_poolout, 1)
            dve.wait_ge(s_brow, 16)
            for cc in range(8):
                dve.wait_ge(s_adr, cc + 1)
                dst = rows[:, 512 * cc:512 * cc + 512]
                dve.tensor_tensor(dst, dst, pp[2 + (cc % 4) // 2][:, 512 * (cc % 2):512 * (cc % 2) + 512],
                                  ALU.add).then_inc(s_adre, 1)
            dve.wait_ge(s_adre, 8)
            dve.wait_ge(s_grow, 32)
            then(dve.tensor_tensor(arow[:, 0], arow[:, 0], grow[:, 0], ALU.mult))
            dve.scalar_tensor_tensor(arow[:, 2], arow[:, 2], 1.0, grow[:, 1], ALU.add, ALU.mult).then_inc(s_gac, 1)
            dve.wait_ge(s_sq, 2)
            then(dve.tensor_tensor(lam, dots[:, 1:2], dots[:, 0:1], ALU.subtract))
            then(dve.tensor_scalar(lam, lam, LAM_INIT, None, ALU.subtract))
            for u in range(16):
                dve.wait_ge(s_sc, u + 1)
                for s in range(2):
                    last = dve.tensor_reduce(mx[:, s:s + 1], pp[s][:, 0:KEYS], AX, ALU.max)
                then(last)
                dve.tensor_scalar(nmx, mx, -SCALE, None, ALU.mult).then_inc(s_nmx, 1)
                dve.wait_ge(s_exp, 2 * u + 2)
                then(dve.reciprocal(rl, lsum))
                then(dve.tensor_tensor(rl[:, 1:2], rl[:, 1:2], lam, ALU.mult))
                then(dve.tensor_scalar(e12[:, 1, :], e12[:, 1, :], rl[:, 1:2], None, ALU.mult))
                dve.scalar_tensor_tensor(e12[:, 0, :], e12[:, 0, :], rl[:, 0:1], e12[:, 1, :],
                                         ALU.mult, ALU.add).then_inc(s_a, 1)
            dve.wait_ge(s_ors, 1)
            then(dve.reciprocal(orst, orst))
            for u in range(16):
                last = dve.tensor_scalar(oall[:, u, :], oall[:, u, :], orst[:, u:u + 1], 1.0 - LAM_INIT,
                                         ALU.mult, ALU.mult)
            last.then_inc(s_on, 1)
            for h in range(HEADS):
                dve.wait_ge(s_oT, h + 1)
                dve.tensor_scalar(catT[:, h, :], pp[2 + h // 2][:, 512 * (h % 2):512 * (h % 2) + 512], gsub, None,
                                  ALU.mult).then_inc(s_cat, 1)
            dve.wait_ge(s_gpf, 16)
            dve.tensor_tensor(arow[:, 3], arow[:, 3], grow[:, 0], ALU.mult).then_inc(s_gac, 1)
            for t in range(NT):
                dve.wait_ge(s_yrs, t + 1)
                then(dve.reciprocal(yrst[:, t:t + 1], yrst[:, t:t + 1]))
                then(dve.scalar_tensor_tensor(y1[:, t, :], y1[:, t, :], yrst[:, t:t + 1], arow[:, 0],
                                              ALU.mult, ALU.mult))
                dve.tensor_tensor(xres[:, t, :], xres[:, t, :], y1[:, t, :], ALU.add).then_inc(s_x1, 1)
            for t in range(NT):
                dve.wait_ge(s_hrs, t + 1)
                then(dve.reciprocal(hrst[:, t:t + 1], hrst[:, t:t + 1]))
                perm = y1[:, t, :].rearrange("p (k q) -> p k q", k=KD)
                then(dve.scalar_tensor_tensor(perm, xres[:, t, :].rearrange("p (q k) -> p k q", k=KD),
                                              hrst[:, t:t + 1], arow[:, 2].rearrange("p (q k) -> p k q", k=KD),
                                              ALU.mult, ALU.mult))
                dve.tensor_tensor(perm, perm, arow[:, 1].rearrange("p (q k) -> p k q", k=KD), ALU.add)\
                   .then_inc(s_h, 1)
            ex, bi, msk, tmp, inc = (rt[:, i, :].rearrange("p (c e) -> p c e", c=NT) for i in range(5))
            dve.wait_ge(s_hst, 16 * NT)
            dve.wait_ge(s_lge, 1)
            dve.wait_ge(s_rb, 16)
            then(dve.tensor_scalar(tmp, ex, 1.0, None, ALU.add))
            then(dve.reciprocal(sct, tmp))
            then(dve.tensor_tensor(bi, sct, brow.rearrange("p (c e) -> p c e", c=1).to_broadcast([P, NT, E]),
                                   ALU.add))
            for t in range(NT):
                for g in range(8):
                    last = dve.max(m8[:, (t * 8 + g) * 8:(t * 8 + g) * 8 + 8], bi[:, t, g * 8:g * 8 + 8])
            then(last)
            top = m8.rearrange("p (n s) -> p n s", s=8)
            gs = tnb[:, 0:32]
            then(dve.tensor_tensor(gs.rearrange("p (n s) -> p n s", s=1), top[:, :, 0:1], top[:, :, 1:2], ALU.add))
            gone = rt[:, 3, :]
            for t in range(NT):
                gj = gs[:, t * 8:t * 8 + 8].rearrange("p (a j) -> p a j", a=1).to_broadcast([P, 8, 8])
                gi = gs[:, t * 8:t * 8 + 8].rearrange("p (i a) -> p i a", a=1).to_broadcast([P, 8, 8])
                x = tmp[:, t, :].rearrange("p (i j) -> p i j", i=8)
                y = inc[:, t, :].rearrange("p (i j) -> p i j", i=8)
                then(dve.tensor_tensor(x, gj, gi, ALU.is_equal))
                then(dve.tensor_tensor(x, x, cst[:, C_JLT:C_JLT + 64].rearrange("p (i j) -> p i j", i=8), ALU.mult))
                then(dve.tensor_tensor(y, gj, gi, ALU.is_gt))
                then(dve.tensor_tensor(x, x, y, ALU.add))
                then(dve.tensor_reduce(tnb[:, 32 + t * 8:40 + t * 8], x, AX, ALU.add))
            then(dve.tensor_scalar(tnb[:, 64:96], tnb[:, 32:64], 4.0, None, ALU.is_lt))
            then(dve.tensor_scalar(tnb[:, 96:128], tnb[:, 64:96], 1.0, 1e30, ALU.subtract, ALU.mult))
            for t in range(NT):
                def spread(c0):
                    return tnb[:, c0 + t * 8:c0 + t * 8 + 8].rearrange("p (g a) -> p g a", a=1).to_broadcast([P, 8, 8])
                b3 = bi[:, t, :].rearrange("p (g j) -> p g j", g=8)
                then(dve.tensor_tensor(b3, b3, spread(64), ALU.mult))
                then(dve.tensor_tensor(b3, b3, spread(96), ALU.add))
                then(dve.max(m8[:, 0:8], bi[:, t, :]))
                then(dve.match_replace(out=msk[:, t, :], in_to_replace=m8[:, 0:8], in_values=bi[:, t, :],
                                       imm_value=3e38))
            then(dve.tensor_scalar(selt, msk, 2e38, None, ALU.is_ge))
            dve.sem_inc(s_sel, 1)
            then(dve.tensor_tensor(sct, sct, selt, ALU.mult))
            then(dve.tensor_reduce(rsum, sct, AX, ALU.add))
            then(dve.reciprocal(rsum, rsum))
            for t in range(NT):
                then(dve.tensor_scalar(rtab[:, t, :, 2], sct[:, t, :], rsum[:, t:t + 1], ROUTED_SCALE,
                                       ALU.mult, ALU.mult))
                then(dve.tensor_tensor_scan(inc[:, t, :], ones[:, 0:E], selt[:, t, :], 0.0, ALU.mult, ALU.add))
                then(dve.tensor_tensor(inc[:, t, :], inc[:, t, :], selt[:, t, :], ALU.subtract))
                then(dve.tensor_scalar(rtab[:, t, :, 1], inc[:, t, :], cst[:, C_TOK8 + t:C_TOK8 + t + 1], None,
                                       ALU.add))
                then(dve.tensor_scalar(rtab[:, t, :, 0], ones[:, 0:E], cst[:, C_TOK + t:C_TOK + t + 1], None,
                                       ALU.mult))
                then(dve.memset(rtab[:, t, :, 3], 0.0))
            dve.wait_ge(s_rk, 1)
            then(dve.tensor_scalar(tmp, pp[1][:, 0:NT * E].rearrange("p (c e) -> p c e", c=NT), 1.0, None, ALU.add))
            then(dve.tensor_tensor(tmp, tmp, selt, ALU.mult))
            then(dve.tensor_scalar(key, tmp, 1.0, None, ALU.subtract))
            nblk, cum, t64 = tnb[:, 0:64], tnb[:, 64:128], tnb[:, 128:192]
            then(dve.tensor_copy(t64, pp[1][:, 512:512 + E]))
            then(dve.tensor_scalar(nblk, t64, 128.5, 1.0, ALU.is_ge, ALU.add))
            for th in (256.5, 384.5):
                then(dve.scalar_tensor_tensor(nblk, t64, th, nblk, ALU.is_ge, ALU.add))
            then(dve.tensor_tensor_scan(cum, ones[:, 0:E], nblk, 0.0, ALU.mult, ALU.add))
            part = cst[:, C_PART:C_PART + 1]
            then(dve.tensor_scalar(t64, cum, part, None, ALU.is_le))
            then(dve.tensor_reduce(btab[:, 0:1], t64, AX, ALU.add))
            then(dve.tensor_tensor(t64, t64, nblk, ALU.mult))
            then(dve.tensor_reduce(btab[:, 1:2], t64, AX, ALU.add))
            then(dve.tensor_scalar(btab[:, 2:3], btab[:, 0:1], 63.5, 1000.0, ALU.is_ge, ALU.mult))
            then(dve.tensor_scalar(btab[:, 0:1], btab[:, 0:1], float(E - 1), None, ALU.min))
            then(dve.tensor_tensor(btab[:, 1:2], part, btab[:, 1:2], ALU.subtract))
            then(dve.scalar_tensor_tensor(btab[:, 1:2], btab[:, 1:2], float(P), btab[:, 2:3], ALU.mult, ALU.add))
            then(dve.tensor_scalar(btab[:, 1:2], btab[:, 1:2], 512.0, None, ALU.min))
            then(dve.tensor_scalar(btab[:, 2:3], btab[:, 0:1], 3.0, None, ALU.max))
            dve.sem_inc(s_bt, 1)
            dve.wait_ge(s_btr, 1)
            then(dve.tensor_copy(tab[0:1, 320:448], pp[2][0:1, 256:384]))
            then(dve.tensor_copy(tab[0:1, 0:256], pp[2][0:1, 0:256]))
            then(dve.tensor_copy(tab[0:1, 256:320], cum[0:1, :]))
            then(dve.tensor_copy(ntab[0:1, 0:1], cum[0:1, E - 1:E]))
            dve.sem_inc(s_tab, 1)

            def onehots(eb, r0):
                for c in range(NT):
                    last = dve.tensor_scalar(oneh[:, c, :], cst[:, bass.ds(r0 + C_IOTA, P)],
                                             key[:, c, bass.ds(eb, 1)], None, ALU.is_equal)
                last.then_inc(s_oh, 1)

            def block_of(b):
                return (dve.value_load(tab[0:1, bass.ds(b, 1)], min_val=0, max_val=E - 1),
                        dve.value_load(tab[0:1, bass.ds(b + P, 1)], min_val=0, max_val=512))

            def gather_index(n):
                dve.wait_ge(s_im, n)
                dve.tensor_scalar(gidx[:, 0:1], pp[3][:, 0:1], FAR, None, ALU.add).then_inc(s_gi, 1)

            for s in (s_hm, s_hte, s_yeD):
                dve.sem_inc(s, 1)
            onehots(*block_of(0))
            gather_index(1)
            dve.tensor_copy(slotf[:], pp[3][:, 0:4]).then_inc(s_sf, 1)
            onehots(*block_of(1))
            nb = dve.value_load(ntab[0:1, 0:1], min_val=E, max_val=MAXB - 1)
            with dve.Fori(0, nb) as b:
                e2, r2 = block_of(b + 2)
                dve.wait_ge(s_gt, b * 16 + 16)
                gather_index(b + 2)
                onehots(e2, r2)
                dve.wait_ge(s_sil, b + 1)
                dve.wait_ge(s_sf, b + 1)
                dve.scalar_tensor_tensor(hmid.rearrange("p j q -> p q j"), sg.rearrange("p (q j) -> p q j", j=FJ),
                                         slotf[:, 2:3], pp[2][:, F:2 * F].rearrange("p (q j) -> p q j", j=FJ),
                                         ALU.mult, ALU.mult).then_inc(s_hm, 1)
                dve.wait_ge(s_ht, b + 1)
                dve.tensor_copy(hTs, pp[2][:, 512:512 + F].rearrange("p (j q) -> p j q", j=FJ)).then_inc(s_hte, 1)
                dve.wait_ge(s_yfree, b + 1)
                dve.tensor_scalar(sidx[:, 0:1], slotf[:, 1:2], FAR, None, ALU.add).then_inc(s_si, 1)
                dve.wait_ge(s_si, b + 1)
                dve.tensor_copy(slotf[:], pp[3][:, 0:4]).then_inc(s_sf, 1)
                dve.wait_ge(s_dn, b + 1)
                dve.tensor_copy(ysb[:, 0:512], pp[0][:, 0:512]).then_inc(s_yeD, 1)
            for j in range(FJ):
                dve.wait_ge(s_shs, j + 1)
                dve.wait_ge(s_shp, j + 1)
                dve.tensor_tensor(hs[:, j, :], sgs[:, j, :], pp[1][:, 512 * j:512 * j + 512], ALU.mult)\
                   .then_inc(s_shm, 1)
            for t in range(NT):
                dve.wait_ge(s_yin[t % 2], 16 * (t // 2 + 1))
                dve.tensor_reduce(acc[:, t, :], yin[t % 2].rearrange("p (k n) -> p n k", k=TOPK), AX, ALU.add)\
                   .then_inc(s_comb, 1)
                dve.wait_ge(s_comb, t + 1)
                dve.wait_ge(s_shd, t + 1)
                dve.tensor_tensor(acc[:, t, :], acc[:, t, :], pp[2 + t % 2][:, :], ALU.add).then_inc(s_she, 1)
            for t in range(NT):
                dve.wait_ge(s_frs, t + 1)
                then(dve.reciprocal(frst[:, t:t + 1], frst[:, t:t + 1]))
                then(dve.scalar_tensor_tensor(acc[:, t, :], acc[:, t, :], frst[:, t:t + 1], arow[:, 3],
                                              ALU.mult, ALU.mult))
                dve.tensor_tensor(acc[:, t, :], acc[:, t, :], xres[:, t, :], ALU.add).then_inc(s_fin, 1)


_INS = ["x", "c", "ctx", "c_ctx", "w_ada", "b_ada", "g_pre_mix", "g_post_mix", "g_pre_ffn", "g_post_ffn", "w_in",
        "lambda_q1", "lambda_k1", "lambda_q2", "lambda_k2", "g_subln", "w_pool", "b_pool", "pool_scale", "w_out",
        "w_router", "router_bias", "w_e_gate", "w_e_up", "w_e_down", "w_sh_gate", "w_sh_up", "w_sh_down"]


def kernel(**inputs):
    import concourse.bacc as bacc
    from concourse.bass_utils import run_bass_kernel_spmd as run

    nc = bacc.Bacc("TRN2", target_bir_lowering=False, num_devices=1)
    arrays, aps = {}, {}
    for name in _INS:
        arr = np.ascontiguousarray(inputs[name])
        arrays[f"in_{name}"] = arr
        aps[name] = nc.dram_tensor(f"in_{name}", arr.shape, mybir.dt.from_np(arr.dtype), kind="ExternalInput").ap()
    arrays["in_consts"] = constants()
    aps["consts"] = nc.dram_tensor("in_consts", (P, NCONST), F32, kind="ExternalInput").ap()
    out = nc.dram_tensor("out_y", (1, T, D), F32, kind="ExternalOutput").ap()
    hbuf = nc.dram_tensor("h_rows", (T, D), F32, kind="Internal").ap()
    ybuf = nc.dram_tensor("contributions", (T * TOPK, D), F32, kind="Internal").ap()
    build(nc, aps, hbuf, ybuf, out)
    r = run(nc, [arrays], core_ids=[0])
    return r.results[0]["out_y"]
```

```python
from contextlib import ExitStack

import concourse.bass as bass
import numpy as np
from concourse import mybir

F32 = mybir.dt.float32
F32R = mybir.dt.float32r
I32 = mybir.dt.int32
U32 = mybir.dt.uint32
ALU = mybir.AluOpType
ACT = mybir.ActivationFunctionType
AX = mybir.AxisListType.X

P = 128
D = 1024
KD = D // P
T = 512
NT = T // P
CTX = 256
NC_ = CTX // P
KEYS = CTX + T
NKEY = KEYS // P
HEADS = 4
E = 64
TOPK = 8
F = 256
FJ = F // P
GRID_W = 64
EPS = 1e-6
LAM_INIT = 0.2
SCALE = 64 ** -0.5
ROUTED_SCALE = 2.5
WINDOWS = (2, 4, 8, 16)
FAR = 8192.0
NE = E + 1
NY = TOPK + 1
MAXB = E + T * TOPK // P + NT
CW = KD * F
EW = 3 * CW
IOTA = 640
PAD = 8
TP = T + 2 * PAD
B_E, B_R0, B_SPLIT, TABW = 1, 129, 257, 384

C_ID = 0
C_TRI = C_ID + P
C_ONE = C_TRI + P
C_IOTA = C_ONE + P
C_JLT = C_IOTA + IOTA
C_TOK = C_JLT + 64
C_TOK8 = C_TOK + NT
C_RANK = C_TOK8 + NT
C_PART = C_RANK + NT
C_FAC = C_PART + 1
C_EPS = C_FAC + 64
NCONST = C_EPS + 1


def constants():
    c = np.zeros((P, NCONST), np.float32)
    p = np.arange(P)
    c[:, C_ID:C_ID + P] = np.eye(P)
    f = p % 64
    freqs = (np.float32(10000.0) ** (-np.arange(0, 32, 2, dtype=np.float32) / np.float32(32))).astype(np.float32)
    t = np.arange(T)
    pos = np.where((f // 32 == 0)[:, None], (t // GRID_W)[None], (t % GRID_W)[None]).astype(np.float32)
    angle = (pos * freqs[f % 16][:, None]).astype(np.float32)
    rope = np.zeros((P, 2 * T), np.float32)
    rope[:, :T] = np.cos(angle)
    rope[:, T:] = np.sin(angle) * np.where(f % 32 < 16, -1.0, 1.0)[:, None]
    c[:, C_TRI:C_TRI + P] = p[:, None] < p[None]
    c[:, C_ONE:C_ONE + P] = 1.0
    c[:, C_IOTA:C_IOTA + IOTA] = np.arange(IOTA)
    c[:, C_JLT:C_JLT + 64] = (np.arange(8)[None] < np.arange(8)[:, None]).reshape(1, 64)
    for a in range(NT):
        c[:, C_TOK + a] = a * P + p - FAR
        c[:, C_TOK8 + a] = (a * P + p) * NY - FAR
        c[:, C_RANK + a] = a * P + p
    c[:, C_PART] = p - 1
    fac = np.ones((4, 2, 8), np.float32)
    for g, w in enumerate(WINDOWS):
        for side, ts in enumerate((range(8), range(T - 8, T))):
            for i, tt in enumerate(ts):
                fac[g, side, i] = w / (min(tt + w - w // 2, T) - max(tt - w // 2, 0))
    c[:, C_FAC:C_FAC + 64] = fac.reshape(1, 64)
    c[:, C_EPS] = EPS
    return c, rope


def build(nc, a, hbuf, ybuf, mark, out):
    with ExitStack() as ctx:
        def sb(name, shape, dt=F32):
            return ctx.enter_context(nc.sbuf_tensor(name, shape, dt))

        def sem(name):
            return ctx.enter_context(nc.semaphore(name))

        xres = sb("xres", [P, NT, D])
        cst = sb("cst", [P, NCONST])
        rows = sb("rows", [P, 4096])
        vec = sb("vec", [P, 256])
        lamv = sb("lamv", [P, 4, 64])
        identr = sb("identr", [P, P], F32R)
        tab = sb("tab", [1, TABW], I32)
        ntab = sb("ntab", [1, 1], I32)
        slotf = sb("slotf", [P, 2, 4])
        gidx = sb("gidx", [P, 2], U32)
        sidx = sb("sidx", [P, 2], U32)
        base = nc.sbuf_base
        with ExitStack() as first:
            def sb1(name, shape, dt=F32):
                return first.enter_context(nc.sbuf_tensor(name, shape, dt))

            ring = sb1("ring", [P, 24576])
            actT = sb1("actT", [P, 6144])
            heads = sb1("heads", [P, 10240])
            rope = sb1("rope", [P, 2 * T])
        assert nc.sbuf_base == base
        with ExitStack() as second:
            def sb2(name, shape, dt=F32):
                return second.enter_context(nc.sbuf_tensor(name, shape, dt))

            raww = sb2("raww", [P, 2 * EW])
            whl = sb2("whl", [P, 4 * EW], F32R)
            hmid = sb2("hmid", [P, FJ, P])
            hTh = sb2("hTh", [P, FJ, P], F32R)
            hTl = sb2("hTl", [P, FJ, P], F32R)
            xTh = sb2("xTh", [P, KD, P], F32R)
            xTl = sb2("xTl", [P, KD, P], F32R)
            xg = sb2("xg", [P, 2, D], F32R)
            ysb = sb2("ysb", [P, D])
        with ExitStack() as third:
            def sb3(name, shape, dt=F32):
                return third.enter_context(nc.sbuf_tensor(name, shape, dt))

            yin2 = sb3("yin2", [P, 2, NY * D])
            acc = sb3("acc", [P, NT, D])
            fscr = sb3("fscr", [P, D])
        pp = [ctx.enter_context(nc.psum_tensor(f"pp{i}", [P, 1024], F32)) for i in range(4)]

        ident = cst[:, C_ID:C_ID + P]
        ones = cst[:, C_ONE:C_ONE + P]
        w_in = ring[:, 8192:24576].rearrange("p (k n) -> p k n", k=KD)
        wa0 = ring[:, 0:8192].rearrange("p (k n) -> p k n", k=KD)
        wa1 = heads[:, 0:8192].rearrange("p (k n) -> p k n", k=KD)
        wac = [ring[:, 4096 * i:4096 * i + 4096].rearrange("p (k n) -> p k n", k=KD) for i in range(2)]
        ctx_in = heads[:, 8192:10240].rearrange("p (c d) -> p c d", c=NC_)
        xn = rows[:, :].rearrange("p (b k q) -> p b k q", b=4, k=KD)
        hxT = actT[:, 0:4096].rearrange("p (k t) -> p k t", k=KD)
        hcT = actT[:, 4096:6144].rearrange("p (k t) -> p k t", k=KD)
        qT = heads[:, 0:2048].rearrange("p (h t) -> p h t", h=HEADS)
        kT = heads[:, 2048:5120].rearrange("p (h t) -> p h t", h=HEADS)
        pT = heads[:, 5120:7168].rearrange("p (g t) -> p g t", g=4)
        vv = heads[:, 7168:10240].rearrange("p (c n) -> p c n", c=NKEY)
        raw = rows[:, 0:1024].rearrange("p (b t) -> p b t", b=2)
        swp = rows[:, 1024:1536]
        sumA = rows[:, 1536:1536 + TP]
        sumB = rows[:, 2064:2064 + TP]
        wpool = rows[:, 3072:3584].rearrange("p (g e) -> p g e", g=4)
        w_out = ring[:, 12288:20480].rearrange("p (j n) -> p j n", j=KD)
        e12 = ring[:, 20480:22016].rearrange("p (s n) -> p s n", s=2)
        aT = ring[:, 22016:23552].rearrange("p (b c q) -> p b c q", b=2, c=NKEY)
        junk = ring[:, 23552:24576]
        catT = actT[:, 0:4096].rearrange("p (j t) -> p j t", j=KD)
        oall = actT[:, 4096:6144].rearrange("p (u n) -> p u n", u=16)
        arow = rows[:, :].rearrange("p (r n) -> p r n", r=4)
        grow = heads[:, 5120:7168].rearrange("p (r n) -> p r n", r=2)
        y1 = heads[:, 6144:10240].rearrange("p (c n) -> p c n", c=NT)
        hT = actT[:, 0:4096].rearrange("p (k t) -> p k t", k=KD)
        w_r = actT[:, 4096:4608].rearrange("p (k e) -> p k e", k=KD)
        rt = actT[:, 4608:6144].rearrange("p (s n) -> p s n", s=6)
        rtab = rows[:, 0:3 * NT * NE].rearrange("p (c e w) -> p c e w", c=NT, w=3)
        sg = rows[:, 780:780 + F]
        key = rows[:, 1040:1040 + NT * NE].rearrange("p (c e) -> p c e", c=NT)
        oneh = rows[:, 1300:1812].rearrange("p (c s) -> p c s", c=NT)
        ysbs = [ysb[:, :], rows[:, 1900:2924]]
        selt = rows[:, 1900:2156].rearrange("p (c e) -> p c e", c=NT)
        sct = rows[:, 2156:2412].rearrange("p (c e) -> p c e", c=NT)
        brow = rows[:, 2412:2476]
        m8 = rows[:, 2476:2732]
        tnb = heads[:, 4096:4352]
        yin = [yin2[:, i, :] for i in range(2)]

        sc2 = vec[:, 0:16].rearrange("p (k s) -> p k s", s=2)
        c2 = vec[:, 16:32].rearrange("p (s k) -> p s k", s=2)
        gcol = vec[:, 32:40]
        bcol = vec[:, 40:56].rearrange("p (r k) -> p r k", r=2)
        modc = vec[:, 56:88].rearrange("p (r k s) -> p r k s", r=2, s=2)
        ssq = vec[:, 88:94]
        rstd = vec[:, 94:100]
        gsub = vec[:, 100:101]
        bpool = vec[:, 101:105]
        pscale = vec[:, 105:109]
        dots = vec[:, 109:111]
        lam = vec[:, 111:112]
        mx = vec[:, 112:114]
        nmx = vec[:, 114:116]
        lsum = vec[:, 116:118]
        rl = vec[:, 118:120]
        ossq = vec[:, 120:136]
        orst = vec[:, 136:152]
        yssq = vec[:, 152:156]
        yrst = vec[:, 156:160]
        hssq = vec[:, 160:164]
        hrst = vec[:, 164:168]
        fssq = vec[:, 168:172]
        frst = vec[:, 172:176]
        btab = vec[:, 176:180]
        rsum = vec[:, 180:184]
        srow = vec[:, 184:186]

        s_small = sem("small_loaded")
        s_x = sem("x_loaded")
        s_ctx = sem("ctx_loaded")
        s_wa0 = sem("ada_shift_loaded")
        s_wa1 = sem("ada_scale_loaded")
        s_win = sem("w_in_loaded")
        s_wac = [sem(f"ada_chunk_loaded{i}") for i in range(2)]
        s_brow = sem("b_ada_rows_loaded")
        s_grow = sem("gain_rows_loaded")
        s_gpf = sem("gain_post_ffn_loaded")
        s_wout = sem("w_out_loaded")
        s_wpool = sem("w_pool_loaded")
        s_wr = sem("router_loaded")
        s_rb = sem("router_bias_loaded")
        s_raw = [[sem(f"raw{i}_{n}_loaded") for n in ("gate", "up", "down")] for i in range(2)]
        s_hi = sem("weights_rounded")
        s_lo = sem("gate_up_split")
        s_lod = sem("down_split")
        s_hst = sem("h_stored")
        s_out = sem("out_stored")
        s_silc = sem("silu_c")
        s_ssq = sem("tile_squares")
        s_sq = sem("tile_rms")
        s_xn = sem("tile_normalised")
        s_tp = sem("tile_transposed")
        s_tev = sem("tile_evacuated")
        s_adc = sem("ada_columns")
        s_mod = sem("modulated")
        s_ip = sem("in_projection")
        s_ipe = sem("in_projection_evacuated")
        s_rope = sem("rotated")
        s_pd = sem("pool_differences")
        s_pm = sem("pool_products")
        s_adr = sem("ada_rows")
        s_adre = sem("ada_rows_added")
        s_poolout = sem("pool_out")
        s_gac = sem("gain_rows_used")
        s_sc = sem("scores")
        s_nmx = sem("score_maxima")
        s_exp = sem("exponentials")
        s_a = sem("probabilities")
        s_aTp = sem("probabilities_transposed")
        s_aTe = sem("probabilities_evacuated")
        s_o = sem("attention_products")
        s_oe = sem("attention_evacuated")
        s_ors = sem("head_rms")
        s_on = sem("heads_normalised")
        s_oT = sem("heads_transposed")
        s_cat = sem("concat_ready")
        s_y = sem("out_projection")
        s_ye = sem("out_projection_evacuated")
        s_yrs = sem("y_rms")
        s_x1 = sem("x1_ready")
        s_hrs = sem("h_rms")
        s_h = sem("h_ready")
        s_htp = sem("h_transposed")
        s_hte0 = sem("hT_evacuated")
        s_lg = sem("router_logits")
        s_lge = sem("router_exponentials")
        s_sel = sem("selection")
        s_rk = sem("ranks")
        s_bt = sem("block_columns")
        s_btr = sem("block_rows")
        s_tab = sem("block_table")
        s_oh = sem("onehot")
        s_im = sem("slot_products")
        s_sf = sem("slot_values_kept")
        s_gi = sem("gather_indices")
        s_gt = [sem(f"gathered{i}") for i in range(2)]
        s_xt = sem("block_transposed")
        s_xte = sem("block_evacuated")
        s_gu = sem("gate_up")
        s_sil = sem("block_silu")
        s_hm = sem("hidden")
        s_ht = sem("hidden_transposed")
        s_hte = sem("hidden_evacuated")
        s_si = sem("scatter_indices")
        s_sr = sem("rows_kept")
        s_dn = sem("down")
        s_yev = sem("down_evacuated")
        s_scat = [sem(f"scattered{i}") for i in range(2)]
        s_routed = sem("all_scattered")
        s_pinit = sem("buffers_cleared")
        s_yin = [sem(f"contributions_loaded{i}") for i in range(2)]
        s_comb = sem("contributions_summed")
        s_frs = sem("final_rms")
        s_fin = sem("final_ready")
        s_xtl = sem("block_split")
        s_hth = sem("hidden_rounded")
        s_pgo = sem("pool_passed")
        s_ca = sem("act_order")
        s_cd = sem("dve_order")

        block = ctx.enter_context(nc.Block())

        NSMALL = 13

        def kp(w, n):
            return w.rearrange("(p k) n -> p k n", k=n)

        @block.sync
        def _(sp):
            sp.dma_start(ctx_in, a["ctx"].rearrange("b (c p) d -> p (b c) d", p=P)).then_inc(s_ctx, 16)
            sp.dma_start(xres[:], a["x"].rearrange("b (c p) d -> p (b c) d", p=P)).then_inc(s_x, 16)
            wada = kp(a["w_ada"][0], KD)
            sp.dma_start(wa0, wada[:, :, 0:D]).then_inc(s_wa0, 16)
            sp.dma_start(wa1, wada[:, :, D:2 * D]).then_inc(s_wa1, 16)
            sp.dma_start(w_in, kp(a["w_in"][0], KD)).then_inc(s_win, 16)
            sp.wait_ge(s_tp, NC_ + NT)
            sp.dma_start(wpool, a["w_pool"][0].rearrange("g c e -> c g e")).then_inc(s_wpool, 16)
            for cc in range(8):
                if cc == 0:
                    sp.wait_ge(s_adc, 1)
                if cc == 2:
                    sp.wait_ge(s_ip, 22)
                    sp.dma_start(w_out, a["w_out"][0].rearrange("(j p) n -> p j n", p=P)).then_inc(s_wout, 16)
                    sp.wait_ge(s_pm, 4)
                    sp.dma_start(rows[:, :], a["b_ada"][0:1, 2 * D:6 * D].to_broadcast([P, 4 * D]),
                                 ).then_inc(s_brow, 16)
                    sp.dma_start(grow[:, 0, :], a["g_post_mix"].to_broadcast([P, D])).then_inc(s_grow, 16)
                    sp.dma_start(grow[:, 1, :], a["g_pre_ffn"].to_broadcast([P, D])).then_inc(s_grow, 16)
                if cc >= 2:
                    sp.wait_ge(s_adr, cc - 1)
                c0 = 2 * D + 512 * cc
                sp.dma_start(wac[cc % 2], wada[:, :, c0:c0 + 512]).then_inc(s_wac[cc % 2], 16)

            def matrices(e):
                return [a["w_e_gate"][0, bass.ds(e, 1)].rearrange("a (p k) f -> p (a k f)", k=KD),
                        a["w_e_up"][0, bass.ds(e, 1)].rearrange("a (p k) f -> p (a k f)", k=KD),
                        a["w_e_down"][0, bass.ds(e, 1)].rearrange("a (p j) n -> p (a j n)", j=FJ)]

            def load(q, s, src):
                sp.dma_start(raww[:, q * EW + s * CW:q * EW + (s + 1) * CW], src).then_inc(s_raw[q][s], 16)

            sp.wait_ge(s_adr, 8)
            for q in range(2):
                for s, src in enumerate(matrices(q)):
                    load(q, s, src)
            sp.wait_ge(s_gac, 1)
            sp.dma_start(grow[:, 0, :], a["g_post_ffn"].to_broadcast([P, D])).then_inc(s_gpf, 16)
            sp.wait_ge(s_oT, HEADS)
            sp.dma_start(w_r, kp(a["w_router"][0], KD)).then_inc(s_wr, 16)
            sp.wait_ge(s_h, NT)
            sp.dma_start(brow, a["router_bias"].to_broadcast([P, E])).then_inc(s_rb, 16)
            with sp.Fori(1, E // 2) as g:
                for q in range(2):
                    e = sp.snap(g * 2 + q)
                    srcs = matrices(e)
                    for s in range(2):
                        split = sp.snap(g * 4 + (2 * (q - 2) + s + 1))
                        sp.wait_ge(s_lo, split)
                        load(q, s, srcs[s])
                    split = sp.snap(g * 2 + (q - 1))
                    sp.wait_ge(s_lod, split)
                    load(q, 2, srcs[2])
            for s, src in enumerate((a["w_sh_gate"][0].rearrange("(p k) f -> p (k f)", k=KD),
                                     a["w_sh_up"][0].rearrange("(p k) f -> p (k f)", k=KD),
                                     a["w_sh_down"][0].rearrange("(p j) n -> p (j n)", j=FJ))):
                if s < 2:
                    sp.wait_ge(s_lo, 2 * (E - 2) + s + 1)
                else:
                    sp.wait_ge(s_lod, E - 1)
                load(0, s, src)
            sp.wait_ge(s_routed, 1)
            for t in range(NT):
                if t >= 2:
                    sp.wait_ge(s_comb, t - 1)
                sp.dma_start(yin[t % 2], ybuf[t * P * NY:(t + 1) * P * NY, :]
                             .rearrange("(p k) n -> p (k n)", k=NY)).then_inc(s_yin[t % 2], 16)
            for t in range(NT):
                sp.wait_ge(s_fin, t + 1)
                sp.dma_start(out[0, t * P:(t + 1) * P, :], acc[:, t, :]).then_inc(s_out, 16)
            sp.wait_ge(s_out, 16 * NT)

        @block.gpsimd
        def _(pool):
            pool.wait_ge(s_htp, NT)
            pool.wait_ge(s_hst, 16 * NT)
            pool.wait_ge(s_lge, 1)
            pool.memset(xg[:, :, :].bitcast(F32), 0.0).then_inc(s_pinit, 1)
            pool.wait_ge(s_pinit, 1)
            for q in range(2):
                pool.dma_start(mark[:, 2 * q:2 * q + 2], xg[:, q, 0:2].bitcast(F32)).then_inc(s_scat[q], 16)

            def gather(q):
                pool.indirect_dma_start(xg[:, q, :].bitcast(F32), None, hbuf[:, :],
                                        bass.IndirectOffsetOnAxis(gidx[:, q:q + 1], 0),
                                        bounds_check=T - 1, oob_is_err=False).then_inc(s_gt[q], 16)

            for q in range(2):
                pool.wait_ge(s_scat[q], 16)
                pool.wait_ge(s_gi, q + 1)
                gather(q)
            pool.wait_ge(s_tab, 1)
            nb = pool.value_load(ntab[0:1, 0:1], min_val=NE, max_val=MAXB)
            def split_down(parity, n_hi):
                pool.wait_ge(s_hi, n_hi)
                o = parity * (2 * EW) + 2 * CW
                pool.tensor_tensor(whl[:, bass.ds(o + EW, CW)], raww[:, bass.ds(parity * EW + 2 * CW, CW)],
                                   whl[:, bass.ds(o, CW)].bitcast(F32), ALU.subtract).then_inc(s_lod, 1)

            split_down(0, 3)

            def scatter(q):
                pool.sem_inc(s_pgo, 1)
                pool.indirect_dma_start(ybuf[:, :], bass.IndirectOffsetOnAxis(sidx[:, q:q + 1], 0), ysbs[q],
                                        None, bounds_check=T * NY - 1, oob_is_err=False).then_inc(s_scat[q], 16)

            with pool.Fori(0, nb, 2) as i:
                for q in range(2):
                    n1 = pool.snap(i + (q + 1))
                    n2 = pool.snap(i + (q + 2))
                    n3 = pool.snap(i + (q + 3))
                    pool.wait_ge(s_xt, n1)
                    pool.wait_ge(s_gi, n3)
                    pool.sem_inc(s_pgo, 1)
                    gather(q)
                    pool.wait_ge(s_yev, n2)
                    pool.wait_ge(s_si, n1)
                    scatter(1 - q)
                    nxt = pool.value_load(tab[0:1, bass.ds(i + (q + B_SPLIT), 1)], min_val=0, max_val=E)
                    par = pool.snap(nxt % 2)
                    with pool.If(nxt):
                        split_down(par, nxt * 3 + 3)
            pairs = (nb + 1) // 2
            n_last = pool.snap(pairs * 2 + 2)
            n_si = pool.snap(pairs * 2 + 1)
            pool.wait_ge(s_yev, n_last)
            pool.wait_ge(s_si, n_si)
            scatter(1)
            n_even = pool.snap(pairs * 16 + 16)
            n_odd = pool.snap(pairs * 16 + 32)
            pool.wait_ge(s_scat[0], n_even)
            pool.wait_ge(s_scat[1], n_odd)
            for q in range(2):
                pool.wait_ge(s_gt[q], n_even)
            pool.sem_inc(s_routed, 1)

        @block.scalar
        def _(act):
            order = [0]

            def then(ins):
                order[0] += 1
                ins.then_inc(s_ca, 1)
                act.wait_ge(s_ca, order[0])

            act.dma_start(cst[:], a["consts"]).then_inc(s_small, 16)
            act.dma_start(rope[:], a["rope"]).then_inc(s_small, 16)
            act.dma_start(c2[:, 0, :], a["c"][0].rearrange("(p k) -> p k", k=KD)).then_inc(s_small, 16)
            act.dma_start(c2[:, 1, :], a["c_ctx"].rearrange("(p k) -> p k", k=KD)).then_inc(s_small, 16)
            act.dma_start(gcol, a["g_pre_mix"][0].rearrange("(p k) -> p k", k=KD)).then_inc(s_small, 16)
            act.dma_start(bcol, a["b_ada"][0, 0:2 * D].rearrange("(r p k) -> p r k", r=2, k=KD)).then_inc(s_small, 16)
            with nc.allow_non_contiguous_dma(reason="three short vectors as columns"):
                act.dma_start(gsub, a["g_subln"][0].rearrange("(p k) -> p k", k=1)).then_inc(s_small, 16)
                act.dma_start(bpool, a["b_pool"][0].rearrange("(g p) -> p g", p=P)).then_inc(s_small, 16)
                act.dma_start(pscale, a["pool_scale"][0].rearrange("(g p) -> p g", p=P)).then_inc(s_small, 16)
            for i, name in enumerate(("lambda_q1", "lambda_k1", "lambda_q2", "lambda_k2")):
                act.dma_start(lamv[:, i, :], a[name].to_broadcast([P, 64])).then_inc(s_small, 16)
            act.wait_ge(s_small, 16 * NSMALL)
            act.activation(sc2.rearrange("p k s -> p s k"), c2, ACT.Silu).then_inc(s_silc, 1)
            for t in range(NC_ + NT):
                if t == 0:
                    act.wait_ge(s_ctx, 16)
                if t == NC_:
                    act.wait_ge(s_x, 16)
                src = ctx_in[:, t, :] if t < NC_ else xres[:, t - NC_, :]
                then(act.activation(actT[:, 0:D], src, ACT.Square, accum_out=ssq[:, t:t + 1]))
            act.activation(rstd, ssq, ACT.Sqrt, scale=1.0 / D, bias=cst[:, C_EPS:C_EPS + 1]).then_inc(s_sq, 1)
            for t in range(NC_ + NT):
                act.wait_ge(s_tp, t + 1)
                dst = hcT[:, :, t * P:(t + 1) * P] if t < NC_ else hxT[:, :, (t - NC_) * P:(t - NC_ + 1) * P]
                act.copy(dst, pp[t % 2][:, :].rearrange("p (k t) -> p k t", k=KD)).then_inc(s_tev, 1)
            act.wait_ge(s_mod, 1)
            then(act.activation(dots, dots, ACT.Exp))
            act.sem_inc(s_sq, 1)
            for n in range(22):
                bank = pp[(n % 4) // 2][:, 512 * (n % 2):512 * (n % 2) + 512]
                act.wait_ge(s_ip, n + 1)
                if n < 4:
                    act.copy(kT[:, n, 0:CTX], bank[:, 0:CTX]).then_inc(s_ipe, 1)
                elif n < 12:
                    if n >= 6:
                        act.wait_ge(s_rope, n - 5)
                    act.copy(raw[:, n % 2, :], bank).then_inc(s_ipe, 1)
                elif n < 16:
                    act.copy(pT[:, n - 12, :], bank).then_inc(s_ipe, 1)
                else:
                    act.copy(vv[:, n - 16, :], bank).then_inc(s_ipe, 1)
            for u in range(16):
                act.wait_ge(s_nmx, u + 1)
                if u:
                    act.wait_ge(s_a, u)
                for s in range(2):
                    act.activation(e12[:, s, :], pp[s][:, 0:KEYS], ACT.Exp, bias=nmx[:, s:s + 1], scale=SCALE,
                                   accum_out=lsum[:, s:s + 1]).then_inc(s_exp, 1)
                act.wait_ge(s_aTp, u + 1)
                if u >= 2:
                    act.wait_ge(s_o, u - 1)
                act.copy(aT[:, u % 2], pp[2][:, 0:KEYS].rearrange("p (c q) -> p c q", c=NKEY)).then_inc(s_aTe, 1)
                act.wait_ge(s_o, u + 1)
                then(act.copy(oall[:, u, :], pp[3][:, 0:P]))
                then(act.activation(junk[:, 0:P], oall[:, u, :], ACT.Square, accum_out=ossq[:, u:u + 1]))
                act.sem_inc(s_oe, 1)
            act.activation(orst, ossq, ACT.Sqrt, scale=1.0 / P, bias=cst[:, C_EPS:C_EPS + 1]).then_inc(s_ors, 1)
            for t in range(NT):
                act.wait_ge(s_y, t + 1)
                then(act.copy(y1[:, t, :], pp[t][:, :]))
                then(act.activation(junk, y1[:, t, :], ACT.Square, accum_out=yssq[:, t:t + 1]))
                act.activation(yrst[:, t:t + 1], yssq[:, t:t + 1], ACT.Sqrt, scale=1.0 / D,
                               bias=cst[:, C_EPS:C_EPS + 1]).then_inc(s_yrs, 1)
            for t in range(NT):
                act.wait_ge(s_x1, t + 1)
                then(act.activation(junk, xres[:, t, :], ACT.Square, accum_out=hssq[:, t:t + 1]))
                act.activation(hrst[:, t:t + 1], hssq[:, t:t + 1], ACT.Sqrt, scale=1.0 / D,
                               bias=cst[:, C_EPS:C_EPS + 1]).then_inc(s_hrs, 1)
            for t in range(NT):
                act.wait_ge(s_h, t + 1)
                act.dma_start(hbuf[t * P:(t + 1) * P, :], y1[:, t, :]).then_inc(s_hst, 16)
            for t in range(NT):
                act.wait_ge(s_htp, t + 1)
                act.copy(hT[:, :, t * P:(t + 1) * P], pp[t][:, :].rearrange("p (k t) -> p k t", k=KD))\
                   .then_inc(s_hte0, 1)
            act.wait_ge(s_lg, 1)
            act.activation(rt[:, 0, :], pp[0][:, 0:NT * E], ACT.Exp, scale=-1.0).then_inc(s_lge, 1)

            def round_weights(s, parity, hi_free):
                if hi_free is not None:
                    act.wait_ge(s_gu if s < 2 else s_dn, hi_free)
                act.copy(whl[:, bass.ds(parity * (2 * EW) + s * CW, CW)],
                         raww[:, bass.ds(parity * EW + s * CW, CW)]).then_inc(s_hi, 1)

            act.wait_ge(s_tab, 1)
            for s in range(3):
                act.wait_ge(s_raw[0][s], 16)
                round_weights(s, 0, None)
            act.activation(sg[:, 0:1], cst[:, C_EPS:C_EPS + 1], ACT.Silu).then_inc(s_ca, 1)
            order[0] += 1

            def evacuate_block(n):
                act.wait_ge(s_xt, n)
                act.copy(xTh[:], pp[1][:, :].rearrange("p (k s) -> p k s", k=KD)).then_inc(s_xte, 1)

            def keep_y(q, n, scattered):
                act.wait_ge(s_dn, n)
                act.wait_ge(s_scat[q], scattered)
                act.copy(ysbs[q], pp[0][:, :]).then_inc(s_yev, 1)

            evacuate_block(1)
            act.sem_inc(s_yev, 1)
            nb = act.value_load(ntab[0:1, 0:1], min_val=NE, max_val=MAXB)
            with act.Fori(0, nb, 2) as i:
                for q in range(2):
                    nxt = act.value_load(tab[0:1, bass.ds(i + (q + B_SPLIT), 1)], min_val=0, max_val=E)
                    par = act.snap(nxt % 2)

                    def raw_ready(s):
                        act.wait_ge(s_raw[0][s], ((nxt + 2) // 2) * 16)
                        act.wait_ge(s_raw[1][s], ((nxt + 1) // 2) * 16)

                    with act.If(nxt):
                        for s in range(2):
                            raw_ready(s)
                            round_weights(s, par, i + (q + 1))
                    act.wait_ge(s_gu, i + (q + 2))
                    act.activation(sg, pp[2][:, 0:F], ACT.Silu).then_inc(s_sil, 1)
                    evacuate_block(i + (q + 2))
                    keep_y(1 - q, i + (q + 1), i * 8 + 16)
                    with act.If(nxt):
                        raw_ready(2)
                        round_weights(2, par, i + (q + 1))
            pairs = (nb + 1) // 2
            keep_y(1, pairs * 2 + 1, pairs * 16 + 16)
            for t in range(NT):
                act.wait_ge(s_comb, t + 1)
                then(act.activation(fscr[:], acc[:, t, :], ACT.Square, accum_out=fssq[:, t:t + 1]))
                act.activation(frst[:, t:t + 1], fssq[:, t:t + 1], ACT.Sqrt, scale=1.0 / D,
                               bias=cst[:, C_EPS:C_EPS + 1]).then_inc(s_frs, 1)

        @block.tensor
        def _(pe):
            pe.wait_ge(s_small, 16 * NSMALL)
            for t in range(NC_ + NT):
                pe.wait_ge(s_xn, t + 1)
                if t >= 2:
                    pe.wait_ge(s_tev, t - 1)
                for k in range(KD):
                    last = pe.transpose(pp[t % 2][:, k * P:(k + 1) * P], xn[:, t % 4, k, :], ident)
                last.then_inc(s_tp, 1)
            pe.wait_ge(s_silc, 1)
            for r, (w, s) in enumerate(((wa0, s_wa0), (wa1, s_wa1))):
                pe.wait_ge(s, 16)
                for k in range(KD):
                    o = pp[2][:, (r * KD + k) * 2:(r * KD + k) * 2 + 2]
                    for kk in range(KD):
                        last = pe.matmul(o, w[:, kk, :].rearrange("p (q k) -> p k q", k=KD)[:, k, :],
                                         sc2[:, kk, :], start=(kk == 0), stop=(kk == KD - 1))
                last.then_inc(s_adc, 1)
            pe.wait_ge(s_win, 16)
            pe.wait_ge(s_mod, 1)
            pe.wait_ge(s_tev, NC_ + NT)
            for n in range(22):
                bank = pp[(n % 4) // 2][:, 512 * (n % 2):512 * (n % 2) + 512]
                if n >= 4:
                    pe.wait_ge(s_ipe, n - 3)
                for k in range(KD):
                    if n < 4:
                        o, l, r = bank[:, 0:CTX], w_in[:, k, 512 + n * P:512 + (n + 1) * P], hcT[:, k, :]
                    elif n < 16:
                        c0 = (n - 4) * P if n < 12 else 1536 + (n - 12) * P
                        o, l, r = bank, w_in[:, k, c0:c0 + P], hxT[:, k, :]
                    else:
                        i = n - 16
                        l = hcT[:, k, i * P:(i + 1) * P] if i < NC_ else hxT[:, k, (i - NC_) * P:(i - NC_ + 1) * P]
                        o, r = bank, w_in[:, k, 1024:1536]
                    last = pe.matmul(o, l, r, start=(k == 0), stop=(k == KD - 1))
                last.then_inc(s_ip, 1)
            pe.wait_ge(s_wpool, 16)
            pe.wait_ge(s_ipe, 22)
            for g in range(4):
                pe.wait_ge(s_pd, g + 1)
                pe.matmul(pp[g // 2][:, 512 * (g % 2):512 * (g % 2) + 512], wpool[:, g, :], pT[:, g, :],
                          start=True, stop=True).then_inc(s_pm, 1)
            for cc in range(8):
                pe.wait_ge(s_wac[cc % 2], 16 * (cc // 2 + 1))
                if cc >= 4:
                    pe.wait_ge(s_adre, cc - 3)
                else:
                    pe.wait_ge(s_mod, 1)
                for kk in range(KD):
                    last = pe.matmul(pp[2 + (cc % 4) // 2][:, 512 * (cc % 2):512 * (cc % 2) + 512],
                                     sc2[:, kk, 0:1].to_broadcast([P, P]), wac[cc % 2][:, kk, :],
                                     start=(kk == 0), stop=(kk == KD - 1))
                last.then_inc(s_adr, 1)

            def scores(u):
                h, qb = divmod(u, NT)
                if u:
                    pe.wait_ge(s_exp, 2 * u)
                for s in range(2):
                    for c0, n in ((0, 512), (512, 256)):
                        last = pe.matmul(pp[s][:, c0:c0 + n], qT[64 * s:64 * s + 64, h, qb * P:(qb + 1) * P],
                                         kT[64 * s:64 * s + 64, h, c0:c0 + n], start=True, stop=True)
                last.then_inc(s_sc, 1)

            pe.wait_ge(s_rope, 8)
            pe.wait_ge(s_poolout, 4)
            pe.wait_ge(s_adre, 8)
            scores(0)
            for u in range(16):
                if u + 1 < 16:
                    scores(u + 1)
                h = u // NT
                pe.wait_ge(s_a, u + 1)
                if u:
                    pe.wait_ge(s_aTe, u)
                for c in range(NKEY):
                    last = pe.transpose(pp[2][:, c * P:(c + 1) * P], e12[:, 0, c * P:(c + 1) * P], ident)
                last.then_inc(s_aTp, 1)
                pe.wait_ge(s_aTe, u + 1)
                if u:
                    pe.wait_ge(s_oe, u)
                for c in range(NKEY):
                    last = pe.matmul(pp[3][:, 0:P], aT[:, u % 2, c, :], vv[:, c, h * P:(h + 1) * P],
                                     start=(c == 0), stop=(c == NKEY - 1))
                last.then_inc(s_o, 1)
            pe.wait_ge(s_oe, 16)
            pe.wait_ge(s_on, 1)
            for h in range(HEADS):
                for qb in range(NT):
                    c0 = 512 * (h % 2) + qb * P
                    last = pe.transpose(pp[2 + h // 2][:, c0:c0 + P], oall[:, h * NT + qb, :], ident)
                last.then_inc(s_oT, 1)
            pe.wait_ge(s_wout, 16)
            pe.wait_ge(s_cat, HEADS)
            for t in range(NT):
                for n in range(2):
                    for j in range(KD):
                        last = pe.matmul(pp[t][:, 512 * n:512 * n + 512], catT[:, j, t * P:(t + 1) * P],
                                         w_out[:, j, 512 * n:512 * n + 512], start=(j == 0), stop=(j == KD - 1))
                last.then_inc(s_y, 1)
            for t in range(NT):
                pe.wait_ge(s_h, t + 1)
                for k in range(KD):
                    last = pe.transpose(pp[t][:, k * P:(k + 1) * P], y1[:, t, k * P:(k + 1) * P], ident)
                last.then_inc(s_htp, 1)
            pe.wait_ge(s_wr, 16)
            pe.wait_ge(s_hte0, NT)
            for t in range(NT):
                for k in range(KD):
                    last = pe.matmul(pp[0][:, t * E:(t + 1) * E], hT[:, k, t * P:(t + 1) * P], w_r[:, k, :],
                                     start=(k == 0), stop=(k == KD - 1))
            last.then_inc(s_lg, 1)
            pe.wait_ge(s_sel, 1)
            for t in range(NT):
                for c in range(t + 1):
                    pe.matmul(pp[1][:, t * E:(t + 1) * E], ones if c < t else cst[:, C_TRI:C_TRI + P],
                              selt[:, c, :], start=(c == 0), stop=(c == t))
            for c in range(NT):
                last = pe.matmul(pp[1][:, 512:512 + E], ones, selt[:, c, :], start=(c == 0), stop=(c == NT - 1))
            last.then_inc(s_rk, 1)
            pe.wait_ge(s_bt, 1)
            for i in range(3):
                last = pe.matmul(pp[2][0:1, i * P:(i + 1) * P], btab[:, i:i + 1], ident, start=True, stop=True)
            last.then_inc(s_btr, 1)

            def slots(eb, n):
                pe.wait_ge(s_oh, n)
                for c in range(NT):
                    last = pe.matmul(pp[3][:, 0:3], oneh[:, c, :],
                                     rtab[:, c, :, :].rearrange("p e w -> p (e w)")[:, bass.ds(eb * 3, 3)],
                                     start=(c == 0), stop=(c == NT - 1))
                last.then_inc(s_im, 1)

            def expert_of(b, d):
                return pe.value_load(tab[0:1, bass.ds(b + (B_E + d), 1)], min_val=0, max_val=E)

            def transpose_block(q):
                for k in range(KD):
                    last = pe.transpose(pp[1][:, k * P:(k + 1) * P].bitcast(F32R), xg[:, q, k * P:(k + 1) * P],
                                        identr[:])
                last.then_inc(s_xt, 1)

            pe.wait_ge(s_tab, 1)
            for q in range(2):
                if q:
                    pe.wait_ge(s_sf, q)
                slots(expert_of(0, q), q + 1)
            pe.wait_ge(s_gt[0], 16)
            transpose_block(0)
            pe.sem_inc(s_gu, 1)
            nb = pe.value_load(ntab[0:1, 0:1], min_val=NE, max_val=MAXB)

            def down(e, n):
                w0 = pe.snap((e % 2) * (2 * EW))
                pe.wait_ge(s_lod, e + 1)
                pe.wait_ge(s_hte, n)
                pe.wait_ge(s_yev, n)
                for m in range(2):
                    for j in range(FJ):
                        o = pp[0][:, 512 * m:512 * m + 512]
                        c0 = 2 * CW + j * D + 512 * m
                        hi = whl[:, bass.ds(w0 + c0, 512)]
                        lo = whl[:, bass.ds(w0 + (EW + c0), 512)]
                        pe.matmul(o, hTh[:, j, :], hi, start=(j == 0), stop=False)
                        pe.matmul(o, hTh[:, j, :], lo, start=False, stop=False)
                        last = pe.matmul(o, hTl[:, j, :], hi, start=False, stop=(j == FJ - 1))
                last.then_inc(s_dn, 1)

            with pe.Fori(0, nb, 2) as i:
                for q in range(2):
                    eb = expert_of(i, q)
                    e2 = expert_of(i, q + 2)
                    pe.wait_ge(s_sf, i + (q + 2))
                    slots(e2, i + (q + 3))
                    w0 = pe.snap((eb % 2) * (2 * EW))
                    pe.wait_ge(s_lo, eb * 2 + 2)
                    pe.wait_ge(s_xtl, i + (q + 1))
                    o = pp[2][:, 0:2 * F].rearrange("p (s f) -> p s f", s=2)
                    hi = whl[:, bass.ds(w0, 2 * CW)].rearrange("p (s k f) -> p s k f", s=2, k=KD)
                    lo = whl[:, bass.ds(w0 + EW, 2 * CW)].rearrange("p (s k f) -> p s k f", s=2, k=KD)
                    for k in range(KD):
                        pe.matmul(o, xTh[:, k, :], hi[:, :, k, :], start=(k == 0), stop=False)
                        pe.matmul(o, xTh[:, k, :], lo[:, :, k, :], start=False, stop=False)
                        last = pe.matmul(o, xTl[:, k, :], hi[:, :, k, :], start=False, stop=(k == KD - 1))
                    last.then_inc(s_gu, 1)
                    pe.wait_ge(s_gt[1 - q], i * 8 + (16 + 16 * q))
                    transpose_block(1 - q)
                    down(expert_of(i, q - 1), i + (q + 1))
                    pe.wait_ge(s_hm, i + (q + 1))
                    for j in range(FJ):
                        last = pe.transpose(pp[2][:, 512 + j * P:512 + (j + 1) * P], hmid[:, j, :], ident)
                    last.then_inc(s_ht, 1)
            pairs = (nb + 1) // 2
            down(NE - 1, pairs * 2 + 1)

        @block.vector
        def _(dve):
            order = [0]

            def then(ins):
                order[0] += 1
                ins.then_inc(s_cd, 1)
                dve.wait_ge(s_cd, order[0])

            dve.wait_ge(s_sq, 1)
            then(dve.reciprocal(rstd, rstd))
            for t in range(NC_ + NT):
                src = ctx_in[:, t, :] if t < NC_ else xres[:, t - NC_, :]
                if t >= 4:
                    dve.wait_ge(s_tp, t - 3)
                dve.tensor_scalar(xn[:, t % 4], src.rearrange("p (q k) -> p k q", k=KD), rstd[:, t:t + 1], None,
                                  ALU.mult).then_inc(s_xn, 1)
            for i in range(2):
                then(dve.tensor_tensor_reduce(lamv[:, 2 * i, :], lamv[:, 2 * i, :], lamv[:, 2 * i + 1, :], 1.0, 0.0,
                                              ALU.mult, ALU.add, dots[:, i:i + 1]))
            dve.wait_ge(s_adc, 2)
            for r in range(2):
                then(dve.tensor_tensor(modc[:, r], pp[2][:, r * 16:r * 16 + 16].rearrange("p (k s) -> p k s", s=2),
                                       bcol[:, r, :].rearrange("p (k s) -> p k s", s=1).to_broadcast([P, KD, 2]),
                                       ALU.add))
            then(dve.scalar_tensor_tensor(modc[:, 1], modc[:, 1], 1.0,
                                          gcol.rearrange("p (k s) -> p k s", s=1).to_broadcast([P, KD, 2]),
                                          ALU.add, ALU.mult))
            dve.wait_ge(s_tev, NC_ + NT)
            for k in range(KD):
                for s, x in ((1, hcT), (0, hxT)):
                    last = dve.tensor_scalar(x[:, k, :], x[:, k, :], modc[:, 1, k, s:s + 1], modc[:, 0, k, s:s + 1],
                                             ALU.mult, ALU.add)
            then(last)
            dve.sem_inc(s_mod, 1)
            mask = [(i + 16) % 32 for i in range(32)]
            cos, sin = rope[:, 0:T], rope[:, T:2 * T]
            for n in range(4, 12):
                h = (n - 4) % HEADS
                dst = qT[:, h, :] if n < 8 else kT[:, h, CTX:]
                r = raw[:, n % 2, :]
                dve.wait_ge(s_ipe, n + 1)
                then(dve.stream_shuffle(swp, r, mask))
                then(dve.tensor_tensor(dst, r, cos, ALU.mult))
                then(dve.tensor_tensor(swp, swp, sin, ALU.mult))
                then(dve.tensor_tensor(dst, dst, swp, ALU.add))
                dve.sem_inc(s_rope, 1)
            for g, w in enumerate(WINDOWS):
                p = pT[:, g, :]
                dve.wait_ge(s_ipe, 13 + g)
                cur, nxt = sumA, sumB
                then(dve.memset(cur, 0.0))
                then(dve.tensor_copy(cur[:, PAD:PAD + T], p))
                then(dve.tensor_tensor(nxt[:, 1:], cur[:, :TP - 1], cur[:, 1:], ALU.add))
                m = 1
                while m < w // 2:
                    cur, nxt = nxt, cur
                    lo, hi = 2 * m, TP - 2 * m + 1
                    then(dve.tensor_tensor(nxt[:, lo:hi], cur[:, lo - m:hi - m], cur[:, lo + m:hi + m], ALU.add))
                    m *= 2
                cur = nxt[:, PAD:PAD + T]
                fac = cst[:, C_FAC + 16 * g:C_FAC + 16 * g + 16]
                then(dve.tensor_tensor(cur[:, 0:8], cur[:, 0:8], fac[:, 0:8], ALU.mult))
                then(dve.tensor_tensor(cur[:, T - 8:], cur[:, T - 8:], fac[:, 8:16], ALU.mult))
                then(dve.scalar_tensor_tensor(p, cur, 1.0 / w, p, ALU.mult, ALU.subtract))
                dve.sem_inc(s_pd, 1)
            for g in range(4):
                dve.wait_ge(s_pm, g + 1)
                dve.tensor_scalar(catT[:, 4 + g, :], pp[g // 2][:, 512 * (g % 2):512 * (g % 2) + 512],
                                  bpool[:, g:g + 1], pscale[:, g:g + 1], ALU.add, ALU.mult).then_inc(s_poolout, 1)
            dve.wait_ge(s_brow, 16)
            for cc in range(8):
                dve.wait_ge(s_adr, cc + 1)
                dst = rows[:, 512 * cc:512 * cc + 512]
                dve.tensor_tensor(dst, dst, pp[2 + (cc % 4) // 2][:, 512 * (cc % 2):512 * (cc % 2) + 512],
                                  ALU.add).then_inc(s_adre, 1)
            dve.wait_ge(s_adre, 8)
            dve.wait_ge(s_grow, 32)
            then(dve.tensor_tensor(arow[:, 0], arow[:, 0], grow[:, 0], ALU.mult))
            dve.scalar_tensor_tensor(arow[:, 2], arow[:, 2], 1.0, grow[:, 1], ALU.add, ALU.mult).then_inc(s_gac, 1)
            dve.wait_ge(s_sq, 2)
            then(dve.tensor_tensor(lam, dots[:, 1:2], dots[:, 0:1], ALU.subtract))
            then(dve.tensor_scalar(lam, lam, LAM_INIT, None, ALU.subtract))
            for u in range(16):
                dve.wait_ge(s_sc, u + 1)
                for s in range(2):
                    last = dve.tensor_reduce(mx[:, s:s + 1], pp[s][:, 0:KEYS], AX, ALU.max)
                then(last)
                dve.tensor_scalar(nmx, mx, -SCALE, None, ALU.mult).then_inc(s_nmx, 1)
                dve.wait_ge(s_exp, 2 * u + 2)
                then(dve.reciprocal(rl, lsum))
                then(dve.tensor_tensor(rl[:, 1:2], rl[:, 1:2], lam, ALU.mult))
                then(dve.tensor_scalar(e12[:, 1, :], e12[:, 1, :], rl[:, 1:2], None, ALU.mult))
                dve.scalar_tensor_tensor(e12[:, 0, :], e12[:, 0, :], rl[:, 0:1], e12[:, 1, :],
                                         ALU.mult, ALU.add).then_inc(s_a, 1)
            dve.wait_ge(s_ors, 1)
            then(dve.reciprocal(orst, orst))
            for u in range(16):
                last = dve.tensor_scalar(oall[:, u, :], oall[:, u, :], orst[:, u:u + 1], 1.0 - LAM_INIT,
                                         ALU.mult, ALU.mult)
            last.then_inc(s_on, 1)
            for h in range(HEADS):
                dve.wait_ge(s_oT, h + 1)
                dve.tensor_scalar(catT[:, h, :], pp[2 + h // 2][:, 512 * (h % 2):512 * (h % 2) + 512], gsub, None,
                                  ALU.mult).then_inc(s_cat, 1)
            dve.wait_ge(s_gpf, 16)
            dve.tensor_tensor(arow[:, 3], arow[:, 3], grow[:, 0], ALU.mult).then_inc(s_gac, 1)
            for t in range(NT):
                dve.wait_ge(s_yrs, t + 1)
                then(dve.reciprocal(yrst[:, t:t + 1], yrst[:, t:t + 1]))
                then(dve.scalar_tensor_tensor(y1[:, t, :], y1[:, t, :], yrst[:, t:t + 1], arow[:, 0],
                                              ALU.mult, ALU.mult))
                dve.tensor_tensor(xres[:, t, :], xres[:, t, :], y1[:, t, :], ALU.add).then_inc(s_x1, 1)
            for t in range(NT):
                dve.wait_ge(s_hrs, t + 1)
                then(dve.reciprocal(hrst[:, t:t + 1], hrst[:, t:t + 1]))
                perm = y1[:, t, :].rearrange("p (k q) -> p k q", k=KD)
                then(dve.scalar_tensor_tensor(perm, xres[:, t, :].rearrange("p (q k) -> p k q", k=KD),
                                              hrst[:, t:t + 1], arow[:, 2].rearrange("p (q k) -> p k q", k=KD),
                                              ALU.mult, ALU.mult))
                dve.tensor_tensor(perm, perm, arow[:, 1].rearrange("p (q k) -> p k q", k=KD), ALU.add)\
                   .then_inc(s_h, 1)
            ex, bi, msk, tmp, inc = (rt[:, i, :].rearrange("p (c e) -> p c e", c=NT) for i in range(5))
            dve.wait_ge(s_hst, 16 * NT)
            dve.wait_ge(s_lge, 1)
            dve.wait_ge(s_rb, 16)
            then(dve.tensor_scalar(tmp, ex, 1.0, None, ALU.add))
            then(dve.reciprocal(sct, tmp))
            then(dve.tensor_tensor(bi, sct, brow.rearrange("p (c e) -> p c e", c=1).to_broadcast([P, NT, E]),
                                   ALU.add))
            for t in range(NT):
                for g in range(8):
                    last = dve.max(m8[:, (t * 8 + g) * 8:(t * 8 + g) * 8 + 8], bi[:, t, g * 8:g * 8 + 8])
            then(last)
            top = m8.rearrange("p (n s) -> p n s", s=8)
            gs = tnb[:, 0:32]
            then(dve.tensor_tensor(gs.rearrange("p (n s) -> p n s", s=1), top[:, :, 0:1], top[:, :, 1:2], ALU.add))
            gone = rt[:, 3, :]
            for t in range(NT):
                gj = gs[:, t * 8:t * 8 + 8].rearrange("p (a j) -> p a j", a=1).to_broadcast([P, 8, 8])
                gi = gs[:, t * 8:t * 8 + 8].rearrange("p (i a) -> p i a", a=1).to_broadcast([P, 8, 8])
                x = tmp[:, t, :].rearrange("p (i j) -> p i j", i=8)
                y = inc[:, t, :].rearrange("p (i j) -> p i j", i=8)
                then(dve.tensor_tensor(x, gj, gi, ALU.is_equal))
                then(dve.tensor_tensor(x, x, cst[:, C_JLT:C_JLT + 64].rearrange("p (i j) -> p i j", i=8), ALU.mult))
                then(dve.tensor_tensor(y, gj, gi, ALU.is_gt))
                then(dve.tensor_tensor(x, x, y, ALU.add))
                then(dve.tensor_reduce(tnb[:, 32 + t * 8:40 + t * 8], x, AX, ALU.add))
            then(dve.tensor_scalar(tnb[:, 64:96], tnb[:, 32:64], 4.0, None, ALU.is_lt))
            then(dve.tensor_scalar(tnb[:, 96:128], tnb[:, 64:96], 1.0, 1e30, ALU.subtract, ALU.mult))
            for t in range(NT):
                def spread(c0):
                    return tnb[:, c0 + t * 8:c0 + t * 8 + 8].rearrange("p (g a) -> p g a", a=1).to_broadcast([P, 8, 8])
                b3 = bi[:, t, :].rearrange("p (g j) -> p g j", g=8)
                then(dve.tensor_tensor(b3, b3, spread(64), ALU.mult))
                then(dve.tensor_tensor(b3, b3, spread(96), ALU.add))
                then(dve.max(m8[:, 0:8], bi[:, t, :]))
                then(dve.match_replace(out=msk[:, t, :], in_to_replace=m8[:, 0:8], in_values=bi[:, t, :],
                                       imm_value=3e38))
            then(dve.tensor_scalar(selt, msk, 2e38, None, ALU.is_ge))
            dve.sem_inc(s_sel, 1)
            then(dve.tensor_tensor(sct, sct, selt, ALU.mult))
            then(dve.tensor_reduce(rsum, sct, AX, ALU.add))
            then(dve.reciprocal(rsum, rsum))
            for t in range(NT):
                then(dve.tensor_scalar(rtab[:, t, 0:E, 2], sct[:, t, :], rsum[:, t:t + 1], ROUTED_SCALE,
                                       ALU.mult, ALU.mult))
                then(dve.tensor_tensor_scan(inc[:, t, :], ones[:, 0:E], selt[:, t, :], 0.0, ALU.mult, ALU.add))
                then(dve.tensor_tensor(inc[:, t, :], inc[:, t, :], selt[:, t, :], ALU.subtract))
                then(dve.tensor_scalar(rtab[:, t, 0:E, 1], inc[:, t, :], cst[:, C_TOK8 + t:C_TOK8 + t + 1], None,
                                       ALU.add))
                then(dve.tensor_scalar(rtab[:, t, :, 0], ones[:, 0:NE], cst[:, C_TOK + t:C_TOK + t + 1], None,
                                       ALU.mult))
            then(dve.memset(rtab[:, :, E, 2], 1.0))
            then(dve.tensor_scalar(rtab[:, :, E, 1], cst[:, C_TOK8:C_TOK8 + NT], float(TOPK), None, ALU.add))
            then(dve.tensor_copy(key[:, :, E], cst[:, C_RANK:C_RANK + NT]))
            dve.wait_ge(s_rk, 1)
            then(dve.tensor_scalar(tmp, pp[1][:, 0:NT * E].rearrange("p (c e) -> p c e", c=NT), 1.0, None, ALU.add))
            then(dve.tensor_tensor(tmp, tmp, selt, ALU.mult))
            then(dve.tensor_scalar(key[:, :, 0:E], tmp, 1.0, None, ALU.subtract))
            nblk, cum, t65 = (heads[:, 4400 + 80 * i:4400 + 80 * i + NE] for i in range(3))
            then(dve.memset(t65, float(T)))
            then(dve.tensor_copy(t65[:, 0:E], pp[1][:, 512:512 + E]))
            then(dve.tensor_scalar(nblk, t65, P + 0.5, 1.0, ALU.is_ge, ALU.add))
            for th in (2 * P + 0.5, 3 * P + 0.5):
                then(dve.scalar_tensor_tensor(nblk, t65, th, nblk, ALU.is_ge, ALU.add))
            then(dve.tensor_tensor_scan(cum, ones[:, 0:NE], nblk, 0.0, ALU.mult, ALU.add))
            part = cst[:, C_PART:C_PART + 1]
            then(dve.tensor_scalar(t65, cum, part, None, ALU.is_le))
            then(dve.tensor_reduce(btab[:, 0:1], t65, AX, ALU.add))
            then(dve.tensor_tensor(t65, t65, nblk, ALU.mult))
            then(dve.tensor_reduce(btab[:, 1:2], t65, AX, ALU.add))
            then(dve.tensor_scalar(btab[:, 2:3], btab[:, 0:1], NE - 0.5, 1000.0, ALU.is_ge, ALU.mult))
            then(dve.tensor_scalar(btab[:, 0:1], btab[:, 0:1], float(NE - 1), None, ALU.min))
            then(dve.tensor_tensor(btab[:, 1:2], part, btab[:, 1:2], ALU.subtract))
            then(dve.scalar_tensor_tensor(btab[:, 1:2], btab[:, 1:2], float(P), btab[:, 2:3], ALU.mult, ALU.add))
            then(dve.tensor_scalar(btab[:, 1:2], btab[:, 1:2], float(T), None, ALU.min))
            then(dve.tensor_scalar(btab[:, 2:3], btab[:, 1:2], 0.0, None, ALU.is_equal))
            then(dve.tensor_scalar(btab[:, 3:4], btab[:, 0:1], 1.0, None, ALU.add))
            then(dve.tensor_tensor(btab[:, 2:3], btab[:, 2:3], btab[:, 3:4], ALU.mult))
            then(dve.tensor_scalar(btab[:, 3:4], btab[:, 0:1], NE - 1.5, None, ALU.is_lt))
            then(dve.tensor_tensor(btab[:, 2:3], btab[:, 2:3], btab[:, 3:4], ALU.mult))
            dve.sem_inc(s_bt, 1)
            then(dve.tensor_copy(identr[:], ident))
            dve.wait_ge(s_btr, 1)
            then(dve.tensor_copy(tab[0:1, :], pp[2][0:1, 0:TABW]))
            then(dve.tensor_copy(ntab[0:1, 0:1], cum[0:1, NE - 1:NE]))
            dve.sem_inc(s_tab, 1)

            def onehots(eb, r0):
                for c in range(NT):
                    last = dve.tensor_scalar(oneh[:, c, :], cst[:, bass.ds(r0 + C_IOTA, P)],
                                             key[:, c, bass.ds(eb, 1)], None, ALU.is_equal)
                last.then_inc(s_oh, 1)

            def block_of(b, d):
                return (dve.value_load(tab[0:1, bass.ds(b + (B_E + d), 1)], min_val=0, max_val=NE - 1),
                        dve.value_load(tab[0:1, bass.ds(b + (B_R0 + d), 1)], min_val=0, max_val=T))

            def gather_index(q):
                dve.tensor_scalar(gidx[:, q:q + 1], pp[3][:, 0:1], FAR, None, ALU.add).then_inc(s_gi, 1)

            def keep_slots(q):
                dve.tensor_copy(slotf[:, q, 0:3], pp[3][:, 0:3]).then_inc(s_sf, 1)

            def scatter_index(q, scattered):
                dve.wait_ge(s_scat[q], scattered)
                dve.tensor_copy(sidx[:, q:q + 1], srow[:, q:q + 1]).then_inc(s_si, 1)

            def split_weights(s, parity, n_hi):
                dve.wait_ge(s_hi, n_hi)
                o = parity * (2 * EW)
                dve.tensor_tensor(whl[:, bass.ds(o + (EW + s * CW), CW)], raww[:, bass.ds(parity * EW + s * CW, CW)],
                                  whl[:, bass.ds(o + s * CW, CW)].bitcast(F32), ALU.subtract).then_inc(s_lo, 1)

            def split_block(n):
                dve.wait_ge(s_xte, n)
                dve.tensor_tensor(xTl[:], pp[1][:, :].rearrange("p (k s) -> p k s", k=KD), xTh[:].bitcast(F32),
                                  ALU.subtract).then_inc(s_xtl, 1)

            for o, sm in ((hTh, s_hth), (hTl, s_hte)):
                dve.tensor_scalar(o[:], cst[:, C_IOTA:C_IOTA + F].rearrange("p (j q) -> p j q", j=FJ), 0.0, None,
                                  ALU.mult).then_inc(sm, 1)
            then(dve.memset(srow, 2 * FAR))
            for n in range(2):
                onehots(*block_of(0, n))
                dve.wait_ge(s_im, n + 1)
                gather_index(n)
                keep_slots(n)
            onehots(*block_of(0, 2))
            for s in range(2):
                split_weights(s, 0, s + 1)
            split_block(1)
            nb = dve.value_load(ntab[0:1, 0:1], min_val=NE, max_val=MAXB)
            with dve.Fori(0, nb, 2) as i:
                for q in range(2):
                    e3, r3 = block_of(i, q + 3)
                    nxt = dve.value_load(tab[0:1, bass.ds(i + (q + B_SPLIT), 1)], min_val=0, max_val=E)
                    par = dve.snap(nxt % 2)
                    dve.wait_ge(s_gt[q], i * 8 + 16)
                    dve.wait_ge(s_im, i + (q + 3))
                    gather_index(q)
                    onehots(e3, r3)
                    scatter_index(1 - q, i * 8 + 16)
                    with dve.If(nxt):
                        for s in range(2):
                            split_weights(s, par, nxt * 3 + (s + 1))
                    dve.wait_ge(s_sf, i + (q + 1))
                    dve.wait_ge(s_sil, i + (q + 1))
                    dve.scalar_tensor_tensor(hmid[:].rearrange("p j q -> p q j"),
                                             sg.rearrange("p (q j) -> p q j", j=FJ), slotf[:, q, 2:3],
                                             pp[2][:, F:2 * F].rearrange("p (q j) -> p q j", j=FJ),
                                             ALU.mult, ALU.mult).then_inc(s_hm, 1)
                    split_block(i + (q + 2))
                    dve.tensor_scalar(srow[:, q:q + 1], slotf[:, q, 1:2], FAR, None, ALU.add).then_inc(s_sr, 1)
                    dve.wait_ge(s_hm, i + (q + 1))
                    dve.wait_ge(s_sr, i + (q + 1))
                    keep_slots(q)
                    dve.wait_ge(s_ht, i + (q + 1))
                    hps = pp[2][:, 512:512 + F].rearrange("p (j q) -> p j q", j=FJ)
                    dve.tensor_copy(hTh[:], hps).then_inc(s_hth, 1)
                    dve.wait_ge(s_hth, i + (q + 2))
                    dve.tensor_tensor(hTl[:], hps, hTh[:].bitcast(F32), ALU.subtract).then_inc(s_hte, 1)
            pairs = (nb + 1) // 2
            dve.wait_ge(s_sr, pairs * 2)
            scatter_index(1, pairs * 16 + 16)
            for t in range(NT):
                dve.wait_ge(s_yin[t % 2], 16 * (t // 2 + 1))
                dve.tensor_reduce(acc[:, t, :], yin[t % 2].rearrange("p (k n) -> p n k", k=NY), AX, ALU.add)\
                   .then_inc(s_comb, 1)
            for t in range(NT):
                dve.wait_ge(s_frs, t + 1)
                then(dve.reciprocal(frst[:, t:t + 1], frst[:, t:t + 1]))
                then(dve.scalar_tensor_tensor(acc[:, t, :], acc[:, t, :], frst[:, t:t + 1], arow[:, 3],
                                              ALU.mult, ALU.mult))
                dve.tensor_tensor(acc[:, t, :], acc[:, t, :], xres[:, t, :], ALU.add).then_inc(s_fin, 1)


_INS = ["x", "c", "ctx", "c_ctx", "w_ada", "b_ada", "g_pre_mix", "g_post_mix", "g_pre_ffn", "g_post_ffn", "w_in",
        "lambda_q1", "lambda_k1", "lambda_q2", "lambda_k2", "g_subln", "w_pool", "b_pool", "pool_scale", "w_out",
        "w_router", "router_bias", "w_e_gate", "w_e_up", "w_e_down", "w_sh_gate", "w_sh_up", "w_sh_down"]


def kernel(**inputs):
    import concourse.bacc as bacc
    from concourse.bass_utils import run_bass_kernel_spmd as run

    nc = bacc.Bacc("TRN2", target_bir_lowering=False, num_devices=1)
    arrays, aps = {}, {}
    for name in _INS:
        arr = np.ascontiguousarray(inputs[name])
        arrays[f"in_{name}"] = arr
        aps[name] = nc.dram_tensor(f"in_{name}", arr.shape, mybir.dt.from_np(arr.dtype), kind="ExternalInput").ap()
    arrays["in_consts"], arrays["in_rope"] = constants()
    aps["rope"] = nc.dram_tensor("in_rope", (P, 2 * T), F32, kind="ExternalInput").ap()
    aps["consts"] = nc.dram_tensor("in_consts", (P, NCONST), F32, kind="ExternalInput").ap()
    out = nc.dram_tensor("out_y", (1, T, D), F32, kind="ExternalOutput").ap()
    hbuf = nc.dram_tensor("h_rows", (T, D), F32, kind="Internal").ap()
    ybuf = nc.dram_tensor("contributions", (T * NY, D), F32, kind="Internal").ap()
    mark = nc.dram_tensor("mark", (P, 4), F32, kind="Internal").ap()
    build(nc, aps, hbuf, ybuf, mark, out)
    r = run(nc, [arrays], core_ids=[0])
    return r.results[0]["out_y"]
```

```python
from contextlib import ExitStack

import concourse.bass as bass
import numpy as np
from concourse import mybir

F32 = mybir.dt.float32
F32R = mybir.dt.float32r
I32 = mybir.dt.int32
U32 = mybir.dt.uint32
ALU = mybir.AluOpType
ACT = mybir.ActivationFunctionType
AX = mybir.AxisListType.X

P = 128
D = 1024
KD = D // P
T = 512
NT = T // P
CTX = 256
NC_ = CTX // P
KEYS = CTX + T
NKEY = KEYS // P
HEADS = 4
E = 64
TOPK = 8
F = 256
FJ = F // P
GRID_W = 64
EPS = 1e-6
LAM_INIT = 0.2
SCALE = 64 ** -0.5
ROUTED_SCALE = 2.5
WINDOWS = (2, 4, 8, 16)
FAR = 8192.0
NE = E + 1
MAXB = NT + E + T * TOPK // P
CW = KD * F
EW = 3 * CW
IOTA = 640
PAD = 8
TP = T + 2 * PAD
B_E, B_R0, B_SPLIT, B_FULL, TABW = 0, 128, 256, 384, 512

C_ID = 0
C_TRI = C_ID + P
C_ONE = C_TRI + P
C_IOTA = C_ONE + P
C_JLT = C_IOTA + IOTA
C_TOK = C_JLT + 64
C_RANK = C_TOK + NT
C_PART = C_RANK + NT
C_FAC = C_PART + 1
C_EPS = C_FAC + 64
NCONST = C_EPS + 1


def constants():
    c = np.zeros((P, NCONST), np.float32)
    p = np.arange(P)
    c[:, C_ID:C_ID + P] = np.eye(P)
    f = p % 64
    freqs = (np.float32(10000.0) ** (-np.arange(0, 32, 2, dtype=np.float32) / np.float32(32))).astype(np.float32)
    t = np.arange(T)
    pos = np.where((f // 32 == 0)[:, None], (t // GRID_W)[None], (t % GRID_W)[None]).astype(np.float32)
    angle = (pos * freqs[f % 16][:, None]).astype(np.float32)
    rope = np.zeros((P, 2 * T), np.float32)
    rope[:, :T] = np.cos(angle)
    rope[:, T:] = np.sin(angle) * np.where(f % 32 < 16, -1.0, 1.0)[:, None]
    c[:, C_TRI:C_TRI + P] = p[:, None] < p[None]
    c[:, C_ONE:C_ONE + P] = 1.0
    c[:, C_IOTA:C_IOTA + IOTA] = np.arange(IOTA)
    c[:, C_JLT:C_JLT + 64] = (np.arange(8)[None] < np.arange(8)[:, None]).reshape(1, 64)
    for a in range(NT):
        c[:, C_TOK + a] = a * P + p - FAR
        c[:, C_RANK + a] = a * P + p
    c[:, C_PART] = p - NT
    fac = np.ones((4, 2, 8), np.float32)
    for g, w in enumerate(WINDOWS):
        for side, ts in enumerate((range(8), range(T - 8, T))):
            for i, tt in enumerate(ts):
                fac[g, side, i] = w / (min(tt + w - w // 2, T) - max(tt - w // 2, 0))
    c[:, C_FAC:C_FAC + 64] = fac.reshape(1, 64)
    c[:, C_EPS] = EPS
    return c, rope


def build(nc, a, hbuf, sums, out):
    with ExitStack() as ctx:
        def sb(name, shape, dt=F32):
            return ctx.enter_context(nc.sbuf_tensor(name, shape, dt))

        def sem(name):
            return ctx.enter_context(nc.semaphore(name))

        xres = sb("xres", [P, NT, D])
        cst = sb("cst", [P, NCONST])
        rows = sb("rows", [P, 4096])
        vec = sb("vec", [P, 192])
        lamtab = sb("lamtab", [P, TABW])
        identr = sb("identr", [P, P], F32R)
        ntab = sb("ntab", [1, 1], I32)
        slotf = sb("slotf", [P, 2, 2])
        gidx = sb("gidx", [P, 2], U32)
        sidx = sb("sidx", [P, 2], U32)
        base = nc.sbuf_base
        with ExitStack() as first:
            def sb1(name, shape, dt=F32):
                return first.enter_context(nc.sbuf_tensor(name, shape, dt))

            ring = sb1("ring", [P, 24576])
            actT = sb1("actT", [P, 6144])
            heads = sb1("heads", [P, 10240])
            rope = sb1("rope", [P, 2 * T])
        assert nc.sbuf_base == base
        with ExitStack() as second:
            def sb2(name, shape, dt=F32):
                return second.enter_context(nc.sbuf_tensor(name, shape, dt))

            raww = sb2("raww", [P, 2 * EW])
            whl = sb2("whl", [P, 4 * EW], F32R)
            hmid = sb2("hmid", [P, FJ, P])
            hTh = sb2("hTh", [P, FJ, P], F32R)
            hTl = sb2("hTl", [P, FJ, P], F32R)
            xTh = sb2("xTh", [P, KD, P], F32R)
            xTl = sb2("xTl", [P, KD, P], F32R)
            xg = sb2("xg", [P, 2, D], F32R)
            ysb = sb2("ysb", [P, D])
        with ExitStack() as third:
            def sb3(name, shape, dt=F32):
                return third.enter_context(nc.sbuf_tensor(name, shape, dt))

            acc = sb3("acc", [P, 2, NT, D])
            fscr = sb3("fscr", [P, D])
        pp = [ctx.enter_context(nc.psum_tensor(f"pp{i}", [P, 1024], F32)) for i in range(4)]

        lamv = lamtab[:, 0:256].rearrange("p (i n) -> p i n", i=4)
        tab = lamtab[0:1, :].bitcast(I32)
        ident = cst[:, C_ID:C_ID + P]
        ones = cst[:, C_ONE:C_ONE + P]
        w_in = ring[:, 8192:24576].rearrange("p (k n) -> p k n", k=KD)
        wa = [r.rearrange("p (k n) -> p k n", k=2)
              for r in (ring[:, 0:4096], ring[:, 4096:8192], heads[:, 0:4096], heads[:, 4096:8192])]
        ada2 = ring[0:2, 4096:6144]
        wrow = [ring[:, 2048 * i:2048 * i + 2048] for i in range(2)]
        part = ring[:, 4096:8192]
        grow = ring[:, 0:3072].rearrange("p (r n) -> p r n", r=3)
        ctx_in = heads[:, 8192:10240].rearrange("p (c d) -> p c d", c=NC_)
        xn = rows[:, :].rearrange("p (b k q) -> p b k q", b=4, k=KD)
        hxT = actT[:, 0:4096].rearrange("p (k t) -> p k t", k=KD)
        hcT = actT[:, 4096:6144].rearrange("p (k t) -> p k t", k=KD)
        qT = heads[:, 0:2048].rearrange("p (h t) -> p h t", h=HEADS)
        kT = heads[:, 2048:5120].rearrange("p (h t) -> p h t", h=HEADS)
        pT = heads[:, 5120:7168].rearrange("p (g t) -> p g t", g=4)
        vv = heads[:, 7168:10240].rearrange("p (c n) -> p c n", c=NKEY)
        raw = rows[:, 0:1024].rearrange("p (b t) -> p b t", b=2)
        swp = rows[:, 1024:1536]
        sumA = rows[:, 1536:1536 + TP]
        sumB = rows[:, 2064:2064 + TP]
        wpool = rows[:, 3072:3584].rearrange("p (g e) -> p g e", g=4)
        e12 = ring[:, 6144:9216].rearrange("p (b s n) -> p b s n", b=2, s=2)
        aT = ring[:, 9216:10752].rearrange("p (b c q) -> p b c q", b=2, c=NKEY)
        junk = ring[:, 10752:11776]
        zeros = ring[:, 11776:12288]
        w_out = ring[:, 12288:20480].rearrange("p (j n) -> p j n", j=KD)
        y1 = ring[:, 20480:22528].rearrange("p (b n) -> p b n", b=2)
        hT = ring[:, 22528:23552].rearrange("p (k t) -> p k t", k=KD)
        oall = ring[:, 23552:24576].rearrange("p (b h n) -> p b h n", b=2, h=HEADS)
        poolT = actT[:, 0:2048].rearrange("p (g t) -> p g t", g=4)
        headT = actT[:, 2048:3072].rearrange("p (b h q) -> p b h q", b=2, h=HEADS)
        arow = rows[:, :].rearrange("p (r n) -> p r n", r=4)
        w_r = actT[:, 3072:3584].rearrange("p (k e) -> p k e", k=KD)
        sct = actT[:, 3584:3840].rearrange("p (c e) -> p c e", c=NT)
        selt = actT[:, 3840:4096].rearrange("p (c e) -> p c e", c=NT)
        m8 = actT[:, 4096:4352]
        brow = actT[:, 4352:4416]
        tnb = actT[:, 4416:4672]
        rt = actT[:, 4672:5952].rearrange("p (s n) -> p s n", s=5)
        rtab = rows[:, 0:2 * NT * NE].rearrange("p (c e w) -> p c e w", c=NT, w=2)
        sg = rows[:, 780:780 + F]
        key = rows[:, 1040:1040 + NT * NE].rearrange("p (c e) -> p c e", c=NT)
        oneh = rows[:, 1300:1812].rearrange("p (c s) -> p c s", c=NT)
        ysbs = [ysb[:, :], rows[:, 1900:2924]]

        sc2 = vec[:, 0:16].rearrange("p (k s) -> p k s", s=2)
        c2 = vec[:, 16:32].rearrange("p (s k) -> p s k", s=2)
        gcol = vec[:, 32:40]
        bcol = vec[:, 40:56].rearrange("p (r k) -> p r k", r=2)
        modc = vec[:, 56:88].rearrange("p (r k s) -> p r k s", r=2, s=2)
        ssq = vec[:, 88:94]
        rstd = vec[:, 94:100]
        gsub = vec[:, 100:101]
        bpool = vec[:, 101:105]
        pscale = vec[:, 105:109]
        dots = vec[:, 109:111]
        lam = vec[:, 111:112]
        mx = vec[:, 112:114]
        nmx = vec[:, 114:116]
        lsum = vec[:, 116:118]
        rl = vec[:, 118:120]
        ossq = vec[:, 120:136]
        orst = vec[:, 136:152]
        yssq = vec[:, 152:156]
        yrst = vec[:, 156:160]
        hssq = vec[:, 160:164]
        hrst = vec[:, 164:168]
        fssq = vec[:, 168:172]
        frst = vec[:, 172:176]
        btab = vec[:, 176:180]
        bfull = vec[:, 186:187]
        rsum = vec[:, 180:184]
        srow = vec[:, 184:186]

        s_c = sem("c_loaded")
        s_cst = sem("constants_loaded")
        s_small = sem("small_loaded")
        s_x = sem("x_loaded")
        s_ctx = sem("ctx_loaded")
        s_wa = [sem(f"ada_pair_loaded{i}") for i in range(4)]
        s_win = [sem(f"w_in_{n}_loaded") for n in ("k", "q", "pool", "v")]
        s_wrow = [sem(f"ada_half_row_loaded{i}") for i in range(2)]
        s_pz = sem("ada_sums_cleared")
        s_pmul = sem("ada_half_row_times_silu")
        s_brow = sem("b_ada_loaded")
        s_part = [sem(f"ada_half_row_added{i}") for i in range(2)]
        s_ad2 = sem("ada_shift_scale")
        s_ad2e = sem("ada_shift_scale_kept")
        s_grow = sem("gain_rows_loaded")
        s_wout = sem("w_out_loaded")
        s_wpool = sem("w_pool_loaded")
        s_wr = sem("router_loaded")
        s_rb = sem("router_bias_loaded")
        s_raw = [[sem(f"raw{i}_{n}_loaded") for n in ("gate", "up", "down")] for i in range(2)]
        s_hi = sem("weights_rounded")
        s_lo = sem("gate_up_split")
        s_lod = sem("down_split")
        s_lo0 = sem("first_gate_up_split")
        s_hst = [sem(f"h_stored{i}") for i in range(2)]
        s_out = sem("out_stored")
        s_silc = sem("silu_c")
        s_sq = sem("tile_rms")
        s_xn = sem("tile_normalised")
        s_tp = sem("tile_transposed")
        s_tev = sem("tile_evacuated")
        s_adc = sem("ada_columns")
        s_mod = sem("modulated")
        s_ip = sem("in_projection")
        s_ipe = sem("in_projection_evacuated")
        s_rope = sem("rotated")
        s_pd = sem("pool_differences")
        s_pm = sem("pool_products")
        s_adr = sem("ada_rows")
        s_adre = sem("ada_rows_added")
        s_poolout = sem("pool_out")
        s_sc = sem("scores")
        s_nmx = sem("score_maxima")
        s_exp = sem("exponentials")
        s_osq = sem("head_squares")
        s_a = sem("probabilities")
        s_aTp = sem("probabilities_transposed")
        s_aTe = sem("probabilities_evacuated")
        s_o = sem("attention_products")
        s_oe = sem("attention_evacuated")
        s_ors = sem("head_rms")
        s_on = sem("heads_normalised")
        s_oT = sem("heads_transposed")
        s_cat = sem("concat_ready")
        s_y = sem("out_projection")
        s_ye = sem("out_projection_evacuated")
        s_yrs = sem("y_rms")
        s_x1 = sem("x1_ready")
        s_hrs = sem("h_rms")
        s_h = sem("h_ready")
        s_htp = sem("h_transposed")
        s_hte0 = sem("hT_evacuated")
        s_lg = sem("router_logits")
        s_lge = sem("router_exponentials")
        s_sel = sem("selection")
        s_rk = sem("ranks")
        s_bt = sem("block_columns")
        s_btr = sem("block_rows")
        s_tab = sem("block_table")
        s_oh = sem("onehot")
        s_im = sem("slot_products")
        s_sf = sem("slot_values_kept")
        s_gi = sem("gather_indices")
        s_gt = [sem(f"gathered{i}") for i in range(2)]
        s_xt = sem("block_transposed")
        s_xte = sem("block_evacuated")
        s_gu = sem("gate_up")
        s_sil = sem("block_silu")
        s_hm = sem("hidden")
        s_ht = sem("hidden_transposed")
        s_hte = sem("hidden_evacuated")
        s_si = sem("scatter_indices")
        s_sr = sem("rows_kept")
        s_dn = sem("down")
        s_yev = sem("down_evacuated")
        s_scat = [sem(f"scattered{i}") for i in range(2)]
        s_routed = sem("all_scattered")
        s_zero = sem("zeros_ready")
        s_sum0 = sem("sums_cleared")
        s_yin = [sem(f"sums_loaded{i}") for i in range(NT)]
        s_comb = sem("sums_added")
        s_frs = sem("final_rms")
        s_fin = sem("final_ready")
        s_xtl = sem("block_split")
        s_hth = sem("hidden_rounded")
        s_pgo = sem("pool_passed")
        s_ca = sem("act_order")
        s_cd = sem("dve_order")

        block = ctx.enter_context(nc.Block())

        NSMALL = 10
        STEPS = 16 + 10

        def tile_at(st, d):
            t, r = divmod(st - d, HEADS)
            return t if r == 0 and 0 <= t < NT else None

        def kp(w, n):
            return w.rearrange("(p k) n -> p k n", k=n)

        @block.sync
        def _(sp):
            wada = kp(a["w_ada"][0], KD)
            sp.dma_start(ctx_in, a["ctx"].rearrange("b (c p) d -> p (b c) d", p=P)).then_inc(s_ctx, 16)
            sp.dma_start(xres[:], a["x"].rearrange("b (c p) d -> p (b c) d", p=P)).then_inc(s_x, 16)
            for i in range(4):
                if i == 1:
                    sp.wait_ge(s_x, 16)
                sp.dma_start(wa[i], wada[:, 2 * i:2 * i + 2, 0:2 * D]).then_inc(s_wa[i], 16)
            win = kp(a["w_in"][0], KD)
            for i, c0 in enumerate((512, 0, 1536, 1024)):
                sp.dma_start(w_in[:, :, c0:c0 + 512], win[:, :, c0:c0 + 512]).then_inc(s_win[i], 16)
            sp.wait_ge(s_tp, NC_ + NT)
            sp.dma_start(wpool, a["w_pool"][0].rearrange("g c e -> c g e")).then_inc(s_wpool, 16)
            sp.wait_ge(s_pz, 1)
            sp.dma_start(part[0:1, :], a["b_ada"][0:1, 2 * D:6 * D]).then_inc(s_brow, 16)
            for k in range(KD):
                for i in range(2):
                    if k == 0:
                        sp.wait_ge(s_ad2, 1)
                    else:
                        sp.wait_ge(s_part[i], k)
                    sp.dma_start(wrow[i], wada[:, k, 2 * D + 2048 * i:2 * D + 2048 * i + 2048])\
                      .then_inc(s_wrow[i], 16)
            for i in range(2):
                sp.wait_ge(s_part[i], KD)
            for i, name in enumerate(("g_post_mix", "g_pre_ffn", "g_post_ffn")):
                sp.dma_start(grow[:, i, :], a[name].to_broadcast([P, D])).then_inc(s_grow, 16)
            sp.wait_ge(s_ip, 22)
            sp.dma_start(w_out, a["w_out"][0].rearrange("(j p) n -> p j n", p=P)).then_inc(s_wout, 16)
            sp.dma_start(w_r, kp(a["w_router"][0], KD)).then_inc(s_wr, 16)
            sp.dma_start(brow, a["router_bias"].to_broadcast([P, E])).then_inc(s_rb, 16)

            def matrices(e):
                return [a["w_e_gate"][0, bass.ds(e, 1)].rearrange("a (p k) f -> p (a k f)", k=KD),
                        a["w_e_up"][0, bass.ds(e, 1)].rearrange("a (p k) f -> p (a k f)", k=KD),
                        a["w_e_down"][0, bass.ds(e, 1)].rearrange("a (p j) n -> p (a j n)", j=FJ)]

            def load(q, s, src):
                sp.dma_start(raww[:, q * EW + s * CW:q * EW + (s + 1) * CW], src).then_inc(s_raw[q][s], 16)

            sp.wait_ge(s_zero, 1)
            for i in range(2):
                sp.dma_start(sums[i].rearrange("(p r) (h n) -> p (r h) n", p=P, h=2),
                             zeros.rearrange("p (a n) -> p a n", a=1).to_broadcast([P, 2 * NT, 512]))\
                  .then_inc(s_sum0, 16)
            sp.wait_ge(s_adr, 8)
            sp.wait_ge(s_adre, 8)
            for s, src in enumerate((a["w_sh_gate"][0].rearrange("(p k) f -> p (k f)", k=KD),
                                     a["w_sh_up"][0].rearrange("(p k) f -> p (k f)", k=KD),
                                     a["w_sh_down"][0].rearrange("(p j) n -> p (j n)", j=FJ))):
                load(0, s, src)
            for i in range(2):
                sp.wait_ge(s_gt[i], 16)
            for s, src in enumerate(matrices(0)):
                load(1, s, src)
            with sp.Fori(1, E // 2) as g:
                for q in range(2):
                    e = sp.snap(g * 2 + q)
                    srcs = matrices(sp.snap(e - 1))
                    for s in range(2):
                        split = sp.snap(g * 4 + (2 * (q - 2) + s + 1))
                        sp.wait_ge(s_lo, split)
                        load(q, s, srcs[s])
                    split = sp.snap(g * 2 + (q - 1))
                    sp.wait_ge(s_lod, split)
                    load(q, 2, srcs[2])
            for s, src in enumerate(matrices(E - 1)):
                if s < 2:
                    sp.wait_ge(s_lo, 2 * (E - 2) + s + 1)
                else:
                    sp.wait_ge(s_lod, E - 1)
                load(0, s, src)
            sp.wait_ge(s_routed, 1)
            for t in range(NT):
                for i in range(2):
                    sp.dma_start(acc[:, i, t, :], sums[i][t * P:(t + 1) * P, :]).then_inc(s_yin[t], 16)
            for t in range(NT):
                sp.wait_ge(s_fin, t + 1)
                sp.dma_start(out[0, t * P:(t + 1) * P, :], acc[:, 0, t, :]).then_inc(s_out, 16)
            sp.wait_ge(s_out, 16 * NT)

        @block.gpsimd
        def _(pool):
            pool.wait_ge(s_adc, 1)
            pool.memset(part, 0.0).then_inc(s_pz, 1)
            pool.wait_ge(s_brow, 16)
            for k in range(KD):
                pool.wait_ge(s_pmul, k + 1)
                if k:
                    pool.wait_ge(s_part[1], k)
                pool.tensor_tensor(part[:, 2048:], part[:, 2048:], wrow[1], ALU.add).then_inc(s_part[1], 1)
            pool.wait_ge(s_ip, 22)
            pool.memset(zeros, 0.0).then_inc(s_zero, 1)

            def gather(q, n=P):
                pool.indirect_dma_start(xg[0:n, q, :].bitcast(F32), None, hbuf[:, :],
                                        bass.IndirectOffsetOnAxis(gidx[0:n, q:q + 1], 0),
                                        bounds_check=T - 1, oob_is_err=False).then_inc(s_gt[q], 16)

            def split_first(s):
                pool.wait_ge(s_hi, s + 1)
                pool.tensor_tensor(whl[:, EW + s * CW:EW + (s + 1) * CW], raww[:, s * CW:(s + 1) * CW],
                                   whl[:, s * CW:(s + 1) * CW].bitcast(F32), ALU.subtract)\
                    .then_inc(s_lod if s == 2 else s_lo0, 1)

            def split_down(parity, n_hi):
                pool.wait_ge(s_hi, n_hi)
                o = parity * (2 * EW) + 2 * CW
                pool.tensor_tensor(whl[:, bass.ds(o + EW, CW)], raww[:, bass.ds(parity * EW + 2 * CW, CW)],
                                   whl[:, bass.ds(o, CW)].bitcast(F32), ALU.subtract).then_inc(s_lod, 1)

            split_first(0)
            pool.wait_ge(s_htp, NT)
            for i in range(2):
                pool.wait_ge(s_hst[i], 16 * NT // 2)
            pool.wait_ge(s_gi, 2)
            pool.sem_inc(s_pgo, 1)
            for q in range(2):
                gather(q)
            split_first(1)
            pool.wait_ge(s_lge, NT)
            split_first(2)

            def scatter(q, n=P):
                pool.indirect_dma_start(sums[q][:, :], bass.IndirectOffsetOnAxis(sidx[0:n, q:q + 1], 0), ysbs[q][0:n],
                                        None, bounds_check=T - 1, oob_is_err=False, compute_op=ALU.add)\
                    .then_inc(s_scat[q], 16)

            def by_size(full, move, q):
                if full is None:
                    move(q)
                else:
                    half = pool.snap(1 - full)
                    with pool.If(full):
                        move(q)
                    with pool.If(half):
                        move(q, P // 2)

            def step(i, q, full2, full1):
                n1 = pool.snap(i + (q + 1))
                n2 = pool.snap(i + (q + 2))
                n3 = pool.snap(i + (q + 3))
                pool.wait_ge(s_xt, n1)
                pool.wait_ge(s_gi, n3)
                pool.sem_inc(s_pgo, 1)
                by_size(full2, gather, q)
                pool.wait_ge(s_yev, n2)
                pool.wait_ge(s_si, n1)
                pool.sem_inc(s_pgo, 1)
                by_size(full1, scatter, 1 - q)

            pool.wait_ge(s_sum0, 32)
            for n in range(NT):
                step(n - n % 2, n % 2, None, None)
            split_down(1, 6)
            pool.wait_ge(s_tab, 1)
            nb = pool.value_load(ntab[0:1, 0:1], min_val=NT + E, max_val=MAXB)
            with pool.Fori(NT, nb, 2) as i:
                for q in range(2):
                    full2, full1 = (pool.value_load(tab[0:1, bass.ds(i + (q + d + B_FULL), 1)], min_val=0, max_val=1)
                                    for d in (2, -1))
                    step(i, q, full2, full1)
                    nxt = pool.value_load(tab[0:1, bass.ds(i + (q + B_SPLIT), 1)], min_val=0, max_val=E)
                    par = pool.snap(nxt % 2)
                    with pool.If(nxt):
                        split_down(par, nxt * 3 + 3)
            pairs = (nb + 1) // 2
            n_last = pool.snap(pairs * 2 + 2)
            n_si = pool.snap(pairs * 2 + 1)
            pool.wait_ge(s_yev, n_last)
            pool.wait_ge(s_si, n_si)
            pool.sem_inc(s_pgo, 1)
            scatter(1)
            n_even = pool.snap(pairs * 16)
            n_odd = pool.snap(pairs * 16 + 16)
            pool.wait_ge(s_scat[0], n_even)
            pool.wait_ge(s_scat[1], n_odd)
            for q in range(2):
                pool.wait_ge(s_gt[q], n_odd)
            pool.sem_inc(s_routed, 1)

        @block.scalar
        def _(act):
            order = [0]

            def then(ins):
                order[0] += 1
                ins.then_inc(s_ca, 1)
                act.wait_ge(s_ca, order[0])

            act.dma_start(c2[:, 0, :], a["c"][0].rearrange("(p k) -> p k", k=KD)).then_inc(s_c, 16)
            act.dma_start(c2[:, 1, :], a["c_ctx"].rearrange("(p k) -> p k", k=KD)).then_inc(s_c, 16)
            act.dma_start(cst[:], a["consts"]).then_inc(s_cst, 16)
            act.dma_start(rope[:], a["rope"]).then_inc(s_small, 16)
            act.dma_start(gcol, a["g_pre_mix"][0].rearrange("(p k) -> p k", k=KD)).then_inc(s_small, 16)
            act.dma_start(bcol, a["b_ada"][0, 0:2 * D].rearrange("(r p k) -> p r k", r=2, k=KD)).then_inc(s_small, 16)
            with nc.allow_non_contiguous_dma(reason="three short vectors as columns"):
                act.dma_start(gsub, a["g_subln"][0].rearrange("(p k) -> p k", k=1)).then_inc(s_small, 16)
                act.dma_start(bpool, a["b_pool"][0].rearrange("(g p) -> p g", p=P)).then_inc(s_small, 16)
                act.dma_start(pscale, a["pool_scale"][0].rearrange("(g p) -> p g", p=P)).then_inc(s_small, 16)
            for i, name in enumerate(("lambda_q1", "lambda_k1", "lambda_q2", "lambda_k2")):
                act.dma_start(lamv[:, i, :], a[name].to_broadcast([P, 64])).then_inc(s_small, 16)
            act.wait_ge(s_c, 32)
            act.activation(sc2.rearrange("p k s -> p s k"), c2, ACT.Silu).then_inc(s_silc, 1)
            for t in range(NC_ + NT):
                if t == 0:
                    act.wait_ge(s_ctx, 16)
                if t == NC_:
                    act.wait_ge(s_x, 16)
                src = ctx_in[:, t, :] if t < NC_ else xres[:, t - NC_, :]
                then(act.activation(actT[:, 0:D], src, ACT.Square, accum_out=ssq[:, t:t + 1]))
            act.wait_ge(s_cst, 16)
            act.activation(rstd, ssq, ACT.Sqrt, scale=1.0 / D, bias=cst[:, C_EPS:C_EPS + 1]).then_inc(s_sq, 1)
            for t in range(NC_ + NT):
                act.wait_ge(s_tp, t + 1)
                dst = hcT[:, :, t * P:(t + 1) * P] if t < NC_ else hxT[:, :, (t - NC_) * P:(t - NC_ + 1) * P]
                act.copy(dst, pp[t % 2][:, :].rearrange("p (k t) -> p k t", k=KD)).then_inc(s_tev, 1)
            act.wait_ge(s_ad2, 1)
            for i in range(2):
                last = act.copy(ada2[:, 1024 * i:1024 * i + 1024], pp[2 + i][0:2, :])
            last.then_inc(s_ad2e, 1)
            act.wait_ge(s_mod, 1)
            then(act.activation(dots, dots, ACT.Exp))
            act.sem_inc(s_sq, 1)
            for n in range(22):
                bank = pp[(n % 4) // 2][:, 512 * (n % 2):512 * (n % 2) + 512]
                act.wait_ge(s_ip, n + 1)
                if n < 4:
                    act.copy(kT[:, n, 0:CTX], bank[:, 0:CTX]).then_inc(s_ipe, 1)
                elif n < 12:
                    if n >= 6:
                        act.wait_ge(s_rope, n - 5)
                    act.copy(raw[:, n % 2, :], bank).then_inc(s_ipe, 1)
                elif n < 16:
                    act.copy(pT[:, n - 12, :], bank).then_inc(s_ipe, 1)
                else:
                    act.copy(vv[:, n - 16, :], bank).then_inc(s_ipe, 1)
                if n % 2 == 0 and 4 <= n < 20:
                    k = (n - 4) // 2
                    act.wait_ge(s_wrow[1], 16 * (k + 1))
                    act.activation(wrow[1], wrow[1], ACT.Copy, scale=sc2[:, k, 0:1]).then_inc(s_pmul, 1)
            def round_weights(s, parity, hi_free):
                if hi_free is not None:
                    act.wait_ge(s_gu if s < 2 else s_dn, hi_free)
                act.copy(whl[:, bass.ds(parity * (2 * EW) + s * CW, CW)],
                         raww[:, bass.ds(parity * EW + s * CW, CW)]).then_inc(s_hi, 1)

            for st in range(STEPS):
                if st < 16:
                    if st >= 2:
                        act.wait_ge(s_aTp, st - 1)
                    for s in range(2):
                        act.wait_ge(s_nmx, 2 * st + s + 1)
                        act.activation(e12[:, st % 2, s, :], pp[s][:, 0:KEYS], ACT.Exp, bias=nmx[:, s:s + 1],
                                       scale=SCALE, accum_out=lsum[:, s:s + 1]).then_inc(s_exp, 1)
                if 1 <= st < 17:
                    u = st - 1
                    act.wait_ge(s_aTp, u + 1)
                    if u >= 2:
                        act.wait_ge(s_o, u - 1)
                    act.copy(aT[:, u % 2], pp[2][:, 0:KEYS].rearrange("p (c q) -> p c q", c=NKEY)).then_inc(s_aTe, 1)
                if 2 <= st < 18:
                    u = st - 2
                    t, h = divmod(u, HEADS)
                    act.wait_ge(s_o, u + 1)
                    act.copy(oall[:, t % 2, h, :], pp[3][:, 0:P]).then_inc(s_oe, 1)
                    act.wait_ge(s_oe, u + 1)
                    act.activation(junk[:, 0:P], oall[:, t % 2, h, :], ACT.Square, accum_out=ossq[:, u:u + 1])\
                       .then_inc(s_osq, 1)
                    act.wait_ge(s_osq, u + 1)
                t = tile_at(st, 5)
                if t is not None:
                    act.activation(orst[:, t * HEADS:(t + 1) * HEADS], ossq[:, t * HEADS:(t + 1) * HEADS], ACT.Sqrt,
                                   scale=1.0 / P, bias=cst[:, C_EPS:C_EPS + 1]).then_inc(s_ors, 1)
                t = tile_at(st, 7)
                if t is not None:
                    act.wait_ge(s_y, t + 1)
                    if t >= 2:
                        act.wait_ge(s_hst[t % 2], 16 * (t // 2))
                    act.copy(y1[:, t % 2, :], pp[3][:, :]).then_inc(s_ye, 1)
                    act.wait_ge(s_ye, t + 1)
                    then(act.activation(junk, y1[:, t % 2, :], ACT.Square, accum_out=yssq[:, t:t + 1]))
                    act.activation(yrst[:, t:t + 1], yssq[:, t:t + 1], ACT.Sqrt, scale=1.0 / D,
                                   bias=cst[:, C_EPS:C_EPS + 1]).then_inc(s_yrs, 1)
                t = tile_at(st, 8)
                if t is not None:
                    act.wait_ge(s_x1, t + 1)
                    then(act.activation(junk, xres[:, t, :], ACT.Square, accum_out=hssq[:, t:t + 1]))
                    act.activation(hrst[:, t:t + 1], hssq[:, t:t + 1], ACT.Sqrt, scale=1.0 / D,
                                   bias=cst[:, C_EPS:C_EPS + 1]).then_inc(s_hrs, 1)
                    if t == NT - 1:
                        act.wait_ge(s_raw[0][0], 16)
                        round_weights(0, 0, None)
                t = tile_at(st, 10)
                if t is not None:
                    act.wait_ge(s_h, t + 1)
                    act.dma_start(hbuf[t * P:(t + 1) * P, :], y1[:, t % 2, :]).then_inc(s_hst[t % 2], 16)
                    act.wait_ge(s_htp, t + 1)
                    act.copy(hT, pp[2][:, :].rearrange("p (k t) -> p k t", k=KD)).then_inc(s_hte0, 1)
                t = tile_at(st, 11)
                if t is not None:
                    act.wait_ge(s_lg, t + 1)
                    act.activation(rt[:, 0, t * E:(t + 1) * E], pp[2][:, 0:E], ACT.Exp, scale=-1.0).then_inc(s_lge, 1)

            for s in (1, 2):
                act.wait_ge(s_raw[0][s], 16)
                round_weights(s, 0, None)
            act.activation(sg[:, 0:1], cst[:, C_EPS:C_EPS + 1], ACT.Silu).then_inc(s_ca, 1)
            order[0] += 1

            def evacuate_block(n):
                act.wait_ge(s_xt, n)
                act.copy(xTh[:], pp[1][:, :].rearrange("p (k s) -> p k s", k=KD)).then_inc(s_xte, 1)

            def keep_y(q, n, scattered):
                act.wait_ge(s_dn, n)
                if not (isinstance(scattered, int) and scattered == 0):
                    act.wait_ge(s_scat[q], scattered)
                act.copy(ysbs[q], pp[0][:, :]).then_inc(s_yev, 1)

            evacuate_block(1)
            act.sem_inc(s_yev, 1)

            def step(i, q, nxt, par):
                def split(ss):
                    for s in ss:
                        act.wait_ge(s_raw[0][s], ((nxt + 2) // 2) * 16)
                        act.wait_ge(s_raw[1][s], ((nxt + 1) // 2) * 16)
                        round_weights(s, par, i + (q + 1))

                def perhaps(ss):
                    if isinstance(nxt, int):
                        if nxt:
                            split(ss)
                    else:
                        with act.If(nxt):
                            split(ss)

                perhaps((0, 1))
                act.wait_ge(s_gu, i + (q + 2))
                act.activation(sg, pp[2][:, 0:F], ACT.Silu).then_inc(s_sil, 1)
                evacuate_block(i + (q + 2))
                keep_y(1 - q, i + (q + 1), i * 8)
                perhaps((2,))

            for n in range(NT):
                if n == NT - 1:
                    act.wait_ge(s_tab, 1)
                step(n - n % 2, n % 2, 1 if n == NT - 1 else 0, 1)
            nb = act.value_load(ntab[0:1, 0:1], min_val=NT + E, max_val=MAXB)
            with act.Fori(NT, nb, 2) as i:
                for q in range(2):
                    nxt = act.value_load(tab[0:1, bass.ds(i + (q + B_SPLIT), 1)], min_val=0, max_val=E)
                    step(i, q, nxt, act.snap(nxt % 2))
            pairs = (nb + 1) // 2
            keep_y(1, pairs * 2 + 1, pairs * 16)
            for t in range(NT):
                act.wait_ge(s_comb, t + 1)
                then(act.activation(fscr[:], acc[:, 0, t, :], ACT.Square, accum_out=fssq[:, t:t + 1]))
                act.activation(frst[:, t:t + 1], fssq[:, t:t + 1], ACT.Sqrt, scale=1.0 / D,
                               bias=cst[:, C_EPS:C_EPS + 1]).then_inc(s_frs, 1)

        @block.tensor
        def _(pe):
            pe.wait_ge(s_cst, 16)
            pe.wait_ge(s_silc, 1)

            def ada_rows(kk):
                if kk % 2 == 0:
                    pe.wait_ge(s_wa[kk // 2], 16)
                for n in range(4):
                    last = pe.matmul(pp[2 + n // 2][0:2, 512 * (n % 2):512 * (n % 2) + 512], sc2[:, kk, :],
                                     wa[kk // 2][:, kk % 2, 512 * n:512 * n + 512], start=(kk == 0),
                                     stop=(kk == KD - 1))
                return last

            for kk in range(KD):
                last = ada_rows(kk)
                for t in range(NC_ + NT)[2 * kk - 2:2 * kk] if 1 <= kk <= 3 else ():
                    pe.wait_ge(s_xn, t + 1)
                    if t >= 2:
                        pe.wait_ge(s_tev, t - 1)
                    for k in range(KD):
                        turned = pe.transpose(pp[t % 2][:, k * P:(k + 1) * P], xn[:, t % 4, k, :], ident)
                    turned.then_inc(s_tp, 1)
            last.then_inc(s_ad2, 1)
            pe.wait_ge(s_ad2e, 1)
            for r in range(2):
                row = ada2[:, r * D:(r + 1) * D].rearrange("s (q k) -> s k q", k=KD)
                for k in range(KD):
                    last = pe.matmul(pp[2][:, (r * KD + k) * 2:(r * KD + k) * 2 + 2], row[:, k, :], ident[0:2, 0:2],
                                     start=True, stop=True)
            last.then_inc(s_adc, 1)
            pe.wait_ge(s_tev, NC_ + NT)
            for n in range(22):
                bank = pp[(n % 4) // 2][:, 512 * (n % 2):512 * (n % 2) + 512]
                if n in (0, 4, 12, 16):
                    pe.wait_ge(s_win[(0, 4, 12, 16).index(n)], 16)
                if n >= 4:
                    pe.wait_ge(s_ipe, n - 3)
                for k in range(KD):
                    if n == 0:
                        pe.wait_ge(s_mod, k + 1)
                    elif n == 4:
                        pe.wait_ge(s_mod, KD + k + 1)
                    if n < 4:
                        o, l, r = bank[:, 0:CTX], w_in[:, k, 512 + n * P:512 + (n + 1) * P], hcT[:, k, :]
                    elif n < 16:
                        c0 = (n - 4) * P if n < 12 else 1536 + (n - 12) * P
                        o, l, r = bank, w_in[:, k, c0:c0 + P], hxT[:, k, :]
                    else:
                        i = n - 16
                        l = hcT[:, k, i * P:(i + 1) * P] if i < NC_ else hxT[:, k, (i - NC_) * P:(i - NC_ + 1) * P]
                        o, r = bank, w_in[:, k, 1024:1536]
                    last = pe.matmul(o, l, r, start=(k == 0), stop=(k == KD - 1))
                last.then_inc(s_ip, 1)
            pe.wait_ge(s_wpool, 16)
            pe.wait_ge(s_ipe, 22)
            for g in range(4):
                pe.wait_ge(s_pd, g + 1)
                pe.matmul(pp[g // 2][:, 512 * (g % 2):512 * (g % 2) + 512], wpool[:, g, :], pT[:, g, :],
                          start=True, stop=True).then_inc(s_pm, 1)
            for i in range(2):
                pe.wait_ge(s_part[i], KD)
            for cc in range(8):
                if cc >= 4:
                    pe.wait_ge(s_adre, cc - 3)
                pe.matmul(pp[2 + (cc % 4) // 2][:, 512 * (cc % 2):512 * (cc % 2) + 512], ones,
                          part[:, 512 * cc:512 * cc + 512], start=True, stop=True).then_inc(s_adr, 1)
            pe.wait_ge(s_rope, 8)
            pe.wait_ge(s_poolout, 4)
            for st in range(STEPS):
                if st < 16:
                    qb, h = divmod(st, HEADS)
                    for s in range(2):
                        if st:
                            pe.wait_ge(s_exp, 2 * st - 1 + s)
                        for c0, n in ((0, 512), (512, 256)):
                            last = pe.matmul(pp[s][:, c0:c0 + n], qT[64 * s:64 * s + 64, h, qb * P:(qb + 1) * P],
                                             kT[64 * s:64 * s + 64, h, c0:c0 + n], start=True, stop=True)
                        last.then_inc(s_sc, 1)
                if 1 <= st < 17:
                    u = st - 1
                    pe.wait_ge(s_a, u + 1)
                    if u == 0:
                        pe.wait_ge(s_adre, 8)
                    else:
                        pe.wait_ge(s_aTe, u)
                    if tile_at(st, 11) is not None:
                        pe.wait_ge(s_hte0, tile_at(st, 11) + 1)
                    if tile_at(st, 12) is not None:
                        pe.wait_ge(s_lge, tile_at(st, 12) + 1)
                    for c in range(NKEY):
                        last = pe.transpose(pp[2][:, c * P:(c + 1) * P], e12[:, u % 2, 0, c * P:(c + 1) * P], ident)
                    last.then_inc(s_aTp, 1)
                if 2 <= st < 18:
                    u = st - 2
                    pe.wait_ge(s_aTe, u + 1)
                    if u:
                        pe.wait_ge(s_oe, u)
                    if tile_at(st, 8) is not None:
                        pe.wait_ge(s_ye, tile_at(st, 8) + 1)
                    for c in range(NKEY):
                        last = pe.matmul(pp[3][:, 0:P], aT[:, u % 2, c, :], vv[:, c, u % HEADS * P:(u % HEADS + 1) * P],
                                         start=(c == 0), stop=(c == NKEY - 1))
                    last.then_inc(s_o, 1)
                t = tile_at(st, 6)
                if t is not None:
                    pe.wait_ge(s_on, t + 1)
                    for h in range(HEADS):
                        last = pe.transpose(pp[3][:, 512 + h * P:512 + (h + 1) * P], oall[:, t % 2, h, :], ident)
                    last.then_inc(s_oT, 1)
                t = tile_at(st, 7)
                if t is not None:
                    if t == 0:
                        pe.wait_ge(s_wout, 16)
                    pe.wait_ge(s_cat, t + 1)
                    pe.wait_ge(s_oe, min(st - 1, 16))
                    for n in range(2):
                        for j in range(KD):
                            l = headT[:, t % 2, j, :] if j < HEADS else poolT[:, j - HEADS, t * P:(t + 1) * P]
                            last = pe.matmul(pp[3][:, 512 * n:512 * n + 512], l, w_out[:, j, 512 * n:512 * n + 512],
                                             start=(j == 0), stop=(j == KD - 1))
                    last.then_inc(s_y, 1)
                t = tile_at(st, 10)
                if t is not None:
                    pe.wait_ge(s_h, t + 1)
                    pe.wait_ge(s_aTe, min(st, 16))
                    for k in range(KD):
                        last = pe.transpose(pp[2][:, k * P:(k + 1) * P], y1[:, t % 2, k * P:(k + 1) * P], ident)
                    last.then_inc(s_htp, 1)
                t = tile_at(st, 11)
                if t is not None:
                    if t == 0:
                        pe.wait_ge(s_wr, 16)
                    pe.wait_ge(s_hte0, t + 1)
                    pe.wait_ge(s_aTe, min(st, 16))
                    for k in range(KD):
                        last = pe.matmul(pp[2][:, 0:E], hT[:, k, :], w_r[:, k, :], start=(k == 0), stop=(k == KD - 1))
                    last.then_inc(s_lg, 1)
            def ranks():
                pe.wait_ge(s_sel, NT)
                for t in range(NT):
                    for c in range(t + 1):
                        pe.matmul(pp[3][:, t * E:(t + 1) * E], ones if c < t else cst[:, C_TRI:C_TRI + P],
                                  selt[:, c, :], start=(c == 0), stop=(c == t))
                for c in range(NT):
                    last = pe.matmul(pp[3][:, 512:512 + E], ones, selt[:, c, :], start=(c == 0), stop=(c == NT - 1))
                last.then_inc(s_rk, 1)

            def table_rows():
                pe.wait_ge(s_bt, 1)
                for i, col in enumerate((btab[:, 0:1], btab[:, 1:2], btab[:, 2:3], bfull)):
                    last = pe.matmul(pp[3][0:1, 512 + i * P:512 + (i + 1) * P], col, ident,
                                     start=(i == 0), stop=(i == 3))
                last.then_inc(s_btr, 1)

            def slots(eb, n):
                pe.wait_ge(s_oh, n)
                for c in range(NT):
                    last = pe.matmul(pp[3][:, 0:2], oneh[:, c, :],
                                     rtab[:, c, :, :].rearrange("p e w -> p (e w)")[:, bass.ds(eb * 2, 2)],
                                     start=(c == 0), stop=(c == NT - 1))
                last.then_inc(s_im, 1)

            def expert_of(b, d):
                return pe.value_load(tab[0:1, bass.ds(b + (B_E + d), 1)], min_val=0, max_val=E)

            def transpose_block(q):
                for k in range(KD):
                    last = pe.transpose(pp[1][:, k * P:(k + 1) * P].bitcast(F32R), xg[:, q, k * P:(k + 1) * P],
                                        identr[:])
                last.then_inc(s_xt, 1)

            def gate_up(w0, n):
                pe.wait_ge(s_xtl, n)
                o = pp[2][:, 0:2 * F].rearrange("p (s f) -> p s f", s=2)
                hi = whl[:, bass.ds(w0, 2 * CW)].rearrange("p (s k f) -> p s k f", s=2, k=KD)
                lo = whl[:, bass.ds(w0 + EW, 2 * CW)].rearrange("p (s k f) -> p s k f", s=2, k=KD)
                for k in range(KD):
                    pe.matmul(o, xTh[:, k, :], hi[:, :, k, :], start=(k == 0), stop=False)
                    pe.matmul(o, xTh[:, k, :], lo[:, :, k, :], start=False, stop=False)
                    last = pe.matmul(o, xTl[:, k, :], hi[:, :, k, :], start=False, stop=(k == KD - 1))
                last.then_inc(s_gu, 1)

            def down(e, n):
                w0 = pe.snap((e % 2) * (2 * EW))
                pe.wait_ge(s_lod, e + 1)
                pe.wait_ge(s_hte, n)
                pe.wait_ge(s_yev, n)
                for m in range(2):
                    for j in range(FJ):
                        o = pp[0][:, 512 * m:512 * m + 512]
                        c0 = 2 * CW + j * D + 512 * m
                        hi = whl[:, bass.ds(w0 + c0, 512)]
                        lo = whl[:, bass.ds(w0 + (EW + c0), 512)]
                        pe.matmul(o, hTh[:, j, :], hi, start=(j == 0), stop=False)
                        pe.matmul(o, hTh[:, j, :], lo, start=False, stop=False)
                        last = pe.matmul(o, hTl[:, j, :], hi, start=False, stop=(j == FJ - 1))
                last.then_inc(s_dn, 1)

            def transpose_hidden(n):
                pe.wait_ge(s_hm, n)
                for j in range(FJ):
                    last = pe.transpose(pp[2][:, 512 + j * P:512 + (j + 1) * P], hmid[:, j, :], ident)
                last.then_inc(s_ht, 1)

            pe.wait_ge(s_gt[0], 16)
            transpose_block(0)
            pe.wait_ge(s_lge, NT)
            pe.sem_inc(s_gu, 1)
            pe.wait_ge(s_lo0, 2)
            for n in range(NT):
                gate_up(0, n + 1)
                if n == 0:
                    ranks()
                if n == 2:
                    table_rows()
                pe.wait_ge(s_gt[1 - n % 2], 16 * ((n + 1) // 2 + 1))
                transpose_block(1 - n % 2)
                down(0, n + 1)
                transpose_hidden(n + 1)
                if n >= 2:
                    if n == 2:
                        pe.wait_ge(s_tab, 1)
                    pe.wait_ge(s_sf, n + 2)
                    slots(expert_of(n, 2), n - 1)
            nb = pe.value_load(ntab[0:1, 0:1], min_val=NT + E, max_val=MAXB)
            with pe.Fori(NT, nb, 2) as i:
                for q in range(2):
                    eb = expert_of(i, q)
                    e2 = expert_of(i, q + 2)
                    pe.wait_ge(s_sf, i + (q + 2))
                    slots(e2, i + (q + 3 - NT))
                    pe.wait_ge(s_lo, eb * 2 + 2)
                    gate_up(pe.snap((eb % 2) * (2 * EW)), i + (q + 1))
                    pe.wait_ge(s_gt[1 - q], i * 8 + (16 + 16 * q))
                    transpose_block(1 - q)
                    down(expert_of(i, q - 1), i + (q + 1))
                    transpose_hidden(i + (q + 1))
            pairs = (nb + 1) // 2
            down(E, pairs * 2 + 1)

        @block.vector
        def _(dve):
            order = [0]

            def then(ins):
                order[0] += 1
                ins.then_inc(s_cd, 1)
                dve.wait_ge(s_cd, order[0])

            dve.wait_ge(s_sq, 1)
            dve.wait_ge(s_small, 16 * NSMALL)
            then(dve.reciprocal(rstd, rstd))
            for t in range(NC_ + NT):
                src = ctx_in[:, t, :] if t < NC_ else xres[:, t - NC_, :]
                if t >= 4:
                    dve.wait_ge(s_tp, t - 3)
                dve.tensor_scalar(xn[:, t % 4], src.rearrange("p (q k) -> p k q", k=KD), rstd[:, t:t + 1], None,
                                  ALU.mult).then_inc(s_xn, 1)
            for i in range(2):
                then(dve.tensor_tensor_reduce(lamv[:, 2 * i, :], lamv[:, 2 * i, :], lamv[:, 2 * i + 1, :], 1.0, 0.0,
                                              ALU.mult, ALU.add, dots[:, i:i + 1]))
            dve.wait_ge(s_adc, 1)
            for r in range(2):
                then(dve.tensor_tensor(modc[:, r], pp[2][:, r * 16:r * 16 + 16].rearrange("p (k s) -> p k s", s=2),
                                       bcol[:, r, :].rearrange("p (k s) -> p k s", s=1).to_broadcast([P, KD, 2]),
                                       ALU.add))
            then(dve.scalar_tensor_tensor(modc[:, 1], modc[:, 1], 1.0,
                                          gcol.rearrange("p (k s) -> p k s", s=1).to_broadcast([P, KD, 2]),
                                          ALU.add, ALU.mult))
            dve.wait_ge(s_tev, NC_ + NT)
            for s, x in ((1, hcT), (0, hxT)):
                for k in range(KD):
                    dve.tensor_scalar(x[:, k, :], x[:, k, :], modc[:, 1, k, s:s + 1], modc[:, 0, k, s:s + 1],
                                      ALU.mult, ALU.add).then_inc(s_mod, 1)
            dve.wait_ge(s_mod, 2 * KD)
            mask = [(i + 16) % 32 for i in range(32)]
            cos, sin = rope[:, 0:T], rope[:, T:2 * T]

            def add_half_row(k):
                if k == 0:
                    dve.wait_ge(s_brow, 16)
                else:
                    dve.wait_ge(s_part[0], k)
                dve.wait_ge(s_wrow[0], 16 * (k + 1))
                dve.scalar_tensor_tensor(part[:, 0:2048], wrow[0], sc2[:, k, 0:1], part[:, 0:2048],
                                         ALU.mult, ALU.add).then_inc(s_part[0], 1)

            for n in range(4, 12):
                h = (n - 4) % HEADS
                dst = qT[:, h, :] if n < 8 else kT[:, h, CTX:]
                r = raw[:, n % 2, :]
                dve.wait_ge(s_ipe, n + 1)
                then(dve.stream_shuffle(swp, r, mask))
                then(dve.tensor_tensor(dst, r, cos, ALU.mult))
                then(dve.tensor_tensor(swp, swp, sin, ALU.mult))
                then(dve.tensor_tensor(dst, dst, swp, ALU.add))
                dve.sem_inc(s_rope, 1)
                if n % 2:
                    add_half_row((n - 5) // 2)
            for g, w in enumerate(WINDOWS):
                p = pT[:, g, :]
                dve.wait_ge(s_ipe, 13 + g)
                cur, nxt = sumA, sumB
                then(dve.memset(cur, 0.0))
                then(dve.tensor_copy(cur[:, PAD:PAD + T], p))
                then(dve.tensor_tensor(nxt[:, 1:], cur[:, :TP - 1], cur[:, 1:], ALU.add))
                m = 1
                while m < w // 2:
                    cur, nxt = nxt, cur
                    lo, hi = 2 * m, TP - 2 * m + 1
                    then(dve.tensor_tensor(nxt[:, lo:hi], cur[:, lo - m:hi - m], cur[:, lo + m:hi + m], ALU.add))
                    m *= 2
                cur = nxt[:, PAD:PAD + T]
                fac = cst[:, C_FAC + 16 * g:C_FAC + 16 * g + 16]
                then(dve.tensor_tensor(cur[:, 0:8], cur[:, 0:8], fac[:, 0:8], ALU.mult))
                then(dve.tensor_tensor(cur[:, T - 8:], cur[:, T - 8:], fac[:, 8:16], ALU.mult))
                then(dve.scalar_tensor_tensor(p, cur, 1.0 / w, p, ALU.mult, ALU.subtract))
                dve.sem_inc(s_pd, 1)
                add_half_row(4 + g)
            for g in range(4):
                dve.wait_ge(s_pm, g + 1)
                dve.tensor_scalar(poolT[:, g, :], pp[g // 2][:, 512 * (g % 2):512 * (g % 2) + 512],
                                  bpool[:, g:g + 1], pscale[:, g:g + 1], ALU.add, ALU.mult).then_inc(s_poolout, 1)
            dve.wait_ge(s_grow, 48)
            for cc in range(8):
                dve.wait_ge(s_adr, cc + 1)
                dst = rows[:, 512 * cc:512 * cc + 512]
                src = pp[2 + (cc % 4) // 2][:, 512 * (cc % 2):512 * (cc % 2) + 512]
                r, c0 = cc // 2, 512 * (cc % 2)
                if r == 1:
                    last = dve.tensor_copy(dst, src)
                elif r == 2:
                    last = dve.scalar_tensor_tensor(dst, src, 1.0, grow[:, 1, c0:c0 + 512], ALU.add, ALU.mult)
                else:
                    last = dve.tensor_tensor(dst, src, grow[:, 0 if r == 0 else 2, c0:c0 + 512], ALU.mult)
                last.then_inc(s_adre, 1)
            dve.wait_ge(s_sq, 2)
            then(dve.tensor_tensor(lam, dots[:, 1:2], dots[:, 0:1], ALU.subtract))
            then(dve.tensor_scalar(lam, lam, LAM_INIT, None, ALU.subtract))
            ex, bi, msk, tmp, inc = (rt[:, i, :].rearrange("p (c e) -> p c e", c=NT) for i in range(5))

            def route(t):
                dve.wait_ge(s_lge, t + 1)
                if t == 0:
                    dve.wait_ge(s_rb, 16)
                then(dve.tensor_scalar(tmp[:, t, :], ex[:, t, :], 1.0, None, ALU.add))
                then(dve.reciprocal(sct[:, t, :], tmp[:, t, :]))
                then(dve.tensor_tensor(bi[:, t, :], sct[:, t, :], brow, ALU.add))
                for g in range(8):
                    last = dve.max(m8[:, g * 8:g * 8 + 8], bi[:, t, g * 8:g * 8 + 8])
                then(last)
                top = m8[:, 0:64].rearrange("p (n s) -> p n s", s=8)
                gs, place, keep, gone = (tnb[:, 8 * i:8 * i + 8] for i in range(4))
                then(dve.tensor_tensor(gs.rearrange("p (n s) -> p n s", s=1), top[:, :, 0:1], top[:, :, 1:2], ALU.add))
                gj = gs.rearrange("p (a j) -> p a j", a=1).to_broadcast([P, 8, 8])
                gi = gs.rearrange("p (i a) -> p i a", a=1).to_broadcast([P, 8, 8])
                x = tmp[:, t, :].rearrange("p (i j) -> p i j", i=8)
                y = inc[:, t, :].rearrange("p (i j) -> p i j", i=8)
                dve.tensor_tensor(y, gj, gi, ALU.is_gt)
                then(dve.tensor_tensor(x, gj, gi, ALU.is_equal))
                then(dve.tensor_tensor(x, x, cst[:, C_JLT:C_JLT + 64].rearrange("p (i j) -> p i j", i=8), ALU.mult))
                then(dve.tensor_tensor(x, x, y, ALU.add))
                then(dve.tensor_reduce(place, x, AX, ALU.add))
                then(dve.tensor_scalar(keep, place, 4.0, None, ALU.is_lt))
                b3 = bi[:, t, :].rearrange("p (g j) -> p g j", g=8)

                def spread(v):
                    return v.rearrange("p (g a) -> p g a", a=1).to_broadcast([P, 8, 8])
                dve.tensor_tensor(b3, b3, spread(keep), ALU.mult)
                then(dve.tensor_scalar(gone, keep, 1.0, 1e30, ALU.subtract, ALU.mult))
                then(dve.tensor_tensor(b3, b3, spread(gone), ALU.add))
                then(dve.max(m8[:, 64:72], bi[:, t, :]))
                then(dve.match_replace(out=msk[:, t, :], in_to_replace=m8[:, 64:72], in_values=bi[:, t, :],
                                       imm_value=3e38))
                then(dve.tensor_scalar(selt[:, t, :], msk[:, t, :], 2e38, None, ALU.is_ge))
                dve.sem_inc(s_sel, 1)
                then(dve.tensor_tensor(sct[:, t, :], sct[:, t, :], selt[:, t, :], ALU.mult))
                then(dve.tensor_reduce(rsum[:, t:t + 1], sct[:, t, :], AX, ALU.add))

            for o, sm in ((hTh, s_hth), (hTl, s_hte)):
                dve.tensor_scalar(o[:], cst[:, C_IOTA:C_IOTA + F].rearrange("p (j q) -> p j q", j=FJ), 0.0, None,
                                  ALU.mult).then_inc(sm, 1)
            then(dve.memset(srow, 2 * FAR))
            then(dve.tensor_copy(identr[:], ident))
            then(dve.memset(slotf[:], 1.0))

            def shared_index(n):
                dve.tensor_copy(gidx[:, n % 2:n % 2 + 1], cst[:, C_RANK + n:C_RANK + n + 1]).then_inc(s_gi, 1)

            def shared_slots(n):
                dve.tensor_copy(slotf[:, n % 2, 0:1], cst[:, C_TOK + n:C_TOK + n + 1]).then_inc(s_sf, 1)

            for n in range(2):
                shared_index(n)
                shared_slots(n)
            for st in range(STEPS):
                if st < 16:
                    e = e12[:, st % 2]
                    for s in range(2):
                        dve.wait_ge(s_sc, 2 * st + s + 1)
                        then(dve.tensor_reduce(mx[:, s:s + 1], pp[s][:, 0:KEYS], AX, ALU.max))
                        dve.tensor_scalar(nmx[:, s:s + 1], mx[:, s:s + 1], -SCALE, None, ALU.mult).then_inc(s_nmx, 1)
                    dve.wait_ge(s_exp, 2 * st + 2)
                    then(dve.reciprocal(rl, lsum))
                    then(dve.tensor_tensor(rl[:, 1:2], rl[:, 1:2], lam, ALU.mult))
                    then(dve.tensor_scalar(e[:, 1, :], e[:, 1, :], rl[:, 1:2], None, ALU.mult))
                    dve.scalar_tensor_tensor(e[:, 0, :], e[:, 0, :], rl[:, 0:1], e[:, 1, :],
                                             ALU.mult, ALU.add).then_inc(s_a, 1)
                t = tile_at(st, 5)
                if t is not None:
                    dve.wait_ge(s_ors, t + 1)
                    then(dve.reciprocal(orst[:, t * HEADS:(t + 1) * HEADS], orst[:, t * HEADS:(t + 1) * HEADS]))
                    for h in range(HEADS):
                        u = t * HEADS + h
                        last = dve.tensor_scalar(oall[:, t % 2, h, :], oall[:, t % 2, h, :], orst[:, u:u + 1],
                                                 1.0 - LAM_INIT, ALU.mult, ALU.mult)
                    last.then_inc(s_on, 1)
                t = tile_at(st, 6)
                if t is not None:
                    dve.wait_ge(s_oT, t + 1)
                    dve.tensor_scalar(headT[:, t % 2], pp[3][:, 512:1024].rearrange("p (h q) -> p h q", h=HEADS),
                                      gsub, None, ALU.mult).then_inc(s_cat, 1)
                t = tile_at(st, 8)
                if t is not None:
                    y = y1[:, t % 2, :]
                    dve.wait_ge(s_yrs, t + 1)
                    then(dve.reciprocal(yrst[:, t:t + 1], yrst[:, t:t + 1]))
                    then(dve.scalar_tensor_tensor(y, y, yrst[:, t:t + 1], arow[:, 0], ALU.mult, ALU.mult))
                    dve.tensor_tensor(xres[:, t, :], xres[:, t, :], y, ALU.add).then_inc(s_x1, 1)
                t = tile_at(st, 9)
                if t is not None:
                    dve.wait_ge(s_hrs, t + 1)
                    then(dve.reciprocal(hrst[:, t:t + 1], hrst[:, t:t + 1]))
                    perm = y1[:, t % 2, :].rearrange("p (k q) -> p k q", k=KD)
                    then(dve.scalar_tensor_tensor(perm, xres[:, t, :].rearrange("p (q k) -> p k q", k=KD),
                                                  hrst[:, t:t + 1], arow[:, 2].rearrange("p (q k) -> p k q", k=KD),
                                                  ALU.mult, ALU.mult))
                    dve.tensor_tensor(perm, perm, arow[:, 1].rearrange("p (q k) -> p k q", k=KD), ALU.add)\
                       .then_inc(s_h, 1)
                t = tile_at(st, 13)
                if t is not None:
                    route(t)
            then(dve.reciprocal(rsum, rsum))
            for t in range(NT):
                dve.tensor_scalar(rtab[:, t, 1:, 1], sct[:, t, :], rsum[:, t:t + 1], ROUTED_SCALE,
                                  ALU.mult, ALU.mult)
                last = dve.tensor_scalar(rtab[:, t, 1:, 0], ones[:, 0:E], cst[:, C_TOK + t:C_TOK + t + 1], None,
                                         ALU.mult)
            then(last)

            def onehots(eb, r0):
                for c in range(NT):
                    last = dve.tensor_scalar(oneh[:, c, :], cst[:, bass.ds(r0 + C_IOTA, P)],
                                             key[:, c, bass.ds(eb, 1)], None, ALU.is_equal)
                last.then_inc(s_oh, 1)

            def block_of(b, d):
                return (dve.value_load(tab[0:1, bass.ds(b + (B_E + d), 1)], min_val=0, max_val=E),
                        dve.value_load(tab[0:1, bass.ds(b + (B_R0 + d), 1)], min_val=0, max_val=T))

            def gather_index(q):
                dve.tensor_scalar(gidx[:, q:q + 1], pp[3][:, 0:1], FAR, None, ALU.add).then_inc(s_gi, 1)

            def keep_slots(q):
                dve.tensor_copy(slotf[:, q, :], pp[3][:, 0:2]).then_inc(s_sf, 1)

            def scatter_index(q, scattered):
                if not (isinstance(scattered, int) and scattered == 0):
                    dve.wait_ge(s_scat[q], scattered)
                dve.tensor_copy(sidx[:, q:q + 1], srow[:, q:q + 1]).then_inc(s_si, 1)

            def split_weights(s, parity, n_hi):
                dve.wait_ge(s_hi, n_hi)
                o = parity * (2 * EW)
                dve.tensor_tensor(whl[:, bass.ds(o + (EW + s * CW), CW)], raww[:, bass.ds(parity * EW + s * CW, CW)],
                                  whl[:, bass.ds(o + s * CW, CW)].bitcast(F32), ALU.subtract).then_inc(s_lo, 1)

            def split_block(n):
                dve.wait_ge(s_xte, n)
                dve.tensor_tensor(xTl[:], pp[1][:, :].rearrange("p (k s) -> p k s", k=KD), xTh[:].bitcast(F32),
                                  ALU.subtract).then_inc(s_xtl, 1)

            def hidden(i, q):
                dve.wait_ge(s_sf, i + (q + 1))
                dve.wait_ge(s_sil, i + (q + 1))
                dve.scalar_tensor_tensor(hmid[:].rearrange("p j q -> p q j"),
                                         sg.rearrange("p (q j) -> p q j", j=FJ), slotf[:, q, 1:2],
                                         pp[2][:, F:2 * F].rearrange("p (q j) -> p q j", j=FJ),
                                         ALU.mult, ALU.mult).then_inc(s_hm, 1)

            def keep_rows(i, q):
                dve.tensor_scalar(srow[:, q:q + 1], slotf[:, q, 0:1], FAR, None, ALU.add).then_inc(s_sr, 1)
                dve.wait_ge(s_hm, i + (q + 1))
                dve.wait_ge(s_sr, i + (q + 1))

            def split_hidden(i, q):
                dve.wait_ge(s_ht, i + (q + 1))
                hps = pp[2][:, 512:512 + F].rearrange("p (j q) -> p j q", j=FJ)
                dve.tensor_copy(hTh[:], hps).then_inc(s_hth, 1)
                dve.wait_ge(s_hth, i + (q + 2))
                dve.tensor_tensor(hTl[:], hps, hTh[:].bitcast(F32), ALU.subtract).then_inc(s_hte, 1)

            def shared_step(n):
                i, q = n - n % 2, n % 2
                if n < 2:
                    dve.wait_ge(s_gt[q], 16)
                    shared_index(n + 2)
                scatter_index(1 - q, i * 8)
                if n == NT - 1:
                    for s in range(2):
                        split_weights(s, 1, 3 + (s + 1))
                hidden(i, q)
                split_block(n + 2)
                keep_rows(i, q)
                if n < 2:
                    shared_slots(n + 2)
                split_hidden(i, q)

            split_block(1)
            for s in range(2):
                dve.wait_ge(s_lo0, s + 1)
                dve.sem_inc(s_lo, 1)
            shared_step(0)
            dve.wait_ge(s_rk, 1)
            then(dve.tensor_scalar(tmp, pp[3][:, 0:NT * E].rearrange("p (c e) -> p c e", c=NT), 1.0, None, ALU.add))
            then(dve.tensor_tensor(tmp, tmp, selt, ALU.mult))
            then(dve.tensor_scalar(key[:, :, 1:], tmp, 1.0, None, ALU.subtract))
            nblk, cum, cnt, done, own = (heads[:, 5120 + 80 * i:5120 + 80 * i + E] for i in range(5))
            then(dve.tensor_copy(cnt, pp[3][:, 512:512 + E]))
            then(dve.tensor_scalar(nblk, cnt, P + 0.5, 1.0, ALU.is_ge, ALU.add))
            for th in (2 * P + 0.5, 3 * P + 0.5):
                then(dve.scalar_tensor_tensor(nblk, cnt, th, nblk, ALU.is_ge, ALU.add))
            then(dve.tensor_tensor_scan(cum, ones[:, 0:E], nblk, 0.0, ALU.mult, ALU.add))

            blk = cst[:, C_PART:C_PART + 1]
            then(dve.tensor_scalar(done, cum, blk, None, ALU.is_le))
            then(dve.tensor_tensor(own, cum, nblk, ALU.subtract))
            then(dve.tensor_scalar(own, own, blk, None, ALU.is_le))
            then(dve.tensor_tensor(own, own, done, ALU.subtract))
            then(dve.tensor_tensor(own, own, cnt, ALU.mult))
            dve.tensor_reduce(bfull, own, AX, ALU.add)
            then(dve.tensor_reduce(btab[:, 0:1], done, AX, ALU.add))
            then(dve.tensor_tensor(done, done, nblk, ALU.mult))
            then(dve.tensor_reduce(btab[:, 1:2], done, AX, ALU.add))
            then(dve.tensor_tensor(btab[:, 1:2], blk, btab[:, 1:2], ALU.subtract))
            then(dve.tensor_scalar(btab[:, 3:4], blk, -0.5, None, ALU.is_ge))
            then(dve.tensor_tensor(btab[:, 0:1], btab[:, 0:1], btab[:, 3:4], ALU.add))
            then(dve.tensor_scalar(btab[:, 2:3], btab[:, 0:1], NE - 0.5, 1000.0, ALU.is_ge, ALU.mult))
            then(dve.tensor_scalar(btab[:, 0:1], btab[:, 0:1], float(E), None, ALU.min))
            then(dve.scalar_tensor_tensor(btab[:, 1:2], btab[:, 1:2], float(P), btab[:, 2:3], ALU.mult, ALU.add))
            then(dve.tensor_tensor(bfull, bfull, btab[:, 1:2], ALU.subtract))
            then(dve.tensor_scalar(bfull, bfull, P // 2 + 0.5, None, ALU.is_ge))
            then(dve.tensor_scalar(btab[:, 1:2], btab[:, 1:2], float(T), None, ALU.min))
            shared_step(1)
            then(dve.tensor_scalar(btab[:, 2:3], btab[:, 1:2], 0.0, None, ALU.is_equal))
            then(dve.tensor_scalar(btab[:, 3:4], btab[:, 0:1], 1.0, None, ALU.add))
            then(dve.tensor_tensor(btab[:, 2:3], btab[:, 2:3], btab[:, 3:4], ALU.mult))
            then(dve.tensor_scalar(btab[:, 3:4], btab[:, 0:1], E - 0.5, None, ALU.is_lt))
            then(dve.tensor_tensor(btab[:, 2:3], btab[:, 2:3], btab[:, 3:4], ALU.mult))
            dve.sem_inc(s_bt, 1)
            dve.wait_ge(s_btr, 1)
            then(dve.tensor_copy(tab[0:1, :], pp[3][0:1, 512:512 + TABW]))
            then(dve.tensor_scalar(ntab[0:1, 0:1], cum[0:1, E - 1:E], float(NT), None, ALU.add))
            dve.sem_inc(s_tab, 1)
            onehots(*block_of(NT, 0))
            shared_step(2)

            def first_slots(n):
                q = n % 2
                dve.wait_ge(s_im, n - NT + 1)
                dve.wait_ge(s_gt[q], 32)
                gather_index(q)
                keep_slots(q)
                dve.wait_ge(s_sf, n + 1)
                onehots(*block_of(n, 1))

            first_slots(NT)
            shared_step(3)
            first_slots(NT + 1)
            nb = dve.value_load(ntab[0:1, 0:1], min_val=NT + E, max_val=MAXB)
            with dve.Fori(NT, nb, 2) as i:
                for q in range(2):
                    e3, r3 = block_of(i, q + 3)
                    nxt = dve.value_load(tab[0:1, bass.ds(i + (q + B_SPLIT), 1)], min_val=0, max_val=E)
                    par = dve.snap(nxt % 2)
                    dve.wait_ge(s_gt[q], i * 8 + 16)
                    dve.wait_ge(s_im, i + (q + 3 - NT))
                    gather_index(q)
                    onehots(e3, r3)
                    scatter_index(1 - q, i * 8)
                    with dve.If(nxt):
                        for s in range(2):
                            split_weights(s, par, nxt * 3 + (s + 1))
                    hidden(i, q)
                    split_block(i + (q + 2))
                    keep_rows(i, q)
                    keep_slots(q)
                    split_hidden(i, q)
            pairs = (nb + 1) // 2
            dve.wait_ge(s_sr, pairs * 2)
            scatter_index(1, pairs * 16)
            def add_sums(t):
                dve.wait_ge(s_yin[t], 32)
                dve.tensor_tensor(acc[:, 0, t, :], acc[:, 0, t, :], acc[:, 1, t, :], ALU.add).then_inc(s_comb, 1)

            def finish(t):
                y = acc[:, 0, t, :]
                dve.wait_ge(s_frs, t + 1)
                then(dve.reciprocal(frst[:, t:t + 1], frst[:, t:t + 1]))
                then(dve.scalar_tensor_tensor(y, y, frst[:, t:t + 1], arow[:, 3], ALU.mult, ALU.mult))
                dve.tensor_tensor(y, y, xres[:, t, :], ALU.add).then_inc(s_fin, 1)

            add_sums(0)
            for t in range(1, NT):
                add_sums(t)
                finish(t - 1)
            finish(NT - 1)


_INS = ["x", "c", "ctx", "c_ctx", "w_ada", "b_ada", "g_pre_mix", "g_post_mix", "g_pre_ffn", "g_post_ffn", "w_in",
        "lambda_q1", "lambda_k1", "lambda_q2", "lambda_k2", "g_subln", "w_pool", "b_pool", "pool_scale", "w_out",
        "w_router", "router_bias", "w_e_gate", "w_e_up", "w_e_down", "w_sh_gate", "w_sh_up", "w_sh_down"]


def kernel(**inputs):
    import concourse.bacc as bacc
    from concourse.bass_utils import run_bass_kernel_spmd as run

    nc = bacc.Bacc("TRN2", target_bir_lowering=False, num_devices=1)
    arrays, aps = {}, {}
    for name in _INS:
        arr = np.ascontiguousarray(inputs[name])
        arrays[f"in_{name}"] = arr
        aps[name] = nc.dram_tensor(f"in_{name}", arr.shape, mybir.dt.from_np(arr.dtype), kind="ExternalInput").ap()
    arrays["in_consts"], arrays["in_rope"] = constants()
    aps["rope"] = nc.dram_tensor("in_rope", (P, 2 * T), F32, kind="ExternalInput").ap()
    aps["consts"] = nc.dram_tensor("in_consts", (P, NCONST), F32, kind="ExternalInput").ap()
    out = nc.dram_tensor("out_y", (1, T, D), F32, kind="ExternalOutput").ap()
    hbuf = nc.dram_tensor("h_rows", (T, D), F32, kind="Internal").ap()
    sums = [nc.dram_tensor(f"expert_sums{i}", (T, D), F32, kind="Internal").ap() for i in range(2)]
    build(nc, aps, hbuf, sums, out)
    r = run(nc, [arrays], core_ids=[0])
    return r.results[0]["out_y"]
```
